# Optimizing a Trainium2 kernel written in Bass

```python
import jax, jax.numpy as jnp
from jax import lax
import numpy as np
import math

D_MODEL = 1024
BATCH = 1
SEQ = 256
DEPTH = 1

GLA_HEADS = 4
GLA_DK = 128
GLA_DV = 256
GLA_RANK = 16
GLA_TAU = 16.0
GLA_CHUNK = 64
GLA_QK = GLA_HEADS * GLA_DK
GLA_V = GLA_HEADS * GLA_DV
SGU_GROUPS = 8
SGU_CH = D_MODEL // SGU_GROUPS
SGU_W = SGU_GROUPS * SGU_CH
SGU_CHUNK = 128
PEER_HEADS = 8
PEER_NKEYS = 128
PEER_NEXP = PEER_NKEYS * PEER_NKEYS
PEER_DQ = 256
PEER_TOPK = 16
PEER_BLOCK = 128
EPS = 1e-6

IN_SIZES = (GLA_QK, GLA_QK, GLA_V, GLA_V, GLA_RANK, SGU_W, SGU_W, D_MODEL, D_MODEL)
IN_WIDTH = sum(IN_SIZES)
IN_SPLITS = [int(s) for s in np.cumsum(IN_SIZES)[:-1]]


def rms_norm(x, w):
    xf = x.astype(jnp.float32)
    y = xf * lax.rsqrt(jnp.mean(xf * xf, axis=-1, keepdims=True) + EPS)
    return (y * w.astype(jnp.float32)).astype(x.dtype)

def layer_norm(x, w, b):
    xf = x.astype(jnp.float32)
    mu = jnp.mean(xf, axis=-1, keepdims=True)
    xc = xf - mu
    y = xc * lax.rsqrt(jnp.mean(xc * xc, axis=-1, keepdims=True) + EPS)
    return (y * w.astype(jnp.float32) + b.astype(jnp.float32)).astype(x.dtype)

def modulate(h, shift, scale):
    return h * (1 + scale[:, None, :]) + shift[:, None, :]

def gla_chunked(q, k, v, log_a):
    B, T, H, dk = q.shape
    dv = v.shape[-1]
    C = GLA_CHUNK
    N = T // C
    f32 = jnp.float32

    def to_chunks(t):
        return t.astype(f32).reshape(B, N, C, H, t.shape[-1]).transpose(1, 0, 3, 2, 4)

    qc, kc, vc, lac = to_chunks(q) * dk ** -0.5, to_chunks(k), to_chunks(v), to_chunks(log_a)
    G = jnp.cumsum(lac, axis=-2)
    G_last = G[..., -1:, :]
    q_dec = qc * jnp.exp(G)
    k_inv = kc * jnp.exp(-G)
    k_tail = kc * jnp.exp(G_last - G)
    mask = jnp.tril(jnp.ones((C, C), dtype=bool))
    A = jnp.where(mask, jnp.einsum('nbhik,nbhjk->nbhij', q_dec, k_inv), 0.0)
    o_intra = jnp.einsum('nbhij,nbhjv->nbhiv', A, vc)

    def step(S, inp):
        qd, kt, vv, gl = inp
        o = jnp.einsum('bhik,bhkv->bhiv', qd, S)
        S = S * jnp.exp(gl)[..., 0, :, None] + jnp.einsum('bhjk,bhjv->bhkv', kt, vv)
        return S, o

    S0 = jnp.zeros((B, H, dk, dv), f32)
    _, o_inter = lax.scan(step, S0, (q_dec, k_tail, vc, G_last))
    o = o_intra + o_inter
    return o.transpose(1, 0, 3, 2, 4).reshape(B, T, H, dv).astype(q.dtype)

def spatial_gating(u, v, w_s, b_s, ln_w, ln_b):
    B, T, _ = v.shape
    N = T // SGU_CHUNK
    v = layer_norm(v, ln_w, ln_b)
    vg = v.reshape(B, N, SGU_CHUNK, SGU_GROUPS, SGU_CH)
    mask = jnp.tril(jnp.ones((SGU_CHUNK, SGU_CHUNK), dtype=bool))
    w = jnp.where(mask[None], w_s, 0)
    s = jnp.einsum('gij,bnjgc->bnigc', w, vg) + b_s.T[None, None, :, :, None]
    return u * s.reshape(B, T, SGU_W)

def peer(h, w_q, keys1, keys2, expert_down, expert_up):
    B, T, D = h.shape
    H, K = PEER_HEADS, PEER_TOPK
    q = jnp.einsum('btd,dq->btq', h, w_q).reshape(B, T, H, 2, PEER_DQ // 2)
    s1 = jnp.einsum('bthc,kc->bthk', q[..., 0, :], keys1).astype(jnp.float32)
    s2 = jnp.einsum('bthc,kc->bthk', q[..., 1, :], keys2).astype(jnp.float32)
    v1, i1 = lax.top_k(s1, K)
    v2, i2 = lax.top_k(s2, K)
    cand = (v1[..., :, None] + v2[..., None, :]).reshape(B, T, H, K * K)
    cidx = (i1[..., :, None] * PEER_NKEYS + i2[..., None, :]).reshape(B, T, H, K * K)
    top_s, pos = lax.top_k(cand, K)
    idx = jnp.take_along_axis(cidx, pos, axis=-1)
    g = jax.nn.softmax(top_s, axis=-1).astype(h.dtype)
    nb = (B * T) // PEER_BLOCK
    xb = h.reshape(nb, PEER_BLOCK, D)
    ib = idx.reshape(nb, PEER_BLOCK, H * K)
    gb = g.reshape(nb, PEER_BLOCK, H * K)

    def block(args):
        xx, ii, gg = args
        u = expert_down[ii]
        a = jax.nn.gelu(jnp.einsum('pd,ped->pe', xx, u), approximate=False)
        vv = expert_up[ii]
        return jnp.einsum('pe,ped->pd', gg * a, vv)

    return lax.map(block, (xb, ib, gb)).reshape(B, T, D)

def first_inputs(seed: int = 0) -> dict:
    key = jax.random.key(seed)
    ks = jax.random.split(key, 24)
    f32 = jnp.float32
    L, D = DEPTH, D_MODEL

    def nrm(k, shape, scale):
        return jax.random.normal(k, shape, f32) * scale

    return {
        'x': nrm(ks[0], (BATCH, SEQ, D), 1.0),
        'c': nrm(ks[1], (BATCH, D), 1.0),
        'w_ada': nrm(ks[2], (L, D, 6 * D), 0.5 * D ** -0.5),
        'b_ada': nrm(ks[3], (L, 6 * D), 0.02),
        'norm1_w': 1.0 + nrm(ks[4], (L, D), 0.02),
        'w_in': nrm(ks[5], (L, D, IN_WIDTH), D ** -0.5),
        'w_alpha_up': nrm(ks[6], (L, GLA_RANK, GLA_QK), GLA_RANK ** -0.5),
        'b_alpha': nrm(ks[7], (L, GLA_QK), 0.1),
        'gla_norm_w': 1.0 + nrm(ks[8], (L, GLA_V), 0.02),
        'sgu_ln_w': 1.0 + nrm(ks[9], (L, SGU_W), 0.02),
        'sgu_ln_b': nrm(ks[10], (L, SGU_W), 0.02),
        'sgu_w': nrm(ks[11], (L, SGU_GROUPS, SGU_CHUNK, SGU_CHUNK), 0.5 * SGU_CHUNK ** -0.5),
        'sgu_b': 1.0 + nrm(ks[12], (L, SGU_GROUPS, SGU_CHUNK), 0.02),
        'w_out': nrm(ks[13], (L, D, D), D ** -0.5),
        'norm2_w': 1.0 + nrm(ks[14], (L, D), 0.02),
        'peer_w_q': nrm(ks[15], (L, D, PEER_HEADS * PEER_DQ), D ** -0.5),
        'peer_keys1': nrm(ks[16], (L, PEER_NKEYS, PEER_DQ // 2), (PEER_DQ // 2) ** -0.5),
        'peer_keys2': nrm(ks[17], (L, PEER_NKEYS, PEER_DQ // 2), (PEER_DQ // 2) ** -0.5),
        'peer_down': nrm(ks[18], (L, PEER_NEXP, D), D ** -0.5),
        'peer_up': nrm(ks[19], (L, PEER_NEXP, D), D ** -0.5),
        'final_norm_w': 1.0 + nrm(ks[20], (D,), 0.02),
    }

def first_block(x, c, w_ada, b_ada, norm1_w, w_in, w_alpha_up, b_alpha, gla_norm_w,
              sgu_ln_w, sgu_ln_b, sgu_w, sgu_b, w_out, norm2_w, peer_w_q, peer_keys1,
              peer_keys2, peer_down, peer_up, final_norm_w):
    B, T, D = x.shape
    silu_c = jax.nn.silu(c)
    for l in range(DEPTH):
        mod = jnp.einsum('bd,de->be', silu_c, w_ada[l]) + b_ada[l]
        shift1, scale1, gate1, shift2, scale2, gate2 = jnp.split(mod, 6, axis=-1)

        h = modulate(rms_norm(x, norm1_w[l]), shift1, scale1)
        proj = jnp.einsum('btd,de->bte', h, w_in[l])
        q, k, v, r, a_lr, su, sv, g_a, g_b = jnp.split(proj, IN_SPLITS, axis=-1)

        z = jnp.einsum('btr,rk->btk', a_lr, w_alpha_up[l]) + b_alpha[l]
        log_a = jax.nn.log_sigmoid(z.astype(jnp.float32)) / GLA_TAU
        o = gla_chunked(q.reshape(B, T, GLA_HEADS, GLA_DK), k.reshape(B, T, GLA_HEADS, GLA_DK),
                        v.reshape(B, T, GLA_HEADS, GLA_DV), log_a.reshape(B, T, GLA_HEADS, GLA_DK))
        o = rms_norm(o, gla_norm_w[l].reshape(GLA_HEADS, GLA_DV)).reshape(B, T, GLA_V)
        o_gla = o * jax.nn.silu(r)

        o_sgu = spatial_gating(jax.nn.gelu(su, approximate=False), jax.nn.gelu(sv, approximate=False),
                               sgu_w[l], sgu_b[l], sgu_ln_w[l], sgu_ln_b[l])

        merged = jax.nn.sigmoid(g_a) * o_gla + jax.nn.sigmoid(g_b) * o_sgu
        y = jnp.einsum('bte,ed->btd', merged, w_out[l])
        x = x + gate1[:, None, :] * y

        h2 = modulate(rms_norm(x, norm2_w[l]), shift2, scale2)
        y2 = peer(h2, peer_w_q[l], peer_keys1[l], peer_keys2[l], peer_down[l], peer_up[l])
        x = x + gate2[:, None, :] * y2
    return rms_norm(x, final_norm_w)


DEPTH_2 = 2

GRID_W = 64
CTX_LEN = 256
ROPE_THETA = 10000.0
Q_BLOCK = 128

MLA_HEADS = 4
MLA_Q_RANK = 256
MLA_KV_RANK = 128
MLA_NOPE = 64
MLA_ROPE = 32
MLA_V = 64
DIFF_HEADS = 4
DIFF_QK = 32
DIFF_V = 2 * DIFF_QK
GQA_HEADS = 8
GQA_KV_HEADS = 2
GQA_DIM = 64
GQA_GROUP = GQA_HEADS // GQA_KV_HEADS

MIX_WIDTH = MLA_HEADS * MLA_V + DIFF_HEADS * DIFF_V + GQA_HEADS * GQA_DIM
FFN_HIDDEN = -(-8 * D_MODEL // (3 * 256)) * 256

IN_SIZES_2 = (
    MLA_Q_RANK,
    MLA_KV_RANK + MLA_ROPE,
    DIFF_HEADS * 2 * DIFF_QK,
    DIFF_HEADS * 2 * DIFF_QK,
    DIFF_HEADS * DIFF_V,
    GQA_HEADS * GQA_DIM,
    GQA_KV_HEADS * GQA_DIM,
    GQA_KV_HEADS * GQA_DIM,
)
IN_WIDTH_2 = sum(IN_SIZES_2)

MLA_SCALE = 1.0 / math.sqrt(MLA_NOPE + MLA_ROPE)
DIFF_SCALE = 1.0 / math.sqrt(DIFF_QK)
GQA_SCALE = 1.0 / math.sqrt(GQA_DIM)


def _rms(x, g):
    xf = x.astype(jnp.float32)
    y = xf * lax.rsqrt(jnp.mean(xf * xf, axis=-1, keepdims=True) + EPS)
    return (y * g.astype(jnp.float32)).astype(x.dtype)

def _axial_rope_tables(row, col, rot_dim):
    quarter = rot_dim // 4
    inv = ROPE_THETA ** (-jnp.arange(quarter, dtype=jnp.float32) / quarter)
    ang = jnp.concatenate([row.astype(jnp.float32)[:, None] * inv,
                           col.astype(jnp.float32)[:, None] * inv], axis=-1)
    return jnp.cos(ang), jnp.sin(ang)

def _rope(x, tables):
    if tables is None:
        return x
    cos, sin = tables
    half = x.shape[-1] // 2
    xf = x.astype(jnp.float32)
    x1, x2 = xf[..., :half], xf[..., half:]
    c = cos[None, :, None, :]
    s = sin[None, :, None, :]
    return jnp.concatenate([x1 * c - x2 * s, x2 * c + x1 * s], axis=-1).astype(x.dtype)

def _hf(t):
    return t.transpose(0, 2, 1, 3)

def _sdpa(q, k, v, scale):
    s = jnp.einsum('bhgqd,bhkd->bhgqk', q, k).astype(jnp.float32) * scale
    p = jax.nn.softmax(s, axis=-1).astype(v.dtype)
    return jnp.einsum('bhgqk,bhkd->bhgqd', p, v)

def _latent_attention(q, k, v, scale):
    B, Hk, G, S, d = q.shape
    nb = S // Q_BLOCK
    qb = q.reshape(B, Hk, G, nb, Q_BLOCK, d).transpose(3, 0, 1, 2, 4, 5)
    ob = lax.map(lambda qi: _sdpa(qi, k, v, scale), qb)
    return ob.transpose(1, 2, 3, 0, 4, 5).reshape(B, Hk, G, S, ob.shape[-1])

def _project(h, w_in, g_mla_q, w_mla_qb, g_mla_kv, w_mla_kvb, g_gqa_q, g_gqa_k,
             rope_small, rope_large):
    B, T, _ = h.shape
    p = h @ w_in
    idx = np.cumsum(IN_SIZES_2)[:-1].tolist()
    q_a, kv_a, dq, dk, dv, gq, gk, gv = jnp.split(p, idx, axis=-1)

    q = (_rms(q_a, g_mla_q) @ w_mla_qb).reshape(B, T, MLA_HEADS, MLA_NOPE + MLA_ROPE)
    q_nope, q_pe = q[..., :MLA_NOPE], _rope(q[..., MLA_NOPE:], rope_small)
    c_kv = kv_a[..., :MLA_KV_RANK]
    k_pe = _rope(kv_a[..., MLA_KV_RANK:][:, :, None, :], rope_small)
    kv = (_rms(c_kv, g_mla_kv) @ w_mla_kvb).reshape(B, T, MLA_HEADS, MLA_NOPE + MLA_V)
    k_nope, v_mla = kv[..., :MLA_NOPE], kv[..., MLA_NOPE:]
    q_mla = jnp.concatenate([q_nope, q_pe], axis=-1)
    k_mla = jnp.concatenate([k_nope, jnp.broadcast_to(k_pe, (B, T, MLA_HEADS, MLA_ROPE))], axis=-1)
    mla = (_hf(q_mla)[:, :, None], _hf(k_mla), _hf(v_mla))

    q_d = _rope(dq.reshape(B, T, DIFF_HEADS * 2, DIFF_QK), rope_small)
    k_d = _rope(dk.reshape(B, T, DIFF_HEADS * 2, DIFF_QK), rope_small)
    v_d = jnp.repeat(dv.reshape(B, T, DIFF_HEADS, DIFF_V), 2, axis=2)
    diff = (_hf(q_d)[:, :, None], _hf(k_d), _hf(v_d))

    q_g = _rope(_rms(gq.reshape(B, T, GQA_HEADS, GQA_DIM), g_gqa_q), rope_large)
    k_g = _rope(_rms(gk.reshape(B, T, GQA_KV_HEADS, GQA_DIM), g_gqa_k), rope_large)
    v_g = gv.reshape(B, T, GQA_KV_HEADS, GQA_DIM)
    q_g = q_g.reshape(B, T, GQA_KV_HEADS, GQA_GROUP, GQA_DIM).transpose(0, 2, 3, 1, 4)
    gqa = (q_g, _hf(k_g), _hf(v_g))
    return (mla, diff, gqa)

def _merge(o_mla, o_diff, o_gqa, lam, lam_init, g_diff_sub):
    B, _, _, T, _ = o_mla.shape
    y_mla = o_mla[:, :, 0].transpose(0, 2, 1, 3).reshape(B, T, MLA_HEADS * MLA_V)
    od = o_diff[:, :, 0].reshape(B, DIFF_HEADS, 2, T, DIFF_V)
    d = od[:, :, 0] - lam.astype(od.dtype) * od[:, :, 1]
    d = _rms(d, g_diff_sub) * (1.0 - lam_init)
    y_diff = d.transpose(0, 2, 1, 3).reshape(B, T, DIFF_HEADS * DIFF_V)
    y_gqa = o_gqa.transpose(0, 3, 1, 2, 4).reshape(B, T, GQA_HEADS * GQA_DIM)
    return jnp.concatenate([y_mla, y_diff, y_gqa], axis=-1)

def _swiglu(h, w_gate, w_up, w_down):
    return (jax.nn.silu(h @ w_gate) * (h @ w_up)) @ w_down

def second_inputs(seed: int = 0) -> dict:
    key = jax.random.key(seed)
    ks = iter(jax.random.split(key, 32))

    def nrm(shape, scale):
        return jax.random.normal(next(ks), shape, jnp.float32) * scale

    def gain(shape):
        return 1.0 + 0.05 * jax.random.normal(next(ks), shape, jnp.float32)

    D = D_MODEL
    return {
        "x": nrm((BATCH, SEQ, D), 1.0),
        "c": nrm((BATCH, D), 1.0),
        "ctx": nrm((BATCH, CTX_LEN, D), 1.0),
        "c_ctx": nrm((D,), 1.0),
        "w_ada": nrm((DEPTH_2, D, 6 * D), 0.5 * D ** -0.5),
        "b_ada": nrm((DEPTH_2, 6 * D), 0.01),
        "g_attn_pre": gain((DEPTH_2, D)),
        "g_attn_post": gain((DEPTH_2, D)),
        "w_in": nrm((DEPTH_2, D, IN_WIDTH_2), D ** -0.5),
        "g_mla_q": gain((DEPTH_2, MLA_Q_RANK)),
        "w_mla_qb": nrm((DEPTH_2, MLA_Q_RANK, MLA_HEADS * (MLA_NOPE + MLA_ROPE)), MLA_Q_RANK ** -0.5),
        "g_mla_kv": gain((DEPTH_2, MLA_KV_RANK)),
        "w_mla_kvb": nrm((DEPTH_2, MLA_KV_RANK, MLA_HEADS * (MLA_NOPE + MLA_V)), MLA_KV_RANK ** -0.5),
        "lambda_q1": nrm((DEPTH_2, DIFF_QK), 0.1),
        "lambda_k1": nrm((DEPTH_2, DIFF_QK), 0.1),
        "lambda_q2": nrm((DEPTH_2, DIFF_QK), 0.1),
        "lambda_k2": nrm((DEPTH_2, DIFF_QK), 0.1),
        "g_diff_sub": gain((DEPTH_2, DIFF_V)),
        "g_gqa_q": gain((DEPTH_2, GQA_DIM)),
        "g_gqa_k": gain((DEPTH_2, GQA_DIM)),
        "w_out": nrm((DEPTH_2, MIX_WIDTH, D), MIX_WIDTH ** -0.5),
        "g_ffn_pre": gain((DEPTH_2, D)),
        "g_ffn_post": gain((DEPTH_2, D)),
        "w_ffn_gate": nrm((DEPTH_2, D, FFN_HIDDEN), D ** -0.5),
        "w_ffn_up": nrm((DEPTH_2, D, FFN_HIDDEN), D ** -0.5),
        "w_ffn_down": nrm((DEPTH_2, FFN_HIDDEN, D), FFN_HIDDEN ** -0.5),
    }

def second_block(x, c, ctx, c_ctx, w_ada, b_ada, g_attn_pre, g_attn_post, w_in, g_mla_q, w_mla_qb,
              g_mla_kv, w_mla_kvb, lambda_q1, lambda_k1, lambda_q2, lambda_k2, g_diff_sub,
              g_gqa_q, g_gqa_k, w_out, g_ffn_pre, g_ffn_post, w_ffn_gate, w_ffn_up, w_ffn_down):
    n_tok = x.shape[1]
    rows = n_tok // GRID_W
    row = jnp.repeat(jnp.arange(rows, dtype=jnp.int32), GRID_W)
    col = jnp.tile(jnp.arange(GRID_W, dtype=jnp.int32), rows)
    rope_small = _axial_rope_tables(row, col, MLA_ROPE)
    rope_large = _axial_rope_tables(row, col, GQA_DIM)

    silu_c = jax.nn.silu(c)
    silu_cc = jax.nn.silu(c_ctx)
    xc = ctx
    scales = (MLA_SCALE, DIFF_SCALE, GQA_SCALE)

    for l in range(DEPTH_2):
        last = l == DEPTH_2 - 1
        mod = (silu_c @ w_ada[l] + b_ada[l])[:, None, :]
        mod_c = (silu_cc @ w_ada[l] + b_ada[l])[None, None, :]
        sh_a, sc_a, gt_a, sh_f, sc_f, gt_f = jnp.split(mod, 6, axis=-1)
        csh_a, csc_a, cgt_a, csh_f, csc_f, cgt_f = jnp.split(mod_c, 6, axis=-1)

        lam_init = 0.8 - 0.6 * math.exp(-0.3 * l)
        lam = (jnp.exp(jnp.sum(lambda_q1[l].astype(jnp.float32) * lambda_k1[l].astype(jnp.float32)))
               - jnp.exp(jnp.sum(lambda_q2[l].astype(jnp.float32) * lambda_k2[l].astype(jnp.float32)))
               + lam_init)

        h = _rms(x, g_attn_pre[l]) * (1.0 + sc_a) + sh_a
        hc = _rms(xc, g_attn_pre[l]) * (1.0 + csc_a) + csh_a
        proj_args = (w_in[l], g_mla_q[l], w_mla_qb[l], g_mla_kv[l], w_mla_kvb[l], g_gqa_q[l], g_gqa_k[l])
        lat = _project(h, *proj_args, rope_small, rope_large)
        cxt = _project(hc, *proj_args, None, None)

        o_lat = []
        for (q, k, v), (qc, kc, vc), s in zip(lat, cxt, scales):
            k_all = jnp.concatenate([k, kc], axis=2)
            v_all = jnp.concatenate([v, vc], axis=2)
            o_lat.append(_latent_attention(q, k_all, v_all, s))
        y = _merge(o_lat[0], o_lat[1], o_lat[2], lam, lam_init, g_diff_sub[l]) @ w_out[l]
        x = x + gt_a * _rms(y, g_attn_post[l])

        if not last:
            o_ctx = [_sdpa(qc, kc, vc, s) for (qc, kc, vc), s in zip(cxt, scales)]
            yc = _merge(o_ctx[0], o_ctx[1], o_ctx[2], lam, lam_init, g_diff_sub[l]) @ w_out[l]
            xc = xc + cgt_a * _rms(yc, g_attn_post[l])

        hf = _rms(x, g_ffn_pre[l]) * (1.0 + sc_f) + sh_f
        x = x + gt_f * _rms(_swiglu(hf, w_ffn_gate[l], w_ffn_up[l], w_ffn_down[l]), g_ffn_post[l])
        if not last:
            hfc = _rms(xc, g_ffn_pre[l]) * (1.0 + csc_f) + csh_f
            xc = xc + cgt_f * _rms(_swiglu(hfc, w_ffn_gate[l], w_ffn_up[l], w_ffn_down[l]), g_ffn_post[l])

    return x


def setup_inputs(seed=0):
    out = dict(first_inputs(seed))
    for name, value in second_inputs(seed + 1).items():
        if name != "x":
            out[name + "_2"] = value
    return out


def reference(
    x, c, w_ada, b_ada, norm1_w, w_in, w_alpha_up, b_alpha, gla_norm_w, sgu_ln_w, sgu_ln_b,
    sgu_w, sgu_b, w_out, norm2_w, peer_w_q, peer_keys1, peer_keys2, peer_down, peer_up,
    final_norm_w, c_2, ctx_2, c_ctx_2, w_ada_2, b_ada_2, g_attn_pre_2, g_attn_post_2, w_in_2,
    g_mla_q_2, w_mla_qb_2, g_mla_kv_2, w_mla_kvb_2, lambda_q1_2, lambda_k1_2, lambda_q2_2,
    lambda_k2_2, g_diff_sub_2, g_gqa_q_2, g_gqa_k_2, w_out_2, g_ffn_pre_2, g_ffn_post_2,
    w_ffn_gate_2, w_ffn_up_2, w_ffn_down_2,
):
    x = first_block(
        x, c, w_ada, b_ada, norm1_w, w_in, w_alpha_up, b_alpha, gla_norm_w, sgu_ln_w, sgu_ln_b,
        sgu_w, sgu_b, w_out, norm2_w, peer_w_q, peer_keys1, peer_keys2, peer_down, peer_up,
        final_norm_w,
    )
    return second_block(
        x, c_2, ctx_2, c_ctx_2, w_ada_2, b_ada_2, g_attn_pre_2, g_attn_post_2, w_in_2,
        g_mla_q_2, w_mla_qb_2, g_mla_kv_2, w_mla_kvb_2, lambda_q1_2, lambda_k1_2, lambda_q2_2,
        lambda_k2_2, g_diff_sub_2, g_gqa_q_2, g_gqa_k_2, w_out_2, g_ffn_pre_2, g_ffn_post_2,
        w_ffn_gate_2, w_ffn_up_2, w_ffn_down_2,
    )


_drawn_inputs = setup_inputs


def setup_inputs(seed=0):
    import zlib

    import numpy as np

    out = dict(_drawn_inputs(seed))
    spreads = {}
    factors = {'b_ada': 4.124,
     'norm1_w': 8.0,
     'w_alpha_up': 2.741,
     'b_alpha': 8.0,
     'gla_norm_w': 8.0,
     'sgu_ln_w': 8.0,
     'sgu_ln_b': 8.0,
     'sgu_b': 8.0,
     'norm2_w': 8.0,
     'peer_w_q': 8.0,
     'peer_keys1': 8.0,
     'peer_keys2': 8.0,
     'peer_down': 8.0,
     'peer_up': 8.0,
     'final_norm_w': 2.899,
     'g_attn_pre_2': 2.919,
     'g_mla_q_2': 8.0,
     'g_mla_kv_2': 6.572,
     'lambda_q2_2': 4.18,
     'lambda_k2_2': 7.059,
     'g_diff_sub_2': 24.616,
     'g_gqa_q_2': 8.0,
     'g_gqa_k_2': 8.0,
     'g_ffn_post_2': 2.893,
     'g_attn_post_2': 4.615,
     'lambda_q1_2': 8.0,
     'lambda_k1_2': 8.0}
    for name, (base, spread) in spreads.items():
        noise = np.random.default_rng([zlib.crc32(name.encode()), seed]).standard_normal(out[name].shape)
        drawn = base * np.exp(spread * noise) if base else spread * noise
        out[name] = __import__('jax').numpy.asarray(drawn.astype(out[name].dtype))
    for name, factor in factors.items():
        out[name] = (out[name] * factor).astype(out[name].dtype)
    return out
```

```python
from contextlib import ExitStack

import numpy as np
import concourse.bass as bass
from concourse import mybir

ALU = mybir.AluOpType
ACT = mybir.ActivationFunctionType
AX = mybir.AxisListType
F32 = mybir.dt.float32
U32 = mybir.dt.uint32
P = 128
EPS = 1e-6
D = 1024
NEG = -3.0e38
LAM_INIT = [0.8 - 0.6 * float(np.exp(-0.3 * l)) for l in range(2)]
SCALES = [1.0 / float(np.sqrt(96.0)), 1.0 / float(np.sqrt(32.0)), 1.0 / 8.0]
GW = 32768
NSLOT = 6
NF = 22

COLS = {}
_n = 0
for _name, _w in [("c", 8), ("c2", 8), ("cc2", 8), ("b_ada", 48), ("b_ada2a", 48), ("b_ada2b", 48), ("norm1", 8),
                  ("norm2", 8), ("apre0", 8), ("apre1", 8), ("apost0", 8), ("apost1", 8), ("fpre0", 8),
                  ("fpre1", 8), ("fpost0", 8), ("fpost1", 8), ("mq0", 2), ("mq1", 2), ("mkv0", 1), ("mkv1", 1),
                  ("b_alpha", 4), ("sgu_b", 8)]:
    COLS[_name] = (_n, _w)
    _n += _w
NCOL = _n
CONS = {}
_n = 0
for _name, _w in [("ident", 128), ("iota", 128), ("cosS", 32), ("sinS", 32), ("cosL", 64), ("sinL", 64)]:
    CONS[_name] = (_n, _w)
    _n += _w
NCON = _n


class Queues:

    def __init__(self, sems):
        self.sem = sems
        self.ops = {e: [] for e in ("pe", "act", "dve", "pool", "sp")}
        self.count = {e: 0 for e in sems}
        self.seen = {e: {} for e in self.ops}
        self.vals = {}

    def wait(self, eng, tokens):
        for t in tokens:
            if t is None:
                continue
            if isinstance(t, list):
                self.wait(eng, t)
                continue
            name, sem, val = t
            if self.seen[eng].get(name, 0) < val:
                self.seen[eng][name] = val
                self.ops[eng].append(("w", sem, val))

    def put(self, eng, fn, waits, mark=True):
        self.wait(eng, waits)
        if not mark:
            self.ops[eng].append(("i", fn, None, 0))
            return None
        self.count[eng] += 1
        self.ops[eng].append(("i", fn, self.sem[eng], 1))
        return (eng, self.sem[eng], self.count[eng])

    def last(self, eng):
        return (eng, self.sem[eng], self.count[eng]) if self.count[eng] else None

    def dma(self, eng, out, in_, name, sem, waits):
        self.wait(eng, waits)
        self.vals[name] = self.vals.get(name, 0) + 16
        self.ops[eng].append(("i", lambda e: e.dma_start(out, in_), sem, 16))
        return (name, sem, self.vals[name])


def build(nc, cols_d, cons_d, rows_d, ada_d, ada2_d, win_d, walr_d, wau_d, sgw_d, wout_d, wq_d, keys_d, peer_d,
          x_d, ctx_d, win2_d, win2k_d, wqb_d, wkvb_d, wout2_d, ffn_d, ffd_d, out_d):
    with ExitStack() as st:
        def sb(name, words):
            return st.enter_context(nc.sbuf_tensor(name, [P, words], F32))

        sems = {e: st.enter_context(nc.semaphore("s_" + e)) for e in ("pe", "act", "dve", "pool")}
        Q = Queues(sems)

        def mm(out, lhsT, rhs, start, stop, *w, mark=False):
            return Q.put("pe", lambda e: e.matmul(out, lhsT, rhs, start=start, stop=stop, skip_group_check=True),
                         w, mark)

        def tr(out, in_, idn, *w, mark=False):
            return Q.put("pe", lambda e: e.transpose(out, in_, idn), w, mark)

        def own(eng, link):
            return Q.last(eng) if link else None

        def act(out, in_, func, *w, bias=0.0, scale=1.0, accum=None, link=True):
            w = [own("act", link), list(w)]
            if accum is None:
                return Q.put("act", lambda e: e.activation(out, in_, func, bias=bias, scale=scale), w)
            return Q.put("act", lambda e: e.activation(out, in_, func, bias=bias, scale=scale, accum_out=accum), w)

        def tt(out, a, b, op, *w, eng="dve", link=True):
            return Q.put(eng, lambda e: e.tensor_tensor(out, a, b, op), [own(eng, link), list(w)])

        def ts(out, a, s1, s2, op0, op1, *w, eng="dve", link=True):
            if op1 is None:
                return Q.put(eng, lambda e: e.tensor_scalar(out, a, s1, None, op0), [own(eng, link), list(w)])
            return Q.put(eng, lambda e: e.tensor_scalar(out, a, s1, s2, op0, op1), [own(eng, link), list(w)])

        def stt(out, a, s, b, op0, op1, *w, link=True):
            return Q.put("dve", lambda e: e.scalar_tensor_tensor(out=out, in0=a, scalar=s, in1=b, op0=op0, op1=op1),
                         [own("dve", link), list(w)])

        def cp(out, a, *w, eng="dve", link=True):
            if eng == "act":
                return act(out, a, ACT.Copy, *w, link=link)
            return Q.put(eng, lambda e: e.tensor_copy(out, a), [own(eng, link), list(w)])

        def rsum(out, a, op, *w, link=True):
            return Q.put("dve", lambda e: e.tensor_reduce(out, a, AX.X, op), [own("dve", link), list(w)])

        def recip(out, a, *w):
            return Q.put("dve", lambda e: e.reciprocal(out, a), [own("dve", True), list(w)])

        def aff(ap, pattern, base, cm, *w):
            return Q.put("pool", lambda e: e.affine_select(out=ap, in_=ap, compare_op=ALU.is_ge, fill=0.0, base=base,
                                                           pattern=pattern, channel_multiplier=cm),
                         [own("pool", True), list(w)])

        G = sb("G", GW)
        RING = sb("RING", NSLOT * 2048)
        X = sb("X", 2048)
        HT = sb("HT", 2048)
        cols = sb("cols", NCOL)
        cons = sb("cons", NCON)
        srow = sb("srow", 640)
        MOD = sb("MOD", 48 + 96 * 2)
        AB = sb("AB", 16 * 11)
        ST = sb("ST", 192)
        TMP = sb("TMP", 1024)
        IDX = sb("IDX", 768)
        bk = [st.enter_context(nc.psum_tensor(f"bk{i}", [P, 512], F32)) for i in range(8)]

        misc = {}

        def msem(name):
            if name not in misc:
                misc[name] = st.enter_context(nc.semaphore("d_" + name))
            return misc[name]

        def load(name, out, in_, *w, eng="sp"):
            return Q.dma(eng, out, in_, name, msem(name), w)

        def v2(ap, a):
            return ap.rearrange("p (a b) -> p a b", a=a)

        X3, HT3 = v2(X[:, :], 2), v2(HT[:, :], 8)
        col = {n: cols[:, o:o + w] for n, (o, w) in COLS.items()}
        con = {n: cons[:, o:o + w] for n, (o, w) in CONS.items()}
        ident, iota = con["ident"], con["iota"]

        slot_sem = [st.enter_context(nc.semaphore(f"r{i}")) for i in range(NSLOT)]
        ring = {"n": 0}
        slot_free = [None] * NSLOT

        class Tile:
            def __init__(self, src, words):
                self.slot = ring["n"] % NSLOT
                ring["n"] += 1
                self.ap = RING[:, self.slot * 2048:self.slot * 2048 + words]
                self.t = Q.dma("sp", self.ap, src, f"r{self.slot}", slot_sem[self.slot], [slot_free[self.slot]])

            def done(self, token):
                slot_free[self.slot] = token

        bank_free = [None] * 8
        rot = {"set": list(range(8)), "n": 0}

        class Bank:
            def __init__(self, index=None):
                if index is None:
                    index = rot["set"][rot["n"] % len(rot["set"])]
                    rot["n"] += 1
                self.i = index
                self.ap = bk[index][:, :]
                self.free = bank_free[index]

            def done(self, *tokens):
                bank_free[self.i] = list(tokens)

        def use_banks(s):
            rot["set"], rot["n"] = s, 0

        heap = {"n": 0}

        def alloc(words):
            a = heap["n"]
            heap["n"] += words
            assert heap["n"] <= GW, heap["n"]
            return G[:, a:a + words]

        def everything():
            return [Q.last(e) for e in ("pe", "act", "dve", "pool")]

        def phase(keep=0):
            heap["n"] = keep
            now = everything()
            for e in ("pe", "act", "dve", "pool", "sp"):
                Q.wait(e, now)
            return now

        stat = {"n": 0}

        def stats(n):
            if stat["n"] + n > 192:
                stat["n"] = 0
            a = stat["n"]
            stat["n"] += n
            return ST[:, a:a + n]

        def rstd(ss, n, width, *w, out=None):
            a, y, r = stats(n), stats(n), stats(n)
            out = stats(n) if out is None else out
            t = ts(a, ss, 1.0 / width, EPS, ALU.mult, ALU.add, *w)
            t = act(y, a, ACT.Sqrt, t)
            recip(r, y, t)
            tt(y, r, r, ALU.mult)
            stt(y, y, -0.5, a, ALU.mult, ALU.mult)
            t = stt(out, y, 1.5, r, ALU.add, ALU.mult)
            return out, t

        def transposes(src, blocks, dst, *w, scale=None, shift=None):
            last = []
            for k0 in range(0, blocks, 4):
                n = min(4, blocks - k0)
                b = Bank()
                for k in range(n):
                    t = tr(b.ap[:, k * P:(k + 1) * P], src[:, (k0 + k) * P:(k0 + k + 1) * P], ident, b.free, *w,
                           mark=(k == n - 1))
                if scale is None:
                    e = "dve" if (k0 // 4) % 2 else "act"
                    u = cp(dst(k0, n), v2(b.ap[:, 0:n * P], n), t, eng=e, link=False)
                    b.done(u)
                    last.append(u)
                else:
                    us = []
                    for k in range(n):
                        if (k0 // 4) % 2:
                            u = ts(dst(k0 + k, 1), b.ap[:, k * P:(k + 1) * P], scale[:, k0 + k:k0 + k + 1],
                                   shift[:, k0 + k:k0 + k + 1], ALU.mult, ALU.add, t, link=False)
                        else:
                            u = act(dst(k0 + k, 1), b.ap[:, k * P:(k + 1) * P], ACT.Identity, t,
                                    scale=scale[:, k0 + k:k0 + k + 1], bias=shift[:, k0 + k:k0 + k + 1], link=False)
                        us.append(u)
                    b.done(*us)
                    last += us
            return last

        def sumsq(src3, ss, junk, *w):
            for i in range(2):
                t = act(junk, src3[:, i, :], ACT.Square, *w, accum=ss[:, i:i + 1])
            return t

        def norm_T(x3, A, B, xn, junk, *w):
            ss = stats(2)
            t = sumsq(x3, ss, junk, *w)
            r, t = rstd(ss, 2, D, t)
            out = []
            for i in range(2):
                t = ts(v2(xn, 2)[:, i, :], x3[:, i, :], r[:, i:i + 1], None, ALU.mult, None)
                out += transposes(v2(xn, 2)[:, i, :], 8, lambda k, n, i=i: HT3[:, k, i * P:(i + 1) * P], t, *w,
                                  scale=A, shift=B)
            return out

        def tok(tile, hT3, b, kc, n, *w):
            w3 = v2(tile.ap, kc)
            for i in range(2):
                for k in range(kc):
                    t = mm(b.ap[:, i * n:(i + 1) * n], hT3[:, k, i * P:(i + 1) * P], w3[:, k, :], k == 0,
                           k == kc - 1, b.free, tile.t, *w, mark=(i == 1 and k == kc - 1))
            tile.done(t)
            return t

        def feat(tile, hT3, b, kc, *w):
            w3 = v2(tile.ap, kc)
            for i in range(2):
                for k in range(kc):
                    t = mm(b.ap[:, i * 256:(i + 1) * 256], w3[:, k, i * P:(i + 1) * P], hT3[:, k, :], k == 0,
                           k == kc - 1, b.free, tile.t, *w, mark=(i == 1 and k == kc - 1))
            tile.done(t)
            return t

        def spread(gcol, dst, *w):
            out = []
            for h in range(2):
                b = Bank()
                for k in range(4):
                    t = mm(b.ap[:, k * P:(k + 1) * P], gcol[:, 4 * h + k:4 * h + k + 1].to_broadcast([P, P]), ident,
                           True, True, b.free, *w, mark=(k == 3))
                u = cp(dst[:, h * 512:(h + 1) * 512], b.ap, t, eng="act", link=False)
                b.done(u)
                out.append(u)
            return out

        t_cols = load("cols", cols[:, :], cols_d[:, :])
        t_cons = load("cons", cons[:, :], cons_d[:, :])
        t_x = load("x", X3, x_d.rearrange("b (i p) d -> p (b i) d", p=P))
        t_srow = load("srow", srow[:, :], rows_d[4096:4736].partition_broadcast(P), eng="act")

        sil = alloc(48)
        t = act(sil[:, 0:24], cols[:, 0:24], ACT.Silu, t_cols)
        t_sil = cp(sil[:, 24:40].rearrange("p (k s) -> p s k", s=2), sil[:, 8:24].rearrange("p (s k) -> p s k", s=2), t)

        def ada(src, ntile, rhs, ns, bias, dst):
            b = Bank()
            for j in range(ntile // 2):
                w = Tile(src[j], 2048)
                w3 = v2(w.ap, 8)
                for i in range(2):
                    for k in range(8):
                        c = (2 * j + i) * ns
                        t = mm(b.ap[:, c:c + ns], w3[:, k, i * P:(i + 1) * P], rhs[:, k * ns:(k + 1) * ns], k == 0,
                               k == 7, b.free, w.t, t_sil, mark=(i == 1 and k == 7))
                w.done(t)
            for s in range(ns):
                t2 = tt(dst[:, s * ntile:(s + 1) * ntile],
                        b.ap[:, 0:ntile * ns].rearrange("p (n s) -> p s n", s=ns)[:, s, :], bias, ALU.add, t)
            b.done(t2)
            return t2

        t_mod = ada(ada_d, 48, sil[:, 0:8], 1, col["b_ada"], MOD[:, 0:48])
        for l in range(2):
            t_mod = ada(ada2_d[l], 48, sil[:, 24:40], 2, col["b_ada2" + "ab"[l]], MOD[:, 48 + 96 * l:144 + 96 * l])

        def affine_cols(n, w, scale):
            o = AB[:, n * 16:n * 16 + 8]
            return o, stt(o, scale, 1.0, w, ALU.add, ALU.mult)

        A1, _ = affine_cols(0, col["norm1"], MOD[:, 8:16])
        A2, t_ab = affine_cols(1, col["norm2"], MOD[:, 32:40])
        lat, cxt = [], []
        for l in range(2):
            for s, lst in ((0, lat), (1, cxt)):
                m = MOD[:, 48 + 96 * l + 48 * s:96 + 96 * l + 48 * s]
                n = 2 + 4 * l + 2 * s
                a, _ = affine_cols(n, col[f"apre{l}"], m[:, 8:16])
                f, _ = affine_cols(n + 1, col[f"fpre{l}"], m[:, 32:40])
                ga, gf = AB[:, n * 16 + 8:n * 16 + 16], AB[:, n * 16 + 24:n * 16 + 32]
                tt(ga, m[:, 16:24], col[f"apost{l}"], ALU.mult)
                t_ab = tt(gf, m[:, 40:48], col[f"fpost{l}"], ALU.mult)
                lst.append(dict(A=a, B=m[:, 0:8], FA=f, FB=m[:, 24:32], ga=ga, gf=gf))
        lamc = AB[:, 160:164]
        for l in range(2):
            r = srow[:, 320 * l + 192:320 * l + 320].rearrange("p (a b c) -> p a b c", a=2, b=2)
            pr, e = alloc(64), stats(2)
            t = tt(v2(pr, 2), r[:, :, 0, :], r[:, :, 1, :], ALU.mult, t_srow)
            t = rsum(e, v2(pr, 2), ALU.add)
            e2 = stats(2)
            t = act(e2, e, ACT.Exp, t)
            lm = lamc[:, l:l + 1]
            tt(lm, e2[:, 1:2], e2[:, 0:1], ALU.subtract, t)
            ts(lm, lm, LAM_INIT[l], None, ALU.subtract, None)
            t_lam = ts(srow[:, 320 * l:320 * l + 64], srow[:, 320 * l:320 * l + 64], 1.0 - LAM_INIT[l], None, ALU.mult,
                       None)

        phase()
        big = alloc(2048)
        qT, kT, vt = alloc(1024), alloc(1024), alloc(2048)
        xn, junk = big, qT
        t_h = norm_T(X3, A1, MOD[:, 0:8], xn, junk, t_x, t_cons, t_ab)
        win = [Tile(win_d[j], 2048) for j in range(4)]
        gws, lnw, lnb = alloc(1024), alloc(1024), alloc(1024)
        t_rows = [load("row", d, rows_d[o:o + 1024].partition_broadcast(P), Q.last("dve"), Q.last("act"), eng="act")
                  for d, o in ((gws, 0), (lnw, 1024), (lnb, 2048))]
        walr, wau = alloc(128), alloc(512)
        t_walr = load("walr", walr, walr_d[:, :], eng="act")
        t_wau = load("wau", wau[0:16, :], wau_d[:, :], eng="act")
        sgw, alrT = alloc(1024), alloc(256)
        t_sgw = load("sgw", sgw, sgw_d[:, :], eng="act")
        t_sgw = aff(v2(sgw, 8), [[0, 8], [1, 128]], 0, -1, t_sgw)
        msk = alloc(256)
        t_msk = Q.put("pool", lambda e: e.memset(msk, 1.0), [])
        t_msk = Q.put("pool", lambda e: e.memset(msk.rearrange("p (a b) -> p a b", b=64)[:, :, 0:1], 0.0), [t_msk])
        for j in range(4):
            b = Bank()
            t = feat(win[j], HT3, b, 8, t_h)
            dst = (qT if j < 2 else kT)[:, (j % 2) * 512:(j % 2) * 512 + 512]
            t_qk = cp(dst, b.ap, t, t_h, eng="act", link=False)
            b.done(t_qk)
        b = Bank()
        for k in range(8):
            t = mm(b.ap[0:16, 0:256], v2(walr, 8)[:, k, :], HT3[:, k, :], k == 0, k == 7, b.free, t_walr,
                   mark=(k == 7))
        t_alr = cp(alrT[0:16, :], b.ap[0:16, 0:256], t)
        b.done(t_alr)
        z, la, Gc, eA = alloc(1024), alloc(1024), alloc(1024), alloc(1024)
        for j in range(2):
            b = Bank()
            for i in range(2):
                h = 2 * j + i
                t = mm(b.ap[:, i * 256:i * 256 + 256], wau[0:16, h * P:(h + 1) * P], alrT[0:16, :], True, True,
                       b.free, t_wau, t_alr, mark=(i == 1))
            for i in range(2):
                h = 2 * j + i
                t_z = ts(z[:, h * 256:(h + 1) * 256], b.ap[:, i * 256:i * 256 + 256], col["b_alpha"][:, h:h + 1],
                         None, ALU.add, None, t, link=False)
            b.done(t_z)
        t = stt(eA, z, -1.0, z, ALU.mult, ALU.min, t_z)
        t = act(eA, eA, ACT.Exp, t)
        t = ts(eA, eA, 1.0, None, ALU.add, None, t)
        t = act(eA, eA, ACT.Ln, t)
        stt(la, z, 0.0, eA, ALU.min, ALU.subtract, t)

        def scan(out, d0, d1, *w):
            return Q.put("dve", lambda e: e.tensor_tensor_scan(out, d0, d1, 0.0, ALU.mult, ALU.add),
                         [own("dve", True), list(w)])

        for h in range(4):
            s = slice(h * 256, (h + 1) * 256)
            t_G = scan(Gc[:, s], msk, la[:, s], t_msk)
        G16 = Gc.rearrange("p (c t) -> p c t", t=64)
        egl = alloc(16)
        t_egl = act(egl, G16[:, :, 63], ACT.Exp, t_G, scale=1.0 / 16)
        t_kt = tt(la.rearrange("p (c t) -> p c t", t=64), G16[:, :, 63:64].to_broadcast([P, 16, 64]), G16,
                  ALU.subtract)
        t_e1 = act(z, Gc, ACT.Exp, scale=1.0 / 16)
        t_e2 = act(eA, Gc, ACT.Exp, scale=-1.0 / 16)
        t_e3 = act(la, la, ACT.Exp, t_kt, scale=1.0 / 16)
        qd, ki = z, eA
        tt(la, kT, la, ALU.mult, t_e3)
        kt = la
        t_ktail = Q.last("dve")
        tt(ki, kT, ki, ALU.mult, t_e2)
        t_qd = stt(qd, qT, 128 ** -0.5, qd, ALU.mult, ALU.mult, t_e1, t_qk)
        ktT = alloc(1024)
        ktT4 = ktT.rearrange("p (i h k) -> p i h k", i=2, h=4)
        t_ktT = []
        for i in range(2):
            b = Bank()
            for h in range(4):
                t = tr(b.ap[:, h * P:(h + 1) * P], kt[:, h * 256 + i * P:h * 256 + (i + 1) * P], ident, b.free,
                       t_ktail, mark=(h == 3))
            t = cp(ktT[:, i * 512:(i + 1) * 512], b.ap, t, eng="act")
            b.done(t)
            t_ktT.append(t)
        AT = alloc(1024)
        t_AT = []
        for i in range(2):
            b = Bank()
            for h in range(4):
                s = slice(h * 256 + i * P, h * 256 + (i + 1) * P)
                t = mm(b.ap[:, h * P:(h + 1) * P], ki[:, s], qd[:, s], True, True, b.free, t_qd, mark=(h == 3))
            a = AT[:, i * 512:(i + 1) * 512]
            t = cp(a, b.ap, t, eng="act")
            b.done(t)
            aff(v2(a, 4), [[0, 4], [1, 128]], 0, -1, t)
            t_AT.append(aff(v2(a, 4)[:, :, 64:128], [[0, 4], [0, 64]], -64, 1))
        vt3 = v2(vt, 2)
        sv, su, sr, ga, gb = alloc(2048), alloc(2048), alloc(2048), alloc(2048), alloc(2048)

        def project(c0, dst, func):
            d3 = v2(dst, 2)
            for j in range(4):
                w = Tile(win_d[c0 + j], 2048)
                b = Bank()
                t = tok(w, HT3, b, 8, 256)
                t = act(d3[:, :, j * 256:(j + 1) * 256], v2(b.ap, 2), func, t, link=False)
                b.done(t)
            return t

        t_v = project(4, vt, ACT.Copy)
        S = [alloc(1024) for _ in range(3)]
        t_S = [None] * 4
        for c in range(3):
            rows = slice(64 * (c % 2), 64 * (c % 2) + 64)
            for j in range(2):
                b = Bank()
                for i in range(2):
                    h = 2 * j + i
                    t = mm(b.ap[:, i * 256:(i + 1) * 256], ktT4[rows, c // 2, h, :],
                           vt3[rows, c // 2, h * 256:(h + 1) * 256], True, True, b.free, t_ktT[c // 2], t_v,
                           mark=(i == 1))
                for i in range(2):
                    h = 2 * j + i
                    d = S[c][:, h * 256:(h + 1) * 256]
                    if c == 0:
                        u = cp(d, b.ap[:, i * 256:(i + 1) * 256], t)
                    else:
                        u = stt(d, S[c - 1][:, h * 256:(h + 1) * 256], egl[:, 4 * h + c:4 * h + c + 1],
                                b.ap[:, i * 256:(i + 1) * 256], ALU.mult, ALU.add, t, t_egl)
                b.done(u)
            t_S[c + 1] = u
        o = G[:, 2048:4096]
        so = stats(8)
        t_o = []
        for i in range(2):
            for j in range(2):
                b = Bank()
                for m in range(2):
                    h = 2 * j + m
                    oc = slice(m * 256, (m + 1) * 256)
                    t = mm(b.ap[:, oc], AT[:, i * 512 + h * P:i * 512 + (h + 1) * P],
                           vt3[:, i, h * 256:(h + 1) * 256], True, False, b.free, t_AT[i], t_v)
                    for c in (2 * i, 2 * i + 1):
                        if c == 0:
                            continue
                        r = slice(64 * (c % 2), 64 * (c % 2) + 64)
                        t = mm(b.ap[r, oc], qd[:, h * 256 + c * 64:h * 256 + c * 64 + 64],
                               S[c - 1][:, h * 256:(h + 1) * 256], False, c % 2 == 1, t_S[c],
                               mark=(c % 2 == 1 and m == 1))
                dst = o[:, i * 1024 + j * 512:i * 1024 + (j + 1) * 512]
                t = cp(dst, b.ap, t)
                b.done(t)
                for m in range(2):
                    n = i * 4 + 2 * j + m
                    t_o = act(xn[:, m * 256:(m + 1) * 256], dst[:, m * 256:(m + 1) * 256], ACT.Square, t,
                              accum=so[:, n:n + 1])
        ro, t_ro = rstd(so, 8, 256, t_o)
        for n in range(8):
            s = slice(n * 256, (n + 1) * 256)
            hs = slice((n % 4) * 256, (n % 4) * 256 + 256)
            t_on = stt(o[:, s], o[:, s], ro[:, n:n + 1], gws[:, hs], ALU.mult, ALU.mult, t_rows, t_ro, link=False)
        t_sv = project(16, sv, ACT.Gelu)
        sv3, xn3 = v2(sv, 2), v2(xn, 2)
        mu, sq = stats(2), stats(2)
        rsum(mu, sv3, ALU.add, t_sv)
        ts(mu, mu, -1.0 / D, None, ALU.mult, None)
        for i in range(2):
            t = ts(sv3[:, i, :], sv3[:, i, :], mu[:, i:i + 1], None, ALU.add, None)
        t = sumsq(sv3, sq, xn3[:, 0, :], t)
        t_su = project(12, su, ACT.Gelu)
        rl, _ = rstd(sq, 2, D, t)
        for i in range(2):
            stt(sv3[:, i, :], sv3[:, i, :], rl[:, i:i + 1], lnw, ALU.mult, ALU.mult, t_rows)
            t_ln = tt(sv3[:, i, :], sv3[:, i, :], lnb, ALU.add)
        t_r = project(8, sr, ACT.Silu)
        sg = []
        for i in range(2):
            for j in range(2):
                b = Bank()
                for m in range(4):
                    g = 4 * j + m
                    t = mm(b.ap[:, m * P:(m + 1) * P], sgw[:, g * P:(g + 1) * P], sv3[:, i, g * P:(g + 1) * P], True,
                           True, b.free, t_sgw, t_ln, mark=(m == 3))
                for m in range(4):
                    g = 4 * j + m
                    d = v2(su, 2)[:, i, g * P:(g + 1) * P]
                    t_s = stt(d, b.ap[:, m * P:(m + 1) * P], col["sgu_b"][:, g:g + 1], d, ALU.add, ALU.mult, t, t_su,
                              link=False)
                b.done(t_s)
        t_m = tt(o, o, sr, ALU.mult, t_r)
        t_ga = project(20, ga, ACT.Sigmoid)
        t_gb = project(24, gb, ACT.Sigmoid)
        tt(o, o, ga, ALU.mult, t_ga)
        t_u = tt(su, su, gb, ALU.mult, t_gb, eng="pool") if False else tt(su, su, gb, ALU.mult, t_gb)
        t_m = tt(o, o, su, ALU.add)
        mT = big
        mT3 = v2(mT, 8)
        t_mT = []
        for i in range(2):
            t_mT += transposes(v2(o, 2)[:, i, :], 8, lambda k, n, i=i: mT3[:, k:k + n, i * P:(i + 1) * P], t_m)
        gB = sr[:, 0:1024]
        t_gB = spread(MOD[:, 16:24], gB, t_m)
        for j in range(4):
            w = Tile(wout_d[j], 2048)
            b = Bank()
            t = tok(w, mT3, b, 8, 256, t_mT)
            y = v2(ga, 4)[:, j, :]
            g = gB[:, j * 256:(j + 1) * 256].unsqueeze(1).to_broadcast([P, 2, 256])
            t = tt(v2(y, 2), v2(b.ap, 2), g, ALU.mult, t, t_gB)
            b.done(t)
            t_x = tt(X3[:, :, j * 256:(j + 1) * 256], X3[:, :, j * 256:(j + 1) * 256], v2(y, 2), ALU.add)

        phase()
        t_h = norm_T(X3, A2, MOD[:, 24:32], alloc(2048), alloc(1024), t_x)
        keys = alloc(256)
        t_keys = load("keys", keys, keys_d[:, :], Q.last("act"), Q.last("dve"), eng="act")
        SC = alloc(4096)
        SC2 = alloc(256)
        qh = [alloc(512), alloc(512)]
        qfree = [None, None]
        V16, I16 = alloc(512), alloc(512).bitcast(U32)
        V5 = V16.rearrange("p (i s h k) -> p i s h k", i=2, s=2, h=8)
        I5 = I16.rearrange("p (i s h k) -> p i s h k", i=2, s=2, h=8)

        def top16(vals, vo, io, work, *w):
            def vmax(out, in_, *w):
                return Q.put("dve", lambda e: e.max(out, in_), [own("dve", True), list(w)])

            def vidx(out, m, in_, *w):
                return Q.put("dve", lambda e: e.max_index(out, m, in_), [own("dve", True), list(w)])

            vmax(vo[:, 0:8], vals, *w)
            vidx(io[:, 0:8], vo[:, 0:8], vals)
            Q.put("dve", lambda e: e.match_replace(work, vo[:, 0:8], vals, NEG), [own("dve", True)])
            vmax(vo[:, 8:16], work)
            return vidx(io[:, 8:16], vo[:, 8:16], work)

        for h in range(8):
            w = Tile(wq_d[h], 2048)
            b = Bank()
            t = feat(w, HT3, b, 8, t_h)
            q = qh[h % 2]
            t_q = cp(q, b.ap, t, qfree[h % 2], eng="act", link=False)
            b.done(t_q)
            b = Bank()
            for i in range(2):
                for s in range(2):
                    t = mm(b.ap[:, (i * 2 + s) * P:(i * 2 + s + 1) * P], q[:, s * 256 + i * P:s * 256 + (i + 1) * P],
                           keys[:, s * P:(s + 1) * P], True, True, b.free, t_q, t_keys, mark=(i == 1 and s == 1))
            qfree[h % 2] = t
            sc = SC[:, h * 512:(h + 1) * 512]
            t = cp(sc, b.ap, t, eng="act", link=False)
            b.done(t)
            for i in range(2):
                for s in range(2):
                    top16(sc[:, (i * 2 + s) * P:(i * 2 + s + 1) * P], V5[:, i, s, h, :], I5[:, i, s, h, :],
                          SC2[:, 0:P], t)
        IF = alloc(512)
        cp(IF, I16)
        I5f = IF.rearrange("p (i s h k) -> p i s h k", i=2, s=2, h=8)
        gateT, i1T, i2T = IDX[:, 0:256], IDX[:, 256:512], IDX[:, 512:768]
        t_idx = []
        for i in range(2):
            cand = alloc(2048)
            c4 = cand.rearrange("p (h a b) -> p h a b", h=8, a=16)
            tt(c4, V5[:, i, 0, :, :].unsqueeze(3).to_broadcast([P, 8, 16, 16]),
               V5[:, i, 1, :, :].unsqueeze(2).to_broadcast([P, 8, 16, 16]), ALU.add)
            tv, tp = alloc(128), alloc(128).bitcast(U32)
            for h in range(8):
                top16(cand[:, h * 256:(h + 1) * 256], tv[:, h * 16:(h + 1) * 16], tp[:, h * 16:(h + 1) * 16], SC2)
            sel = []
            for s in range(2):
                pu, pf, res = alloc(128).bitcast(U32), alloc(128), alloc(128)
                if s == 0:
                    ts(pu, tp, 4, None, ALU.logical_shift_right, None)
                else:
                    ts(pu, tp, 15, None, ALU.bitwise_and, None)
                cp(pf, pu)
                oh = cand.rearrange("p (n a) -> p n a", a=16)
                tt(oh, pf.unsqueeze(2).to_broadcast([P, 128, 16]),
                   iota[:, 0:16].unsqueeze(1).to_broadcast([P, 128, 16]), ALU.is_equal)
                oh4 = cand.rearrange("p (h k a) -> p h k a", h=8, k=16)
                tt(oh4, oh4, I5f[:, i, s, :, :].unsqueeze(2).to_broadcast([P, 8, 16, 16]), ALU.mult)
                rsum(res, oh, ALU.add)
                sel.append(res)
            gt = alloc(128)
            tv3, gt3 = v2(tv, 8), v2(gt, 8)
            sm = stats(8)
            t = tt(gt3, tv3, tv3[:, :, 0:1].to_broadcast([P, 8, 16]), ALU.subtract)
            t = act(gt, gt, ACT.Exp, t)
            rsum(sm, gt3, ALU.add, t)
            recip(sm, sm)
            t = tt(gt3, gt3, sm.unsqueeze(2).to_broadcast([P, 8, 16]), ALU.mult)
            b = Bank()
            for n, src in enumerate((gt, sel[0], sel[1])):
                t = tr(b.ap[:, n * P:(n + 1) * P], src, ident, b.free, t, mark=(n == 2))
            u = cp(v2(IDX[:, :], 3)[:, :, i * P:(i + 1) * P], v2(b.ap[:, 0:384], 3), t)
            b.done(u)
            t_idx.append(u)
        ph = phase()
        G3 = G[:, :].rearrange("p (e t) -> p e t", t=256)
        oh_free = [None] * 4
        for t4 in range(64):
            b = Bank()
            for m in range(4):
                tk = 4 * t4 + m
                n = tk % 4
                o1, o2 = TMP[:, n * 256:n * 256 + 128], TMP[:, n * 256 + 128:n * 256 + 256]
                ts(o1, iota, i1T[:, tk:tk + 1], gateT[:, tk:tk + 1], ALU.is_equal, ALU.mult, oh_free[n], t_idx,
                   link=False)
                t = ts(o2, iota, i2T[:, tk:tk + 1], None, ALU.is_equal, None, oh_free[n], link=False)
                t = mm(b.ap[:, m * P:(m + 1) * P], o1, o2, True, True, b.free, t, mark=True)
                oh_free[n] = t
            t_G = cp(G3[:, :, 4 * t4:4 * t4 + 4], b.ap.rearrange("p (m e) -> p e m", m=4), t, eng="act", link=False)
            b.done(t_G)

        def two_products(n, first, middle, second, lag=2):
            for j in range(n + lag):
                if j < n:
                    first(j)
                    middle(j)
                if j >= lag:
                    second(j - lag)

        acc = [Bank(i) for i in range(4)]
        use_banks([4, 5, 6, 7])
        held = {}
        wfree = [None] * 4

        def peer_first(j):
            w = Tile(peer_d[j], 2048)
            b = Bank()
            w3 = v2(w.ap[:, 0:1024], 8)
            for k in range(8):
                t = mm(b.ap[:, 0:256], w3[:, k, :], HT3[:, k, :], k == 0, k == 7, b.free, w.t, mark=(k == 7))
            held[j] = [w, b, t]

        def peer_middle(j):
            w, b, t = held[j]
            a = TMP[:, (j % 4) * 256:(j % 4) * 256 + 256]
            t = act(a, b.ap[:, 0:256], ACT.Gelu, t, wfree[j % 4], link=False)
            b.done(t)
            held[j] = [w, a, tt(a, a, G3[:, j, :], ALU.mult, t, t_G, link=False)]

        def add_up(j, wide, w, a, t, n):
            for i in range(2):
                for h in range(2):
                    c = acc[2 * i + h]
                    u = mm(c.ap, a[:, i * P:(i + 1) * P], wide[:, h * 512:(h + 1) * 512], j == 0, j == n - 1, c.free,
                           t, mark=(i == 1 and h == 1))
            w.done(u)
            wfree[j % 4] = u
            return u

        def peer_second(j):
            w, a, t = held.pop(j)
            held["y"] = add_up(j, w.ap[:, 1024:2048], w, a, t, 128)

        two_products(128, peer_first, peer_middle, peer_second)
        phase()
        gB, fn, Y = alloc(1024), alloc(1024), alloc(2048)
        t_fn = load("row", fn, rows_d[3072:4096].partition_broadcast(P), eng="act")
        t_gB = spread(MOD[:, 40:48], gB)
        for i in range(2):
            for h in range(2):
                c = acc[2 * i + h]
                s = slice(h * 512, (h + 1) * 512)
                y = v2(Y, 2)[:, i, s]
                t = tt(y, c.ap, gB[:, s], ALU.mult, held["y"], t_gB, link=False)
                c.done(t)
                t_x = tt(X3[:, i, s], X3[:, i, s], y, ALU.add, t)
        ss = stats(2)
        t = sumsq(X3, ss, alloc(1024), t_x)
        r, _ = rstd(ss, 2, D, t)
        for i in range(2):
            t_x = stt(X3[:, i, :], X3[:, i, :], r[:, i:i + 1], fn, ALU.mult, ALU.mult, t_fn)
        use_banks(list(range(8)))

        phase()
        XC3 = v2(alloc(2048), 2)
        t_xc = load("xc", XC3, ctx_d.rearrange("b (i p) d -> p (b i) d", p=P))
        KM, KD, KG = alloc(2048), alloc(1024), alloc(1024)
        VV = alloc(4 * 640)
        QM, QD, QG = alloc(1024), alloc(512), alloc(1024)
        KM3, KD3, KG3 = v2(KM, 4), v2(KD, 2), v2(KG, 2)
        VV3 = v2(VV, 4)
        QM3, QD3, QG3 = v2(QM, 4), v2(QD, 2), v2(QG, 4)
        kept = heap["n"]

        def rope(x4, cs, sn, n, half, *w):
            c = v2(cs, 2).unsqueeze(2).to_broadcast([P, 2, n, half])
            s = v2(sn, 2).unsqueeze(2).to_broadcast([P, 2, n, half])
            a, b2 = alloc(2 * n * half), alloc(2 * n * half)
            a4 = a.rearrange("p (i n d) -> p i n d", i=2, n=n)
            b4 = b2.rearrange("p (i n d) -> p i n d", i=2, n=n)
            x1, x2 = x4[:, :, :, 0:half], x4[:, :, :, half:2 * half]
            tt(a4, x1, s, ALU.mult, *w)
            tt(b4, x2, s, ALU.mult)
            tt(x1, x1, c, ALU.mult)
            tt(x1, x1, b4, ALU.subtract)
            tt(x2, x2, c, ALU.mult)
            return tt(x2, x2, a4, ALU.add)

        def qkv(l, s, x3, m, k0, queries, *w):
            phase(kept)
            PJ = alloc(2 * 1952)
            PJ3 = v2(PJ, 2)
            xn, junk = alloc(2048), alloc(1024)
            t_h = norm_T(x3, m["A"], m["B"], xn, junk, *w)
            small = [alloc(768), alloc(512)]
            t_wqb = load("wqb", small[0], wqb_d[l], eng="act")
            t_wkvb = load("wkvb", small[1], wkvb_d[l], eng="act")
            tp = {}
            for j in ([7, 0, 4, 5, 6, 1, 2, 3] if queries else [7, 6, 2, 3]):
                n = 160 if j == 7 else 256
                wt = Tile(win2k_d[l] if j == 7 else win2_d[l, j], 8 * n)
                b = Bank()
                t = tok(wt, HT3, b, 8, n, t_h)
                e = "act" if j % 2 else "dve"
                tp[j] = cp(PJ3[:, :, j * 256:j * 256 + n], v2(b.ap[:, 0:2 * n], 2), t, eng=e, link=False)
                b.done(tp[j])
            rot_small = s == 0

            def low_rank(c0, kc, g, wb, t_wb, n, *w):
                width = kc * P
                ssx = stats(2)
                for i in range(2):
                    t = act(junk[:, 0:width], PJ3[:, i, c0:c0 + width], ACT.Square, *w, accum=ssx[:, i:i + 1])
                r, _ = rstd(ssx, 2, width, t)
                aT, tm = alloc(kc * 256), alloc(kc * 256)
                aT3 = v2(aT, kc)
                b = Bank()
                for i in range(2):
                    t = ts(tm[:, i * width:(i + 1) * width], PJ3[:, i, c0:c0 + width], r[:, i:i + 1], None, ALU.mult,
                           None)
                    for k in range(kc):
                        t = tr(b.ap[:, k * 256 + i * P:k * 256 + (i + 1) * P],
                               tm[:, i * width + k * P:i * width + (k + 1) * P], ident, b.free, t, mark=True)
                for k in range(kc):
                    u = ts(aT3[:, k, :], b.ap[:, k * 256:(k + 1) * 256], g[:, k:k + 1], None, ALU.mult, None, t)
                b.done(u)
                out = []
                for i in range(2):
                    b = Bank()
                    for k in range(kc):
                        t = mm(b.ap[:, 0:n], aT3[:, k, i * P:(i + 1) * P], v2(wb, kc)[:, k, :], k == 0, k == kc - 1,
                               b.free, u, t_wb, mark=(k == kc - 1))
                    out.append((b, t))
                return out

            def turned(srcs, dst, rows, *w):
                for i in range(2):
                    b = Bank()
                    for n, a in enumerate(srcs(i)):
                        t = tr(b.ap[0:rows, n * P:(n + 1) * P], a, ident, b.free, *w, mark=True)
                    us = [cp(d, v2(b.ap[0:rows, f * P:(f + c) * P], c), t, eng=("act" if i else "dve"), link=False)
                          for d, f, c in dst(i)]
                    b.done(*us)
                    tq.append(us)

            tq = []
            KA = alloc(768)
            KA4 = KA.rearrange("p (i h d) -> p i h d", i=2, h=4)
            out = low_rank(1792, 1, col[f"mkv{l}"], small[1], t_wkvb, 512, tp[7])
            for i, (b, t) in enumerate(out):
                kv = b.ap.rearrange("p (h d) -> p h d", h=4)
                cp(KA4[:, i, :, 0:64], kv[:, :, 0:64], t)
                u = cp(VV3[:, k0 + i, 0:256].rearrange("p (h d) -> p h d", h=4), kv[:, :, 64:128])
                b.done(u)
            kpe = PJ3[:, :, 1920:1952].unsqueeze(2)
            if rot_small:
                rope(kpe, con["cosS"], con["sinS"], 1, 16, tp[7])
            t = cp(KA4[:, :, :, 64:96], kpe.to_broadcast([P, 2, 4, 32]), tp[7])
            keyT = slice(k0 * P, k0 * P + P)

            def kcols(i):
                return slice((k0 + i) * P, (k0 + i + 1) * P)

            turned(lambda i: [KA4[:, i, h, :] for h in range(4)],
                   lambda i: [(KM3[0:96, :, kcols(i)], 0, 4)], 96, t)
            n0 = 0 if queries else 8
            hd = PJ3[:, :, 1024:1664].rearrange("p i (n d) -> p i n d", d=64)[:, :, n0:10, :]
            nh = 10 - n0
            sqt = alloc(2 * nh * 64)
            sq4 = sqt.rearrange("p (i n d) -> p i n d", i=2, n=nh)
            ssg = stats(2 * nh)
            t = tt(sq4, hd, hd, ALU.mult, [tp[j] for j in tp])
            t = rsum(v2(ssg, 2), sq4, ALU.add)
            r, _ = rstd(ssg, 2 * nh, 64, t)
            tt(hd, hd, v2(r, 2).unsqueeze(3).to_broadcast([P, 2, nh, 64]), ALU.mult)
            for i in range(2):
                if queries:
                    tt(hd[:, i, 0:8, :], hd[:, i, 0:8, :],
                       srow[:, 320 * l + 64:320 * l + 128].unsqueeze(1).to_broadcast([P, 8, 64]), ALU.mult)
                t = tt(hd[:, i, nh - 2:nh, :], hd[:, i, nh - 2:nh, :],
                       srow[:, 320 * l + 128:320 * l + 192].unsqueeze(1).to_broadcast([P, 2, 64]), ALU.mult)
            if rot_small:
                t = rope(hd, con["cosL"], con["sinL"], nh, 32)
            KK = alloc(512)
            KK5 = KK.rearrange("p (i n u d) -> p i n u d", i=2, n=2, u=2)
            for i in range(2):
                t = cp(KK5[:, i, :, :, :], hd[:, i, nh - 2:nh, :].unsqueeze(2).to_broadcast([P, 2, 2, 64]))
            turned(lambda i: [KK[:, i * 256 + n * P:i * 256 + (n + 1) * P] for n in range(2)],
                   lambda i: [(KG3[:, :, kcols(i)], 0, 2)], P, t)
            if queries:
                turned(lambda i: [PJ3[:, i, 1024 + n * P:1024 + (n + 1) * P] for n in range(4)],
                       lambda i: [(QG3[:, :, i * P:(i + 1) * P], 0, 4)], P, t)
            if rot_small:
                dd = PJ3[:, :, 256:768].rearrange("p i (n d) -> p i n d", d=32)
                t = rope(dd, con["cosS"], con["sinS"], 16, 16)
            if queries:
                turned(lambda i: [PJ3[:, i, 256 + n * P:256 + (n + 1) * P] for n in range(4)],
                       lambda i: [(QD3[:, :, i * P:(i + 1) * P], 0, 2), (KD3[:, :, kcols(i)], 2, 2)], P, t,
                       tp[1], tp[2])
            else:
                turned(lambda i: [PJ3[:, i, 512 + n * P:512 + (n + 1) * P] for n in range(2)],
                       lambda i: [(KD3[:, :, kcols(i)], 0, 2)], P, t, tp[2])
            cp(VV3[:, k0:k0 + 2, 256:512], PJ3[:, :, 768:1024], tp[3])
            t_vv = cp(VV3[:, k0:k0 + 2, 512:640], PJ3[:, :, 1664:1792], tp[6])
            if queries:
                out = low_rank(0, 2, col[f"mq{l}"], small[0], t_wqb, 384, tp[0])
                QA = alloc(768)
                QA4 = QA.rearrange("p (i h d) -> p i h d", i=2, h=4)
                for i, (b, t) in enumerate(out):
                    u = cp(QA[:, i * 384:(i + 1) * 384], b.ap[:, 0:384], t)
                    b.done(u)
                t = u
                if rot_small:
                    t = rope(QA4[:, :, :, 64:96], con["cosS"], con["sinS"], 4, 16)
                turned(lambda i: [QA4[:, i, h, :] for h in range(4)],
                       lambda i: [(QM3[0:96, :, i * P:(i + 1) * P], 0, 4)], 96, t)

        def attend(l, kt0, nk):
            phase(kept)
            W = nk * P
            PR = [alloc(512) for _ in range(3)]
            PT = [alloc(512) for _ in range(3)]
            pfree, ptfree = [None] * 3, [None] * 3
            Yt = alloc(2048)
            units = []
            for i in range(2):
                for h in range(4):
                    units.append((i, 0, h, QM3[0:96, h], KM3[0:96, h], 64 * h, 0, h == 3))
                for h in range(8):
                    r = slice(32 * (h % 4), 32 * (h % 4) + 32)
                    units.append((i, 1, h, QD3[r, h // 4], KD3[r, h // 4], 256 + 64 * (h // 2), 1, h == 7))
                for h in range(8):
                    r = slice(64 * (h % 2), 64 * (h % 2) + 64)
                    units.append((i, 2, h, QG3[r, h // 2], KG3[r, h // 4], 512 + 64 * (h // 4), 2, h == 7))
            use_banks([0, 1, 2, 3, 4, 5])
            obank = {}
            done = []
            rs = {}
            info = {}
            N = len(units)

            def score(n):
                i, kind, h, q, k, _, _, _ = units[n]
                b = Bank()
                t = mm(b.ap[:, 0:W], q[:, i * P:(i + 1) * P], k[:, kt0 * P:kt0 * P + W], True, True, b.free,
                       mark=True)
                if h == 0:
                    rs[(i, kind)] = alloc(8)
                mx = stats(2)
                rsum(mx[:, 0:1], b.ap[:, 0:W], ALU.max, t, link=False)
                t = ts(mx[:, 1:2], mx[:, 0:1], -SCALES[kind], None, ALU.mult, None)
                t = act(PR[n % 3][:, 0:W], b.ap[:, 0:W], ACT.Exp, t, pfree[n % 3], bias=mx[:, 1:2],
                        scale=SCALES[kind], accum=rs[(i, kind)][:, h:h + 1], link=False)
                b.done(t)
                info[n] = t

            def turn(n):
                b = Bank()
                for k in range(nk):
                    t = tr(b.ap[:, k * P:(k + 1) * P], PR[n % 3][:, k * P:(k + 1) * P], ident, b.free, info[n],
                           mark=(k == nk - 1))
                pfree[n % 3] = t
                t = cp(PT[n % 3][:, 0:W], b.ap[:, 0:W], t, ptfree[n % 3], eng=("act" if n % 3 == 0 else "dve"),
                       link=False)
                b.done(t)
                info[n] = [t, info[n]]

            def values(n):
                i, kind, h, _, _, vc, _, final = units[n]
                if h == 0:
                    obank[(i, kind)] = Bank(6 + (3 * i + kind) % 2)
                b = obank[(i, kind)]
                for k in range(nk):
                    t = mm(b.ap[:, 64 * h:64 * h + 64], PT[n % 3][:, k * P:(k + 1) * P],
                           VV3[:, kt0 + k, vc:vc + 64], k == 0, k == nk - 1, b.free, info[n], mark=(k == nk - 1))
                ptfree[n % 3] = t
                if not final:
                    return
                c = [4, 8, 8][kind]
                r = rs[(i, kind)]
                recip(r[:, 0:c], r[:, 0:c], t, info[n])
                o3 = b.ap[:, 0:64 * c].rearrange("p (h d) -> p h d", h=c)
                rb = r[:, 0:c].unsqueeze(2).to_broadcast([P, c, 64])
                y = Yt[:, i * 1024:(i + 1) * 1024]
                if kind != 1:
                    d = y[:, 0:256] if kind == 0 else y[:, 512:1024]
                    t = tt(d.rearrange("p (h d) -> p h d", h=c), o3, rb, ALU.mult, t)
                    b.done(t)
                    done.append(t)
                    return
                on, sqd = alloc(512), alloc(256)
                t = tt(on.rearrange("p (h d) -> p h d", h=8), o3, rb, ALU.mult, t)
                b.done(t)
                on4 = on.rearrange("p (h u d) -> p h u d", h=4, u=2)
                d3 = y[:, 256:512].rearrange("p (h d) -> p h d", h=4)
                stt(d3, on4[:, :, 1, :], lamc[:, l:l + 1], on4[:, :, 0, :], ALU.mult, ALU.add)
                s3 = sqd.rearrange("p (h d) -> p h d", h=4)
                tt(s3, d3, d3, ALU.mult)
                sd = stats(4)
                t = rsum(sd, s3, ALU.add)
                r2, _ = rstd(sd, 4, 64, t)
                tt(d3, d3, r2.unsqueeze(2).to_broadcast([P, 4, 64]), ALU.mult)
                done.append(tt(d3, d3, srow[:, 320 * l:320 * l + 64].unsqueeze(1).to_broadcast([P, 4, 64]),
                               ALU.mult))

            for n in range(N + 2):
                if n < N:
                    score(n)
                if 1 <= n <= N:
                    turn(n - 1)
                if n >= 2:
                    values(n - 2)
            use_banks(list(range(8)))
            out = []
            for i in range(2):
                out += transposes(Yt[:, i * 1024:(i + 1) * 1024], 8,
                                  lambda k, n, i=i: HT3[:, k:k + n, i * P:(i + 1) * P], done)
            return out

        def add_normed(x3, Y, junk, gB, *w):
            ssx = stats(2)
            t = sumsq(v2(Y, 2), ssx, junk, *w)
            r, _ = rstd(ssx, 2, D, t)
            for i in range(2):
                y = v2(Y, 2)[:, i, :]
                stt(y, y, r[:, i:i + 1], gB, ALU.mult, ALU.mult, *w)
                t = tt(x3[:, i, :], x3[:, i, :], y, ALU.add)
            return t

        def out_proj(l, x3, m, t_y):
            phase(kept)
            gB, Y, junk = alloc(1024), alloc(2048), alloc(1024)
            t_gB = spread(m["ga"], gB)
            for j in range(4):
                w = Tile(wout2_d[l, j], 2048)
                b = Bank()
                t = tok(w, HT3, b, 8, 256, t_y)
                t = cp(v2(Y, 2)[:, :, j * 256:(j + 1) * 256], v2(b.ap, 2), t, eng="act", link=False)
                b.done(t)
            return add_normed(x3, Y, junk, gB, t, t_gB)

        def ffn(l, x3, m, t_x):
            phase(kept)
            gB, Y, junk = alloc(1024), alloc(2048), alloc(1024)
            norm_T(x3, m["FA"], m["FB"], Y, junk, t_x)
            t_gB = spread(m["gf"], gB)
            t_h = everything()
            acc[:] = [Bank(i) for i in range(4)]
            use_banks([4, 5, 6, 7])
            hb = alloc(1024)
            held.clear()
            wfree[:] = [None] * 4

            def first(j):
                w = Tile(ffn_d[l, j], 2048)
                b = Bank()
                t = feat(w, HT3, b, 8, t_h)
                held[j] = [b, t]

            def middle(j):
                b, t = held[j]
                a = hb[:, (j % 4) * 256:(j % 4) * 256 + 256]
                u = act(a, b.ap[:, 0:256], ACT.Silu, t, wfree[j % 4], link=False)
                u = tt(a, a, b.ap[:, 256:512], ALU.mult, u, link=False)
                b.done(u)
                held[j] = [a, u]

            def second(j):
                a, t = held.pop(j)
                if j % 2 == 0:
                    held["w"] = Tile(ffd_d[l, j // 2], 2048)
                w = held["w"]
                held["y"] = add_up(j, w.ap[:, (j % 2) * 1024:(j % 2) * 1024 + 1024], w, a, [t, w.t], NF)

            two_products(NF, first, middle, second)
            t = []
            for i in range(2):
                for h in range(2):
                    c = acc[2 * i + h]
                    u = cp(v2(Y, 2)[:, i, h * 512:(h + 1) * 512], c.ap, held["y"], eng="act" if h else "dve",
                           link=False)
                    c.done(u)
                    t.append(u)
            use_banks(list(range(8)))
            return add_normed(x3, Y, junk, gB, t, t_gB)

        for l in range(2):
            qkv(l, 1, XC3, cxt[l], 2, l == 0, t_xc)
            if l == 0:
                t_y = attend(l, 2, 2)
                t_xc = out_proj(l, XC3, cxt[l], t_y)
                t_xc = ffn(l, XC3, cxt[l], t_xc)
            qkv(l, 0, X3, lat[l], 0, True, t_x)
            t_y = attend(l, 0, 4)
            t_x = out_proj(l, X3, lat[l], t_y)
            t_x = ffn(l, X3, lat[l], t_x)
        t = load("out", out_d.rearrange("b (i p) d -> p (b i) d", p=P), X3, t_x)
        Q.wait("sp", [t])

        block = st.enter_context(nc.Block())

        def run(eng, name):
            for op in Q.ops[name]:
                if op[0] == "w":
                    eng.wait_ge(op[1], op[2])
                else:
                    ins = op[1](eng)
                    if op[2] is not None:
                        ins.then_inc(op[2], op[3])

        @block.sync
        def _(eng):
            run(eng, "sp")

        @block.gpsimd
        def _(eng):
            run(eng, "pool")

        @block.scalar
        def _(eng):
            run(eng, "act")

        @block.vector
        def _(eng):
            run(eng, "dve")

        @block.tensor
        def _(eng):
            run(eng, "pe")


def constants():
    c = np.zeros((P, NCON), np.float32)
    c[:, 0:128] = np.eye(P, dtype=np.float32)
    c[:, 128:256] = np.arange(P, dtype=np.float32)[None, :]
    tok_ = np.arange(256)
    row, colm = (tok_ // 64).astype(np.float32), (tok_ % 64).astype(np.float32)
    for name, rot in (("S", 32), ("L", 64)):
        q = rot // 4
        inv = np.power(np.float32(10000.0), -np.arange(q, dtype=np.float32) / np.float32(q)).astype(np.float32)
        ang = np.concatenate([row[:, None] * inv, colm[:, None] * inv], axis=-1).astype(np.float32)
        for f, a in (("cos", np.cos(ang)), ("sin", np.sin(ang))):
            o, w = CONS[f + name]
            c[:, o:o + w] = a.astype(np.float32).reshape(2, P, w // 2).transpose(1, 0, 2).reshape(P, w)
    return c


def kernel(**inputs):
    import concourse.bacc as bacc
    from concourse.bass_utils import run_bass_kernel_spmd as launch

    a = {k: np.asarray(v) for k, v in inputs.items()}
    f = np.float32

    def c8(v):
        return v.reshape(-1, P).T

    def tiles(w, n):
        k = w.shape[0] // P
        return w.reshape(k, P, w.shape[1] // n, n).transpose(2, 1, 0, 3).reshape(w.shape[1] // n, P, k * n)

    cols = np.concatenate(
        [c8(a["c"][0]), c8(a["c_2"][0]), c8(a["c_ctx_2"]), c8(a["b_ada"][0]), c8(a["b_ada_2"][0]),
         c8(a["b_ada_2"][1]), c8(a["norm1_w"][0]), c8(a["norm2_w"][0])]
        + [c8(a[n][l]) for n in ("g_attn_pre_2", "g_attn_post_2", "g_ffn_pre_2", "g_ffn_post_2") for l in range(2)]
        + [c8(a["g_mla_q_2"][l]) for l in range(2)] + [c8(a["g_mla_kv_2"][l]) for l in range(2)]
        + [c8(a["b_alpha"][0]), a["sgu_b"][0].T], axis=1)
    rows = np.concatenate(
        [a["gla_norm_w"][0], a["sgu_ln_w"][0], a["sgu_ln_b"][0], a["final_norm_w"]]
        + [a[n][l] for l in range(2) for n in ("g_diff_sub_2", "g_gqa_q_2", "g_gqa_k_2", "lambda_q1_2",
                                               "lambda_k1_2", "lambda_q2_2", "lambda_k2_2")])
    win = a["w_in"][0]
    e = a["peer_down"][0].reshape(P, P, 8, P).transpose(1, 3, 2, 0).reshape(P, P, D)
    u = a["peer_up"][0].reshape(P, P, D).transpose(1, 0, 2)
    w2 = a["w_in_2"]
    o2 = np.cumsum([0, 256, 160, 256, 256, 256, 512, 128, 128])
    qa, kva, dq, dk, dv, gq, gk, gv = [w2[:, :, o2[n]:o2[n + 1]] for n in range(8)]
    w2r = np.concatenate([qa, dq, dk, dv, gq, gk, gv], axis=2)
    ffn = np.concatenate([a["w_ffn_gate_2"].reshape(2, D, NF, 1, P), a["w_ffn_up_2"].reshape(2, D, NF, 1, P)],
                         axis=3).reshape(2, D, NF * 256)
    arrays = {
        "cols": cols,
        "cons": constants(),
        "rows": rows,
        "ada": tiles(a["w_ada"][0], 256),
        "ada2": np.stack([tiles(a["w_ada_2"][l], 256) for l in range(2)]),
        "win": tiles(np.concatenate([win[:, :3072], win[:, 3088:]], axis=1), 256),
        "walr": tiles(win[:, 3072:3088], 16)[0],
        "wau": a["w_alpha_up"][0],
        "sgw": a["sgu_w"][0].transpose(2, 0, 1).reshape(P, 1024),
        "wout": tiles(a["w_out"][0], 256),
        "wq": tiles(a["peer_w_q"][0], 256),
        "keys": np.concatenate([a["peer_keys1"][0].T, a["peer_keys2"][0].T], axis=1),
        "peer": np.concatenate([e, u], axis=2),
        "x": a["x"],
        "ctx": a["ctx_2"],
        "win2": np.stack([tiles(w2r[l], 256) for l in range(2)]),
        "win2k": np.stack([tiles(kva[l], 160)[0] for l in range(2)]),
        "wqb": np.stack([tiles(a["w_mla_qb_2"][l], 384)[0] for l in range(2)]),
        "wkvb": a["w_mla_kvb_2"],
        "wout2": np.stack([tiles(a["w_out_2"][l], 256) for l in range(2)]),
        "ffn": np.stack([tiles(ffn[l], 256) for l in range(2)]),
        "ffd": a["w_ffn_down_2"].reshape(2, NF // 2, 2, P, D).transpose(0, 1, 3, 2, 4).reshape(2, NF // 2, P, 2 * D),
    }
    nc = bacc.Bacc("TRN2", target_bir_lowering=False, num_devices=1)
    maps, args = {}, []
    for name, v in arrays.items():
        v = np.ascontiguousarray(v)
        maps["in_" + name] = v
        args.append(nc.dram_tensor("in_" + name, v.shape, mybir.dt.from_np(v.dtype), kind="ExternalInput").ap())
    args.append(nc.dram_tensor("out_0", (1, 256, D), F32, kind="ExternalOutput").ap())
    build(nc, *args)
    r = launch(nc, [maps], core_ids=[0])
    return r.results[0]["out_0"]
```

```python
from contextlib import ExitStack

import numpy as np
import concourse.bass as bass
from concourse import mybir

ALU = mybir.AluOpType
ACT = mybir.ActivationFunctionType
AX = mybir.AxisListType
F32 = mybir.dt.float32
F32R = mybir.dt.float32r
U32 = mybir.dt.uint32
P = 128
EPS = 1e-6
D = 1024
NEG = -3.0e38
LAM_INIT = [0.8 - 0.6 * float(np.exp(-0.3 * l)) for l in range(2)]
SCALES = [1.0 / float(np.sqrt(96.0)), 1.0 / float(np.sqrt(32.0)), 1.0 / 8.0]
NRAW = 4
NSPL = 3
NF = 22
ENGINES = ("pe", "act", "dve", "pool")

COLS = {}
_n = 0
for _name, _w in [("c", 8), ("c2", 8), ("cc2", 8), ("b_ada", 48), ("b_ada2a", 48), ("b_ada2b", 48), ("norm1", 8),
                  ("norm2", 8), ("apre0", 8), ("apre1", 8), ("apost0", 8), ("apost1", 8), ("fpre0", 8),
                  ("fpre1", 8), ("fpost0", 8), ("fpost1", 8), ("mq0", 2), ("mq1", 2), ("mkv0", 1), ("mkv1", 1),
                  ("b_alpha", 4), ("sgu_b", 8)]:
    COLS[_name] = (_n, _w)
    _n += _w
NCOL = _n
CONS = {}
_n = 0
for _name, _w in [("ident", 128), ("iota", 128), ("cosS", 32), ("sinS", 32), ("cosL", 64), ("sinL", 64), ("sel", 2)]:
    CONS[_name] = (_n, _w)
    _n += _w
NCON = _n


class Thread:

    def __init__(self, name, steps=None):
        self.name, self.steps, self.ready, self.over = name, steps, 0.0, False
        self.last = {}
        self.pend = {}


class Queues:

    def __init__(self, sems):
        self.sem = sems
        self.ops = {e: [] for e in ENGINES + ("sp",)}
        self.count = {e: 0 for e in ENGINES}
        self.seen = {e: {} for e in self.ops}
        self.vals = {}
        self.thread = Thread("start")
        self.clock = 0.0

    def wait(self, eng, tokens):
        for t in tokens:
            if t is None:
                continue
            if isinstance(t, list):
                self.wait(eng, t)
                continue
            name, sem, val = t
            if self.seen[eng].get(name, 0) < val:
                self.seen[eng][name] = val
                self.ops[eng].append(("w", sem, val))

    def put(self, eng, fn, waits, mark=True):
        self.wait(eng, self.thread.pend.pop(eng, []))
        self.wait(eng, waits)
        if not mark:
            self.ops[eng].append(("i", fn, None, 0))
            return None
        self.count[eng] += 1
        self.ops[eng].append(("i", fn, self.sem[eng], 1))
        t = (eng, self.sem[eng], self.count[eng])
        self.thread.last[eng] = t
        return t

    def latest(self, eng):
        return (eng, self.sem[eng], self.count[eng]) if self.count[eng] else None

    def dma(self, eng, out, in_, name, sem, waits):
        self.wait(eng, self.thread.pend.pop("dma", []))
        self.wait(eng, waits)
        self.vals[name] = self.vals.get(name, 0) + 16
        self.ops[eng].append(("i", lambda e: e.dma_start(out, in_), sem, 16))
        return (name, sem, self.vals[name])

    def barrier(self):
        now = list(self.thread.last.values())
        for e in ENGINES + ("dma",):
            self.thread.pend[e] = now + self.thread.pend.get(e, [])


def interleave(q, threads, flags, locks):
    outer = q.thread

    def step(t):
        q.thread = t
        try:
            said = next(t.steps)
        except StopIteration:
            t.over = True
            return
        t.need = None
        if isinstance(said, tuple):
            t.need = said
        else:
            t.ready = q.clock + said

    def blocked(t):
        if t.need is None:
            return False
        kind, key = t.need
        if kind == "flag":
            return key not in flags
        return locks.get(key, t.name) != t.name

    for t in threads:
        t.need = None
    while True:
        alive = [t for t in threads if not t.over]
        if not alive:
            break
        free = [t for t in alive if not blocked(t)]
        assert free
        now = [t for t in free if t.ready <= q.clock]
        if not now:
            q.clock = min(t.ready for t in free)
            continue
        t = now[0]
        if t.need is not None and t.need[0] == "lock":
            locks[t.need[1]] = t.name
        step(t)
    q.thread = outer


def program(nc, dram, out_d, xs_d, order):
    used = []
    with ExitStack() as st:
        def sb(name, words, dt=F32, where=st):
            return where.enter_context(nc.sbuf_tensor(name, [P, words], dt))

        sems = {e: st.enter_context(nc.semaphore("s_" + e)) for e in ENGINES}
        Q = Queues(sems)

        def mm(out, lhsT, rhs, start, stop, *w, mark=False, passes=4):
            n = 1
            for s in rhs.shape[1:]:
                n *= s
            Q.clock += passes * max(n, 64) / 2400.0
            return Q.put("pe", lambda e: e.matmul(out, lhsT, rhs, start=start, stop=stop, skip_group_check=True),
                         w, mark)

        def tr(out, in_, idn, *w, mark=False):
            Q.clock += 0.055
            return Q.put("pe", lambda e: e.transpose(out, in_, idn), w, mark)

        def own(eng, link):
            return Q.latest(eng) if link else None

        def act(out, in_, func, *w, bias=0.0, scale=1.0, accum=None, link=True):
            w = [own("act", link), list(w)]
            if accum is None:
                return Q.put("act", lambda e: e.activation(out, in_, func, bias=bias, scale=scale), w)
            return Q.put("act", lambda e: e.activation(out, in_, func, bias=bias, scale=scale, accum_out=accum), w)

        def tt(out, a, b, op, *w, eng="dve", link=True):
            return Q.put(eng, lambda e: e.tensor_tensor(out, a, b, op), [own(eng, link), list(w)])

        def ts(out, a, s1, s2, op0, op1, *w, link=True):
            if op1 is None:
                return Q.put("dve", lambda e: e.tensor_scalar(out, a, s1, None, op0), [own("dve", link), list(w)])
            return Q.put("dve", lambda e: e.tensor_scalar(out, a, s1, s2, op0, op1), [own("dve", link), list(w)])

        def stt(out, a, s, b, op0, op1, *w, link=True):
            return Q.put("dve", lambda e: e.scalar_tensor_tensor(out=out, in0=a, scalar=s, in1=b, op0=op0, op1=op1),
                         [own("dve", link), list(w)])

        def cp(out, a, *w, eng="dve", link=True):
            if eng == "act":
                return act(out, a, ACT.Copy, *w, link=link)
            return Q.put(eng, lambda e: e.tensor_copy(out, a), [own(eng, link), list(w)])

        def rsum(out, a, op, *w, link=True):
            return Q.put("dve", lambda e: e.tensor_reduce(out, a, AX.X, op), [own("dve", link), list(w)])

        def recip(out, a, *w):
            return Q.put("dve", lambda e: e.reciprocal(out, a), [own("dve", True), list(w)])

        def aff(ap, pattern, base, cm, *w):
            return Q.put("pool", lambda e: e.affine_select(out=ap, in_=ap, compare_op=ALU.is_ge, fill=0.0, base=base,
                                                           pattern=pattern, channel_multiplier=cm),
                         [own("pool", True), list(w)])

        RAW = sb("RAW", NRAW * 1024)
        SPL = sb("SPL", NSPL * 2048, F32R)
        HH, HL = sb("HH", 2048, F32R), sb("HL", 2048, F32R)
        WHL = sb("WHL", 3 * 512, F32R)
        CS = sb("CS", 48, F32R)
        cols, cons = sb("cols", NCOL), sb("cons", NCON)
        MOD, AB, ST = sb("MOD", 240), sb("AB", 176), sb("ST", 320)
        TMP = sb("TMP", 2816)
        bk = [st.enter_context(nc.psum_tensor(f"bk{i}", [P, 512], F32)) for i in range(8)]
        misc = {}

        def load(name, out, in_, *w, eng="pool"):
            if name not in misc:
                misc[name] = st.enter_context(nc.semaphore("d_" + name))
            return Q.dma(eng, out, in_, name, misc[name], w)

        def v2(ap, a):
            return ap.rearrange("p (a b) -> p a b", a=a)

        H1 = (v2(HH[:, :], 8), v2(HL[:, :], 8))
        col = {n: cols[:, o:o + w] for n, (o, w) in COLS.items()}
        con = {n: cons[:, o:o + w] for n, (o, w) in CONS.items()}
        ident, iota = con["ident"], con["iota"]

        raw_sem = [st.enter_context(nc.semaphore(f"raw{i}")) for i in range(NRAW)]
        stream = {"use": 0, "dma": 0, "split": 0}
        ring = Thread("ring")
        raw_t, raw_free, split_t, split_free = {}, {}, {}, {}

        def source(key):
            a = dram[key[0]]
            for k in key[1:-1]:
                a = a[k]
            lo, hi = key[-1]
            return a[:, lo:hi]

        def ring_dma(n):
            s = n % NRAW
            src = source(order[n])
            w = src.shape[1]
            raw_t[n] = Q.dma("sp", RAW[:, s * 1024:s * 1024 + w], src, f"raw{s}", raw_sem[s],
                             [raw_free.get(n - NRAW)])
            stream["dma"] += 1

        def ring_split(n):
            s, z = n % NRAW, n % NSPL
            w = source(order[n]).shape[1]
            raw = RAW[:, s * 1024:s * 1024 + w]
            hi, lo = SPL[:, z * 2048:z * 2048 + w], SPL[:, z * 2048 + 1024:z * 2048 + 1024 + w]
            a = act(hi, raw, ACT.Copy, raw_t[n], split_free.get(n - NSPL), link=False)
            pool = n % 3 == 1 or order[n][0] == "ada2" and n % 2 == 0
            b = tt(lo, raw, hi.bitcast(F32), ALU.subtract, a, eng=("pool" if pool else "dve"), link=False)
            raw_free[n] = [a, b]
            split_t[n] = [a, b]
            stream["split"] += 1

        class Chunk:
            def __init__(self, key):
                self.n = stream["use"]
                stream["use"] += 1
                used.append(key)
                w = key[-1][1] - key[-1][0]
                z = self.n % NSPL
                self.hi, self.lo = SPL[:, z * 2048:z * 2048 + w], SPL[:, z * 2048 + 1024:z * 2048 + 1024 + w]
                self.t = None
                if order is None:
                    return
                assert order[self.n] == key
                mine, Q.thread = Q.thread, ring
                while stream["split"] < min(self.n + NSPL, len(order)):
                    while stream["dma"] < min(stream["split"] + NRAW, len(order)):
                        ring_dma(stream["dma"])
                    ring_split(stream["split"])
                while stream["dma"] < min(stream["split"] + NRAW, len(order)):
                    ring_dma(stream["dma"])
                Q.thread = mine
                self.t = split_t[self.n]

            def done(self, token):
                split_free[self.n] = token

        def pairs(a, b):
            return ((a[0], b[0]), (a[0], b[1]), (a[1], b[0]))

        bank_free = [None] * 8
        rots = {}

        class Bank:
            def __init__(self, index=None):
                if index is None:
                    r = rots[Q.thread.name]
                    index = r[0][r[1] % len(r[0])]
                    r[1] += 1
                self.i, self.ap, self.free = index, bk[index][:, :], bank_free[index]

            def done(self, *tokens):
                bank_free[self.i] = list(tokens)

        def use_banks(s):
            rots[Q.thread.name] = [s, 0]

        heaps = {}

        def alloc(words):
            h = heaps[Q.thread.name]
            a = h["n"]
            h["n"] += words
            assert h["n"] <= h["end"], (Q.thread.name, h["n"] - h["start"], h["end"] - h["start"])
            return h["in"][:, a:a + words]

        def heap(tensor, start, end):
            heaps[Q.thread.name] = {"in": tensor, "start": start, "n": start, "end": end}

        def phase(keep=None):
            h = heaps[Q.thread.name]
            h["n"] = h["start"] if keep is None else keep
            Q.barrier()

        def mark():
            return heaps[Q.thread.name]["n"]

        stat = {"n": {}}

        def stats(n):
            b = 160 if Q.thread.name in ("B", "C") else 0
            a = stat["n"].get(b, 0)
            if a + n > 160:
                a = 0
            stat["n"][b] = a + n
            return ST[:, b + a:b + a + n]

        def rstd(ss, n, width, *w):
            a, y, r, out = stats(n), stats(n), stats(n), stats(n)
            t = ts(a, ss, 1.0 / width, EPS, ALU.mult, ALU.add, *w)
            t = act(y, a, ACT.Sqrt, t)
            recip(r, y, t)
            tt(y, r, r, ALU.mult)
            stt(y, y, -0.5, a, ALU.mult, ALU.mult)
            t = stt(out, y, 1.5, r, ALU.add, ALU.mult)
            return out, t

        def sumsq(src3, ss, junk, *w):
            for i in range(2):
                t = act(junk, src3[:, i, :], ACT.Square, *w, accum=ss[:, i:i + 1])
            return t

        def norm(x3, xn, junk, *w):
            ss = stats(2)
            t = sumsq(x3, ss, junk[:, 0:1024], *w)
            r, t = rstd(ss, 2, D, t)
            return [ts(v2(xn, 2)[:, i, :], x3[:, i, :], r[:, i:i + 1], None, ALU.mult, None) for i in range(2)]

        def norm_T(x3, A, B, xn, ht, H, *w, tx=None):
            if tx is None:
                tx = norm(x3, xn, ht, *w)
                yield 9.0
            out = []
            ht3 = v2(ht, 8)
            for i in range(2):
                c = slice(i * P, (i + 1) * P)
                src = v2(xn, 2)[:, i, :]
                us = []
                for k0 in (0, 4):
                    b = Bank()
                    for k in range(4):
                        t = tr(b.ap[:, k * P:(k + 1) * P], src[:, (k0 + k) * P:(k0 + k + 1) * P], ident, b.free,
                               tx[i], *w, mark=(k == 3))
                    for k in range(4):
                        q = slice(k0 + k, k0 + k + 1)
                        if k0:
                            u = ts(ht3[:, k0 + k, c], b.ap[:, k * P:(k + 1) * P], A[:, q], B[:, q], ALU.mult,
                                   ALU.add, t, link=False)
                        else:
                            u = act(ht3[:, k, c], b.ap[:, k * P:(k + 1) * P], ACT.Identity, t, scale=A[:, q],
                                    bias=B[:, q], link=False)
                    b.done(u)
                    us.append(u)
                u = act(H[0][:, :, c], ht3[:, :, c], ACT.Copy, us)
                out += [u, tt(H[1][:, :, c], ht3[:, :, c], H[0][:, :, c].bitcast(F32), ALU.subtract, u, us)]
            yield 4.0
            return out

        def turn_split(src, H, i, *w):
            out = []
            for k0 in (0, 4):
                b = Bank()
                for k in range(4):
                    t = tr(b.ap[:, k * P:(k + 1) * P], src[:, (k0 + k) * P:(k0 + k + 1) * P], ident, b.free, *w,
                           mark=(k == 3))
                c = slice(i * P, (i + 1) * P)
                hi, lo = H[0][:, k0:k0 + 4, c], H[1][:, k0:k0 + 4, c]
                u = cp(hi, v2(b.ap, 4), t, eng="act", link=False)
                v = tt(lo, v2(b.ap, 4), hi.bitcast(F32), ALU.subtract, u, link=False)
                b.done(v)
                out += [u, v]
            return out

        def tok(keys, H, b, n, *w):
            first = True
            for c, key in enumerate(keys):
                ch = Chunk(key)
                wp = (v2(ch.hi, 4), v2(ch.lo, 4))
                for i in range(2):
                    for k in range(4):
                        hs = [h[:, 4 * c + k, i * P:(i + 1) * P] for h in H]
                        for m, (x, y) in enumerate(pairs(hs, [q[:, k, :] for q in wp])):
                            last = i == 1 and k == 3 and m == 2
                            t = mm(b.ap[:, i * n:(i + 1) * n], x, y, first, c == 1 and k == 3 and m == 2, b.free,
                                   ch.t, *w, mark=last, passes=1)
                            first = False
                ch.done(t)
            return t

        def feat(key, H, out, b, *w):
            ch = Chunk(key)
            wp = (v2(ch.hi, 8), v2(ch.lo, 8))
            for k in range(8):
                for m, (x, y) in enumerate(pairs([q[:, k, :] for q in wp], [h[:, k, :] for h in H])):
                    t = mm(out, x, y, k == 0 and m == 0, k == 7 and m == 2, b.free, ch.t, *w,
                           mark=(k == 7 and m == 2), passes=1)
            ch.done(t)
            return t

        def spread(gcol, dst, *w):
            out = []
            for h in range(2):
                b = Bank()
                for k in range(4):
                    t = mm(b.ap[:, k * P:(k + 1) * P], gcol[:, 4 * h + k:4 * h + k + 1].to_broadcast([P, P]), ident,
                           True, True, b.free, *w, mark=(k == 3))
                u = cp(dst[:, h * 512:(h + 1) * 512], b.ap, t, eng="act", link=False)
                b.done(u)
                out.append(u)
            return out

        flags = {}

        scope = ExitStack()
        R = sb("R1", 32768, where=scope)
        X = R[:, 0:2048]
        X3 = v2(X, 2)
        heap(R, 2048, 4096)
        t_cols = load("cols", cols[:, :], dram["cols"][:, :], eng="act")
        t_cons = load("cons", cons[:, :], dram["cons"][:, :], eng="act")
        t_x = load("x", X3, dram["x"].rearrange("b (i p) d -> p (b i) d", p=P))
        sil = alloc(24)
        t = act(sil, cols[:, 0:24], ACT.Silu, t_cols)
        c1 = CS[:, 0:16].rearrange("p (k m) -> p k m", m=2)
        c2 = CS[:, 16:48].rearrange("p (k s m) -> p s k m", s=2, m=2)
        s3 = v2(sil[:, 8:24], 2)
        cp(c1[:, :, 0], sil[:, 0:8], t)
        tt(c1[:, :, 1], sil[:, 0:8], c1[:, :, 0].bitcast(F32), ALU.subtract)
        cp(c2[:, :, :, 0], s3)
        t_cs = tt(c2[:, :, :, 1], s3, c2[:, :, :, 0].bitcast(F32), ALU.subtract)
        rowb = {"n": 0, "free": [None, None]}

        def ada(name, cs, ns, groups, bias, dst, rows=TMP, pace=0.0):
            m = 2 * ns
            for g in groups:
                b = Bank()
                for c in range(4):
                    ch = Chunk(name + (g, (c * 1024, (c + 1) * 1024)))
                    for k in range(2):
                        x = cs[:, (2 * c + k) * m:(2 * c + k + 1) * m]
                        for n, y in enumerate((ch.hi, ch.lo)):
                            last = k == 1 and n == 1
                            t = mm(b.ap[0:m, :], x, y[:, k * 512:(k + 1) * 512], c == 0 and k == 0 and n == 0,
                                   c == 3 and last, b.free, ch.t, t_cs, mark=last, passes=1)
                    ch.done(t)
                    yield pace
                z = rowb["n"] % 2
                rowb["n"] += 1
                row = rows[:, z * 512:(z + 1) * 512]
                u = cp(row[0:m, :], b.ap[0:m, :], t, rowb["free"][z], eng="act", link=False)
                b.done(u)
                yield 1.0
                b = Bank()
                for n in range(4):
                    t = mm(b.ap[:, n * ns:(n + 1) * ns], row[0:m, n * P:(n + 1) * P], con["sel"][0:m, 0:ns], True,
                           True, b.free, u, t_cons, mark=(n == 3))
                rowb["free"][z] = t
                d = v2(dst, ns)[:, :, 4 * g:4 * g + 4]
                t = tt(d, b.ap[:, 0:4 * ns].rearrange("p (n s) -> p s n", s=ns),
                       bias[:, 4 * g:4 * g + 4].unsqueeze(1).to_broadcast([P, ns, 4]), ALU.add, t, link=False)
                b.done(t)
                flags[name + ("t",)] = t

        def affine_cols(n, w, scale, *wt):
            o = AB[:, n * 16:n * 16 + 8]
            return o, stt(o, scale, 1.0, w, ALU.add, ALU.mult, *wt)

        lat, cxt = [], []

        def modulate2(l, rows, pace):
            mod = MOD[:, 48 + 96 * l:144 + 96 * l]
            yield from ada(("ada2", l), CS[:, 16:48], 2, range(12), col["b_ada2" + "ab"[l]], mod, rows, pace)
            for s, lst in ((0, lat), (1, cxt)):
                m = mod[:, 48 * s:48 * s + 48]
                n = 2 + 4 * l + 2 * s
                a, _ = affine_cols(n, col[f"apre{l}"], m[:, 8:16], flags[("ada2", l, "t")])
                f, _ = affine_cols(n + 1, col[f"fpre{l}"], m[:, 32:40])
                ga, gf = AB[:, n * 16 + 8:n * 16 + 16], AB[:, n * 16 + 24:n * 16 + 32]
                tt(ga, m[:, 16:24], col[f"apost{l}"], ALU.mult)
                tt(gf, m[:, 40:48], col[f"fpost{l}"], ALU.mult)
                lst.append(dict(A=a, B=m[:, 0:8], FA=f, FB=m[:, 24:32], ga=ga, gf=gf))

        def modulations():
            use_banks([6, 7])
            yield from ada(("ada",), CS[:, 0:16], 1, range(4, 12), col["b_ada"], MOD[:, 0:48])
            flags["A2"] = affine_cols(1, col["norm2"], MOD[:, 32:40], flags[("ada", "t")])
            yield from modulate2(0, TMP, 0.0)

        gateT, i1T, i2T = TMP[:, 2048:2304], TMP[:, 2304:2560], TMP[:, 2560:2816]
        t_idx = []

        def mixer():
            nonlocal t_x
            use_banks([0, 1, 2, 3, 4, 5])
            heap(R, 2112, 32768)
            big, ht = alloc(2048), alloc(2048)
            tx = norm(X3, big, ht, t_x)
            yield from ada(("ada",), CS[:, 0:16], 1, range(0, 4), col["b_ada"], MOD[:, 0:48])
            A1, t_A1 = affine_cols(0, col["norm1"], MOD[:, 8:16], flags[("ada", "t")])
            t_h = yield from norm_T(X3, A1, MOD[:, 0:8], big, ht, H1, t_cons, t_A1, tx=tx)
            HT3 = v2(ht, 8)
            qT, kT, vt = alloc(1024), alloc(1024), alloc(2048)
            sgw, walr, wau = alloc(1024), alloc(128), alloc(512)
            t_walr = load("walr", walr, dram["walr"][:, :])
            t_wau = load("wau", wau[0:16, :], dram["wau"][:, :])
            gws, lnw, lnb = alloc(1024), alloc(1024), alloc(1024)
            t_rows = [load("row", d, dram["rows"][o:o + 1024].partition_broadcast(P))
                      for d, o in ((gws, 0), (lnw, 1024), (lnb, 2048))]
            alrT = alloc(256)
            t_sgw = load("sgw", sgw, dram["sgw"][:, :])
            t_sgw = aff(v2(sgw, 8), [[0, 8], [1, 128]], 0, -1, t_sgw)
            msk = alloc(256)
            t_msk = Q.put("pool", lambda e: e.memset(msk, 1.0), [])
            t_msk = Q.put("pool", lambda e: e.memset(msk.rearrange("p (a b) -> p a b", b=64)[:, :, 0:1], 0.0),
                          [t_msk])
            b = Bank()
            for k in range(8):
                t = mm(b.ap[0:16, 0:256], v2(walr, 8)[:, k, :], HT3[:, k, :], k == 0, k == 7, b.free, t_walr, t_h,
                       mark=(k == 7))
            t_alr = cp(alrT[0:16, :], b.ap[0:16, 0:256], t)
            b.done(t_alr)
            for j in range(4):
                b = Bank()
                for n in range(2):
                    t = feat(("wqk", 2 * j + n, (0, 1024)), H1, b.ap[:, n * 256:(n + 1) * 256], b, t_h)
                dst = (qT if j < 2 else kT)[:, (j % 2) * 512:(j % 2) * 512 + 512]
                t_qk = cp(dst, b.ap, t, eng="act", link=False)
                b.done(t_qk)
                yield 0.0
            z, la, Gc, eA = alloc(1024), alloc(1024), alloc(1024), alloc(1024)
            for j in range(2):
                b = Bank()
                for i in range(2):
                    h = 2 * j + i
                    t = mm(b.ap[:, i * 256:i * 256 + 256], wau[0:16, h * P:(h + 1) * P], alrT[0:16, :], True, True,
                           b.free, t_wau, t_alr, mark=(i == 1))
                for i in range(2):
                    h = 2 * j + i
                    t_z = ts(z[:, h * 256:(h + 1) * 256], b.ap[:, i * 256:i * 256 + 256],
                             col["b_alpha"][:, h:h + 1], None, ALU.add, None, t, link=False)
                b.done(t_z)
            t = stt(eA, z, -1.0, z, ALU.mult, ALU.min, t_z)
            t = act(eA, eA, ACT.Exp, t)
            t = ts(eA, eA, 1.0, None, ALU.add, None, t)
            t = act(eA, eA, ACT.Ln, t)
            stt(la, z, 0.0, eA, ALU.min, ALU.subtract, t)

            def scan(out, d0, d1, *w):
                return Q.put("dve", lambda e: e.tensor_tensor_scan(out, d0, d1, 0.0, ALU.mult, ALU.add),
                             [own("dve", True), list(w)])

            for h in range(4):
                s = slice(h * 256, (h + 1) * 256)
                t_G = scan(Gc[:, s], msk, la[:, s], t_msk)
            yield 0.0

            def project(c0, evac):
                for j in range(4):
                    b = Bank()
                    t = tok([("win", c0 + j, (c * 1024, (c + 1) * 1024)) for c in range(2)], H1, b, 256)
                    evac(j, b, t)
                    yield 0.0

            def evac_to(dst, func):
                def evac(j, b, t):
                    t = act(v2(dst, 2)[:, :, j * 256:(j + 1) * 256], v2(b.ap, 2), func, t, link=False)
                    b.done(t)
                    flags["ev"] = t
                return evac

            vt3 = v2(vt, 2)
            G16 = Gc.rearrange("p (c t) -> p c t", t=64)
            egl = alloc(16)
            t_egl = act(egl, G16[:, :, 63], ACT.Exp, t_G, scale=1.0 / 16)
            t_kt = tt(la.rearrange("p (c t) -> p c t", t=64), G16[:, :, 63:64].to_broadcast([P, 16, 64]), G16,
                      ALU.subtract)
            t_e1 = act(z, Gc, ACT.Exp, scale=1.0 / 16)
            t_e2 = act(eA, Gc, ACT.Exp, scale=-1.0 / 16)
            t_e3 = act(la, la, ACT.Exp, t_kt, scale=1.0 / 16)
            qd, ki, kt = z, eA, la
            t_ktail = tt(kt, kT, la, ALU.mult, t_e3, t_qk)
            tt(ki, kT, ki, ALU.mult, t_e2)
            t_qd = stt(qd, qT, 128 ** -0.5, qd, ALU.mult, ALU.mult, t_e1, t_qk)
            yield from project(0, evac_to(vt, ACT.Copy))
            t_v = flags["ev"]
            ktT = alloc(1024)
            ktT4 = ktT.rearrange("p (i h k) -> p i h k", i=2, h=4)
            t_ktT = []
            for i in range(2):
                b = Bank()
                for h in range(4):
                    t = tr(b.ap[:, h * P:(h + 1) * P], kt[:, h * 256 + i * P:h * 256 + (i + 1) * P], ident, b.free,
                           t_ktail, mark=(h == 3))
                t = cp(ktT[:, i * 512:(i + 1) * 512], b.ap, t, eng="act", link=False)
                b.done(t)
                t_ktT.append(t)
            AT = alloc(1024)
            t_AT = []
            for i in range(2):
                b = Bank()
                for h in range(4):
                    s = slice(h * 256 + i * P, h * 256 + (i + 1) * P)
                    t = mm(b.ap[:, h * P:(h + 1) * P], ki[:, s], qd[:, s], True, True, b.free, t_qd, mark=(h == 3))
                a = AT[:, i * 512:(i + 1) * 512]
                t = cp(a, b.ap, t, eng="act", link=False)
                b.done(t)
                aff(v2(a, 4), [[0, 4], [1, 128]], 0, -1, t)
                t_AT.append(aff(v2(a, 4)[:, :, 64:128], [[0, 4], [0, 64]], -64, 1))
            S = [alloc(1024) for _ in range(3)]
            t_S = [None] * 4
            for c in range(3):
                rows = slice(64 * (c % 2), 64 * (c % 2) + 64)
                for j in range(2):
                    b = Bank()
                    for i in range(2):
                        h = 2 * j + i
                        t = mm(b.ap[:, i * 256:(i + 1) * 256], ktT4[rows, c // 2, h, :],
                               vt3[rows, c // 2, h * 256:(h + 1) * 256], True, True, b.free, t_ktT[c // 2], t_v,
                               mark=(i == 1))
                    for i in range(2):
                        h = 2 * j + i
                        d = S[c][:, h * 256:(h + 1) * 256]
                        if c == 0:
                            u = cp(d, b.ap[:, i * 256:(i + 1) * 256], t, link=False)
                        else:
                            u = stt(d, S[c - 1][:, h * 256:(h + 1) * 256], egl[:, 4 * h + c:4 * h + c + 1],
                                    b.ap[:, i * 256:(i + 1) * 256], ALU.mult, ALU.add, t, t_egl, t_S[c], link=False)
                    b.done(u)
                t_S[c + 1] = u
            sv, su = alloc(2048), alloc(2048)
            yield from project(12, evac_to(sv, ACT.Gelu))
            t_sv = flags["ev"]
            o, xn = alloc(2048), big
            so = stats(8)
            for i in range(2):
                for j in range(2):
                    b = Bank()
                    for m in range(2):
                        h = 2 * j + m
                        oc = slice(m * 256, (m + 1) * 256)
                        t = mm(b.ap[:, oc], AT[:, i * 512 + h * P:i * 512 + (h + 1) * P],
                               vt3[:, i, h * 256:(h + 1) * 256], True, False, b.free, t_AT[i], t_v)
                        for c in (2 * i, 2 * i + 1):
                            if c == 0:
                                continue
                            r = slice(64 * (c % 2), 64 * (c % 2) + 64)
                            t = mm(b.ap[r, oc], qd[:, h * 256 + c * 64:h * 256 + c * 64 + 64],
                                   S[c - 1][:, h * 256:(h + 1) * 256], False, c % 2 == 1, t_S[c],
                                   mark=(c % 2 == 1 and m == 1))
                    dst = o[:, i * 1024 + j * 512:i * 1024 + (j + 1) * 512]
                    t = cp(dst, b.ap, t, link=False)
                    b.done(t)
                    for m in range(2):
                        n = i * 4 + 2 * j + m
                        t_o = act(xn[:, m * 256:(m + 1) * 256], dst[:, m * 256:(m + 1) * 256], ACT.Square, t,
                                  accum=so[:, n:n + 1])
            ro, t_ro = rstd(so, 8, 256, t_o)
            for n in range(8):
                s = slice(n * 256, (n + 1) * 256)
                hs = slice((n % 4) * 256, (n % 4) * 256 + 256)
                t_on = stt(o[:, s], o[:, s], ro[:, n:n + 1], gws[:, hs], ALU.mult, ALU.mult, t_rows, t_ro,
                           link=False)
            sv3, xn3 = v2(sv, 2), v2(xn, 2)
            mu, sq = stats(2), stats(2)
            rsum(mu, sv3, ALU.add, t_sv)
            ts(mu, mu, -1.0 / D, None, ALU.mult, None)
            for i in range(2):
                t = ts(sv3[:, i, :], sv3[:, i, :], mu[:, i:i + 1], None, ALU.add, None)
            t = sumsq(sv3, sq, xn3[:, 0, :], t)
            rl, _ = rstd(sq, 2, D, t)
            for i in range(2):
                stt(sv3[:, i, :], sv3[:, i, :], rl[:, i:i + 1], lnw, ALU.mult, ALU.mult, t_rows)
                t_ln = tt(sv3[:, i, :], sv3[:, i, :], lnb, ALU.add)
            yield 0.0
            yield from project(8, evac_to(su, ACT.Gelu))
            t_su = flags["ev"]
            for i in range(2):
                for j in range(2):
                    b = Bank()
                    for m in range(4):
                        g = 4 * j + m
                        t = mm(b.ap[:, m * P:(m + 1) * P], sgw[:, g * P:(g + 1) * P], sv3[:, i, g * P:(g + 1) * P],
                               True, True, b.free, t_sgw, t_ln, mark=(m == 3))
                    for m in range(4):
                        g = 4 * j + m
                        d = v2(su, 2)[:, i, g * P:(g + 1) * P]
                        t_s = stt(d, b.ap[:, m * P:(m + 1) * P], col["sgu_b"][:, g:g + 1], d, ALU.add, ALU.mult, t,
                                  t_su, link=False)
                    b.done(t_s)

            def evac_gate(dst, func, *w):
                def evac(j, b, t):
                    tmp = xn[:, (j % 2) * 512:(j % 2) * 512 + 512]
                    t = act(v2(tmp, 2), v2(b.ap, 2), func, t, Q.latest("dve"), link=False)
                    b.done(t)
                    d = v2(dst, 2)[:, :, j * 256:(j + 1) * 256]
                    flags["m"] = tt(d, d, v2(tmp, 2), ALU.mult, t, *w, link=False)
                return evac

            yield from project(4, evac_gate(o, ACT.Silu, t_on))
            yield from project(16, evac_gate(o, ACT.Sigmoid, t_on, flags["m"]))
            yield from project(20, evac_gate(su, ACT.Sigmoid, t_s))
            t_m = []
            for i in range(2):
                oi = v2(o, 2)[:, i, :]
                t_m.append(tt(oi, oi, v2(su, 2)[:, i, :], ALU.add, flags["m"]))
            yield ("flag", "A2")
            gB = lnw
            t_gB = spread(MOD[:, 16:24], gB, flags["A2"][1], t_ln)
            t_mT = []
            for i in range(2):
                t_mT += turn_split(v2(o, 2)[:, i, :], H1, i, t_m[i])
            yield 2.0
            for j in range(4):
                b = Bank()
                t = tok([("wout", j, (c * 1024, (c + 1) * 1024)) for c in range(2)], H1, b, 256, t_mT)
                y = v2(xn, 4)[:, j, :]
                g = gB[:, j * 256:(j + 1) * 256].unsqueeze(1).to_broadcast([P, 2, 256])
                t = tt(v2(y, 2), v2(b.ap, 2), g, ALU.mult, t, t_gB)
                b.done(t)
                t_x = tt(X3[:, :, j * 256:(j + 1) * 256], X3[:, :, j * 256:(j + 1) * 256], v2(y, 2), ALU.add)
                yield 0.0
            phase()
            flags["xs"] = load("xs", xs_d[:, :], X, t_x)
            keys = alloc(256)
            t_keys = load("keys", keys, dram["keys"][:, :])
            t_h = yield from norm_T(X3, flags["A2"][0], MOD[:, 24:32], alloc(2048), alloc(2048), H1, t_x)
            SC = alloc(4096)
            SC2 = alloc(1024)
            qh = [alloc(512), alloc(512)]
            qfree = [None, None]
            V16, I16 = alloc(512), alloc(512).bitcast(U32)
            V5 = V16.rearrange("p (i s h k) -> p i s h k", i=2, s=2, h=8)
            I5 = I16.rearrange("p (i s h k) -> p i s h k", i=2, s=2, h=8)

            def top16(lists, *w):
                def vmax(out, in_, *w):
                    return Q.put("dve", lambda e: e.max(out, in_), w)

                def vidx(out, m, in_, *w):
                    return Q.put("dve", lambda e: e.max_index(out, m, in_), w)

                def drop(work, m, vals, *w):
                    return Q.put("dve", lambda e: e.match_replace(work, m, vals, NEG), w)

                t = [vmax(vo[:, 0:8], vals, *w) for vals, vo, io, work in lists]
                u = [drop(work, vo[:, 0:8], vals, t[n], own("dve", True) if n == 0 else None)
                     for n, (vals, vo, io, work) in enumerate(lists)]
                for n, (vals, vo, io, work) in enumerate(lists):
                    vidx(io[:, 0:8], vo[:, 0:8], vals, t[n])
                t = [vmax(vo[:, 8:16], work, u[n]) for n, (vals, vo, io, work) in enumerate(lists)]
                return [vidx(io[:, 8:16], vo[:, 8:16], work, t[n]) for n, (vals, vo, io, work) in enumerate(lists)]

            for h in range(8):
                b = Bank()
                for n in range(2):
                    t = feat(("wq", 2 * h + n, (0, 1024)), H1, b.ap[:, n * 256:(n + 1) * 256], b, t_h)
                q = qh[h % 2]
                t_q = cp(q, b.ap, t, qfree[h % 2], eng="act", link=False)
                b.done(t_q)
                yield 0.0
                b = Bank()
                for i in range(2):
                    for s in range(2):
                        t = mm(b.ap[:, (i * 2 + s) * P:(i * 2 + s + 1) * P],
                               q[:, s * 256 + i * P:s * 256 + (i + 1) * P], keys[:, s * P:(s + 1) * P], True, True,
                               b.free, t_q, t_keys, mark=(i == 1 and s == 1))
                qfree[h % 2] = t
                sc = SC[:, h * 512:(h + 1) * 512]
                t = cp(sc, b.ap, t, eng="act", link=False)
                b.done(t)
                top16([(sc[:, n * P:(n + 1) * P], V5[:, n // 2, n % 2, h, :], I5[:, n // 2, n % 2, h, :],
                        SC2[:, n * P:(n + 1) * P]) for n in range(4)], t)
                yield 0.0
            IF = alloc(512)
            t_if = cp(IF, I16)
            I5f = IF.rearrange("p (i s h k) -> p i s h k", i=2, s=2, h=8)
            yield 12.0
            for i in range(2):
                cand = alloc(2048)
                c4 = cand.rearrange("p (h a b) -> p h a b", h=8, a=16)
                tt(c4, V5[:, i, 0, :, :].unsqueeze(3).to_broadcast([P, 8, 16, 16]),
                   V5[:, i, 1, :, :].unsqueeze(2).to_broadcast([P, 8, 16, 16]), ALU.add)
                tv, tp = alloc(128), alloc(128).bitcast(U32)
                for h4 in (0, 4):
                    top16([(cand[:, h * 256:(h + 1) * 256], tv[:, h * 16:(h + 1) * 16], tp[:, h * 16:(h + 1) * 16],
                            SC2[:, (h - h4) * 256:(h - h4 + 1) * 256]) for h in range(h4, h4 + 4)],
                          own("dve", True))
                    yield 8.0
                sel = []
                for s in range(2):
                    pu, pf, res, ohb = alloc(128).bitcast(U32), alloc(128), alloc(128), alloc(2048)
                    eng = ("dve", "pool")[s]
                    if s == 0:
                        ts(pu, tp, 4, None, ALU.logical_shift_right, None)
                    else:
                        ts(pu, tp, 15, None, ALU.bitwise_and, None)
                    t = cp(pf, pu)
                    oh = ohb.rearrange("p (n a) -> p n a", a=16)
                    t = tt(oh, pf.unsqueeze(2).to_broadcast([P, 128, 16]),
                       iota[:, 0:16].unsqueeze(1).to_broadcast([P, 128, 16]), ALU.is_equal, t)
                    oh4 = ohb.rearrange("p (h k a) -> p h k a", h=8, k=16)
                    t = tt(oh4, oh4, I5f[:, i, s, :, :].unsqueeze(2).to_broadcast([P, 8, 16, 16]), ALU.mult, t_if,
                           t, eng=eng)
                    sel.append((res, oh, t))
                gt = alloc(128)
                tv3, gt3 = v2(tv, 8), v2(gt, 8)
                sm = stats(8)
                t = tt(gt3, tv3, tv3[:, :, 0:1].to_broadcast([P, 8, 16]), ALU.subtract)
                t = act(gt, gt, ACT.Exp, t)
                rsum(sm, gt3, ALU.add, t)
                recip(sm, sm)
                t = tt(gt3, gt3, sm.unsqueeze(2).to_broadcast([P, 8, 16]), ALU.mult)
                for res, oh, t in sel:
                    t = rsum(res, oh, ALU.add, t)
                yield 10.0
                b = Bank()
                for n, src in enumerate((gt, sel[0][0], sel[1][0])):
                    t2 = tr(b.ap[:, n * P:(n + 1) * P], src, ident, b.free, t, mark=(n == 2))
                u = cp(TMP[:, 2048:2816].rearrange("p (n t) -> p n t", n=3)[:, :, i * P:(i + 1) * P],
                       v2(b.ap[:, 0:384], 3), t2, eng="act", link=False)
                b.done(u)
                t_idx.append(u)

        threads = [Thread("A", mixer()), Thread("B", modulations())]
        interleave(Q, threads, flags, {})
        ends = [list(t.last.values()) for t in threads] + [flags["xs"]]
        scope.close()

        main = Thread("M")
        Q.thread = main
        for e in ENGINES + ("dma",):
            main.pend[e] = [ends]
        use_banks([4, 5, 6, 7])
        scope = ExitStack()
        G3 = sb("G", 32768, where=scope)[:, :].rearrange("p (e t) -> p e t", t=256)
        oh_free = [None] * 2
        for t4 in range(64):
            b = Bank()
            z = t4 % 2
            o1 = TMP[:, z * 1024:z * 1024 + 512].rearrange("p (m e) -> p m e", m=4)
            o2 = TMP[:, z * 1024 + 512:z * 1024 + 1024].rearrange("p (m e) -> p m e", m=4)
            four = slice(4 * t4, 4 * t4 + 4)
            io = iota.unsqueeze(1).to_broadcast([P, 4, P])
            u = tt(o1, io, i1T[:, four].unsqueeze(2).to_broadcast([P, 4, P]), ALU.is_equal, oh_free[z], t_idx,
                   link=False)
            u = tt(o1, o1, gateT[:, four].unsqueeze(2).to_broadcast([P, 4, P]), ALU.mult, u, eng="pool", link=False)
            v = tt(o2, io, i2T[:, four].unsqueeze(2).to_broadcast([P, 4, P]), ALU.is_equal, oh_free[z], link=False)
            for m in range(4):
                t = mm(b.ap[:, m * P:(m + 1) * P], o1[:, m, :], o2[:, m, :], True, True, b.free, u, v,
                       mark=(m == 3))
            oh_free[z] = t
            t_G = cp(G3[:, :, 4 * t4:4 * t4 + 4], b.ap.rearrange("p (m e) -> p e m", m=4), t, eng="act", link=False)
            b.done(t_G)

        wfree = [None] * 3
        afree = [None] * 3

        def split_hidden(j, a, *w):
            z = j % 3
            hi, lo = WHL[:, z * 512:z * 512 + 256], WHL[:, z * 512 + 256:z * 512 + 512]
            u = act(hi, a, ACT.Copy, wfree[z], *w, link=False)
            v = tt(lo, a, hi.bitcast(F32), ALU.subtract, u, *w, link=False)
            afree[z] = [u, v]
            return (hi, lo), [u, v]

        def second_product(j, key, acc, x, t, n):
            ch = Chunk(key)
            for i in range(2):
                for h in range(2):
                    c = acc[2 * i + h]
                    xs = [q[:, i * P:(i + 1) * P] for q in x]
                    ys = [q[:, h * 512:(h + 1) * 512] for q in (ch.hi, ch.lo)]
                    for m, (p, q) in enumerate(pairs(xs, ys)):
                        u = mm(c.ap, p, q, j == 0 and m == 0, j == n - 1 and m == 2, c.free, ch.t, t,
                               mark=(i == 1 and h == 1 and m == 2), passes=1)
            ch.done(u)
            wfree[j % 3] = u
            return u

        acc = [Bank(i) for i in range(4)]
        LAG = 2

        def peer():
            use_banks([4, 5])
            held = {}
            for j in range(P + LAG):
                if j < P:
                    b = Bank()
                    t = feat(("peer", j, (0, 1024)), H1, b.ap[:, 0:256], b)
                    a = TMP[:, (j % 3) * 256:(j % 3) * 256 + 256]
                    u = act(a, b.ap[:, 0:256], ACT.Gelu, t, afree[j % 3], oh_free, link=False)
                    b.done(u)
                    v = tt(a, a, G3[:, j, :], ALU.mult, u, t_G, link=False)
                    held[j] = split_hidden(j, a, v)
                if j >= LAG:
                    x, t = held.pop(j - LAG)
                    flags["y"] = second_product(j - LAG, ("peer", j - LAG, (1024, 2048)), acc, x, t, P)
                yield 0.0

        def modulations_late():
            use_banks([6, 7])
            yield 10.0
            yield from modulate2(1, TMP[:, 1024:2048], 10.0)

        threads = [Thread("F", modulations_late()), Thread("P", peer())]
        for t in threads:
            for e in ENGINES:
                t.pend[e] = [list(main.last.values())]
        interleave(Q, threads, flags, {})
        t_peer = flags["y"]
        ends = [list(t.last.values()) for t in threads]
        for e in ENGINES + ("dma",):
            main.pend[e] = [ends]
        main.last = {e: t for th in threads for e, t in th.last.items()}
        scope.close()

        S3 = sb("R3", 28800)
        HC = (v2(sb("HCH", 2048, F32R)[:, :], 8), v2(sb("HCL", 2048, F32R)[:, :], 8))
        X3, XC3 = v2(S3[:, 0:2048], 2), v2(S3[:, 2048:4096], 2)
        heap(S3, 4096, 4096 + 644)
        srow, lamc = alloc(640), alloc(4)
        t_x = load("x3", S3[:, 0:2048], xs_d[:, :])
        t_xc = load("xc", XC3, dram["ctx"].rearrange("b (i p) d -> p (b i) d", p=P))
        t_srow = load("srow", srow, dram["rows"][4096:4736].partition_broadcast(P))
        KV = 3328
        base = 4096 + 644
        kvc = S3[:, base:base + KV]
        L0, L1 = base + KV, base + KV + 11584
        C1 = 28800
        heap(S3, L0, L1)
        gB, fn, yb = alloc(1024), alloc(1024), alloc(1024)
        t_fn = load("fn", fn, dram["rows"][3072:4096].partition_broadcast(P))
        begun = list(main.last.values())

        def kv_views(m):
            return (v2(m[:, 0:1024], 4), v2(m[:, 1024:1536], 2), v2(m[:, 1536:2048], 2), v2(m[:, 2048:3328], 2))

        def q_views(m):
            return (v2(m[:, 0:1024], 4), v2(m[:, 1024:1536], 2), v2(m[:, 1536:2560], 4))

        def rope(x4, cs, sn, n, half, DS, *w):
            c = v2(cs, 2).unsqueeze(2).to_broadcast([P, 2, n, half])
            s = v2(sn, 2).unsqueeze(2).to_broadcast([P, 2, n, half])
            a4 = DS[:, 0:2 * n * half].rearrange("p (i n d) -> p i n d", i=2, n=n)
            b4 = DS[:, 640:640 + 2 * n * half].rearrange("p (i n d) -> p i n d", i=2, n=n)
            x1, x2 = x4[:, :, :, 0:half], x4[:, :, :, half:2 * half]
            tt(a4, x1, s, ALU.mult, *w)
            tt(b4, x2, s, ALU.mult)
            tt(x1, x1, c, ALU.mult)
            tt(x1, x1, b4, ALU.subtract)
            tt(x2, x2, c, ALU.mult)
            return tt(x2, x2, a4, ALU.add)

        def turned(srcs, dst, rows, *w):
            us = []
            for i in range(2):
                b = Bank()
                blocks = srcs(i)
                for n, a in enumerate(blocks):
                    t = tr(b.ap[0:rows, n * P:(n + 1) * P], a, ident, b.free, *w, mark=(n == len(blocks) - 1))
                for d, f, c in dst(i):
                    u = cp(d, v2(b.ap[0:rows, f * P:(f + c) * P], c), t, eng="act", link=False)
                b.done(u)
                us.append(u)
            return us

        def qkv(l, s, x3, m, H, kv, q, DS, *w):
            keep = mark()
            HTv = alloc(2048)
            xn = alloc(2048)
            t_h = yield from norm_T(x3, m["A"], m["B"], xn, HTv, H, *w)
            phase(keep)
            KM3, KD3, KG3, VV3 = kv_views(kv)
            PM, PG = alloc(832), alloc(1280)
            PM3, PG3 = v2(PM, 2), v2(PG, 2)
            PD3 = v2(PG[:, 0:1024], 2)
            wqb, wkvb = alloc(768), alloc(512)
            nm = f"{l}{s}"
            t_wkvb = load("wkvb" + nm, wkvb, dram["wkvb"][l])
            if q is not None:
                QM3, QD3, QG3 = q_views(q)
                t_wqb = load("wqb" + nm, wqb, dram["wqb"][l])
            KA, aT = alloc(768), alloc(1024)
            KK = alloc(512)
            KA4 = KA.rearrange("p (i h d) -> p i h d", i=2, h=4)

            def chunk(j, n=256):
                b = Bank()
                nme = "win2k" if j == 7 else "win2"
                key = (nme, l) if j == 7 else (nme, l, j)
                return b, tok([key + ((c * 4 * n, (c + 1) * 4 * n),) for c in range(2)], H, b, n, t_h)

            def low_rank(src3, kc, g, wb, t_wb, n, t, t_a):
                width = kc * P
                ssx = stats(2)
                for i in range(2):
                    t = act(DS[:, 0:width], src3[:, i, :], ACT.Square, t, Q.latest("dve"), accum=ssx[:, i:i + 1])
                r, _ = rstd(ssx, 2, width, t)
                for i in range(2):
                    t = ts(aT[:, 512 + i * width:512 + (i + 1) * width] if kc == 1 else
                           src3[:, i, :], src3[:, i, :], r[:, i:i + 1], None, ALU.mult, None)
                yield 7.0
                aT3 = v2(aT[:, 0:kc * 256], kc)
                b = Bank()
                for i in range(2):
                    src = aT[:, 512 + i * width:512 + (i + 1) * width] if kc == 1 else src3[:, i, :]
                    for k in range(kc):
                        t2 = tr(b.ap[:, k * 256 + i * P:k * 256 + (i + 1) * P], src[:, k * P:(k + 1) * P], ident,
                                b.free, t, mark=(i == 1 and k == kc - 1))
                for k in range(kc):
                    u = ts(aT3[:, k, :], b.ap[:, k * 256:(k + 1) * 256], g[:, k:k + 1], None, ALU.mult, None, t2,
                           t_a, link=False)
                b.done(u)
                yield 2.0
                out = []
                for i in range(2):
                    b = Bank()
                    for k in range(kc):
                        t = mm(b.ap[:, 0:n], aT3[:, k, i * P:(i + 1) * P], v2(wb, kc)[:, k, :], k == 0, k == kc - 1,
                               b.free, u, t_wb, mark=(k == kc - 1))
                    out.append((b, t))
                return out

            b, t = chunk(7, 160)
            t_km = cp(PM3[:, :, 256:416], v2(b.ap[:, 0:320], 2), t, eng="act", link=False)
            b.done(t_km)
            yield 0.0
            if q is not None:
                b, t = chunk(0)
                t_qm = cp(PM3[:, :, 0:256], v2(b.ap, 2), t, eng="act", link=False)
                b.done(t_qm)
                yield 0.0
            out = yield from low_rank(PM3[:, :, 256:384], 1, col[f"mkv{l}"], wkvb, t_wkvb, 512, t_km, None)
            for i, (b, t) in enumerate(out):
                kvp = b.ap.rearrange("p (h d) -> p h d", h=4)
                cp(KA4[:, i, :, 0:64], kvp[:, :, 0:64], t, link=False)
                u = cp(VV3[:, i, 0:256].rearrange("p (h d) -> p h d", h=4), kvp[:, :, 64:128], t, link=False)
                b.done(u)
            t_kv = t
            kpe = PM3[:, :, 384:416].unsqueeze(2)
            if s == 0:
                rope(kpe, con["cosS"], con["sinS"], 1, 16, DS, t_km)
            t = cp(KA4[:, :, :, 64:96], kpe.to_broadcast([P, 2, 4, 32]), t_km)
            for j in ((4, 5, 6) if q is not None else (6,)):
                b, t2 = chunk(j)
                if j == 6:
                    u = cp(PG3[:, :, 512:640], v2(b.ap, 2)[:, :, 0:128], t2, eng="act", link=False)
                    u = cp(VV3[:, :, 512:640], v2(b.ap, 2)[:, :, 128:256], t2, eng="act", link=False)
                else:
                    u = cp(PG3[:, :, (j - 4) * 256:(j - 3) * 256], v2(b.ap, 2), t2, eng="act", link=False)
                b.done(u)
                yield 0.0
            t_pg = u
            t_ka = turned(lambda i: [KA4[:, i, h, :] for h in range(4)],
                          lambda i: [(KM3[0:96, :, i * P:(i + 1) * P], 0, 4)], 96, t)
            n0 = 0 if q is not None else 8
            nh = 10 - n0
            hd = PG3.rearrange("p i (n d) -> p i n d", d=64)[:, :, n0:10, :]
            sq4 = DS[:, 0:2 * nh * 64].rearrange("p (i n d) -> p i n d", i=2, n=nh)
            ssg = stats(2 * nh)
            t = tt(sq4, hd, hd, ALU.mult, t_pg)
            t = rsum(v2(ssg, 2), sq4, ALU.add)
            r, _ = rstd(ssg, 2 * nh, 64, t)
            tt(hd, hd, v2(r, 2).unsqueeze(3).to_broadcast([P, 2, nh, 64]), ALU.mult)
            for i in range(2):
                if q is not None:
                    tt(hd[:, i, 0:8, :], hd[:, i, 0:8, :],
                       srow[:, 320 * l + 64:320 * l + 128].unsqueeze(1).to_broadcast([P, 8, 64]), ALU.mult)
                t = tt(hd[:, i, nh - 2:nh, :], hd[:, i, nh - 2:nh, :],
                       srow[:, 320 * l + 128:320 * l + 192].unsqueeze(1).to_broadcast([P, 2, 64]), ALU.mult)
            if s == 0:
                t = rope(hd, con["cosL"], con["sinL"], nh, 32, DS)
            KK5 = KK.rearrange("p (i n u d) -> p i n u d", i=2, n=2, u=2)
            for i in range(2):
                t = cp(KK5[:, i, :, :, :], hd[:, i, nh - 2:nh, :].unsqueeze(2).to_broadcast([P, 2, 2, 64]))
            b, t2 = chunk(3)
            u = cp(VV3[:, :, 256:512], v2(b.ap, 2), t2, eng="act", link=False)
            b.done(u)
            if q is not None:
                yield from ()
                out_q = yield from low_rank(PM3[:, :, 0:256], 2, col[f"mq{l}"], wqb, t_wqb, 384, t_qm, t_kv)
                for i, (b, t3) in enumerate(out_q):
                    u = cp(KA[:, i * 384:(i + 1) * 384], b.ap[:, 0:384], t3, t_ka)
                    b.done(u)
                if s == 0:
                    u = rope(KA4[:, :, :, 64:96], con["cosS"], con["sinS"], 4, 16, DS)
                yield 6.0
            else:
                yield 8.0
            tg = turned(lambda i: [KK[:, i * 256 + n * P:i * 256 + (n + 1) * P] for n in range(2)],
                        lambda i: [(KG3[:, :, i * P:(i + 1) * P], 0, 2)], P, t)
            if q is not None:
                tg = turned(lambda i: [PG3[:, i, n * P:(n + 1) * P] for n in range(4)],
                            lambda i: [(QG3[:, :, i * P:(i + 1) * P], 0, 4)], P, t)
                turned(lambda i: [KA4[:, i, h, :] for h in range(4)],
                       lambda i: [(QM3[0:96, :, i * P:(i + 1) * P], 0, 4)], 96, u)
            tg2 = Q.latest("pe")
            for j in ((1, 2) if q is not None else (2,)):
                b, t2 = chunk(j)
                u = cp(PD3[:, :, (j - 1) * 256:j * 256], v2(b.ap, 2), t2, tg2, Q.latest("dve"), eng="act",
                       link=False)
                b.done(u)
                yield 0.0
            d0 = 0 if q is not None else 256
            t = u
            if s == 0:
                dd = PD3[:, :, d0:512].rearrange("p i (n d) -> p i n d", d=32)
                t = rope(dd, con["cosS"], con["sinS"], (512 - d0) // 32, 16, DS, u)
            yield 5.0
            if q is not None:
                turned(lambda i: [PD3[:, i, n * P:(n + 1) * P] for n in range(4)],
                       lambda i: [(QD3[:, :, i * P:(i + 1) * P], 0, 2), (KD3[:, :, i * P:(i + 1) * P], 2, 2)], P, t)
            else:
                turned(lambda i: [PD3[:, i, 256 + n * P:256 + (n + 1) * P] for n in range(2)],
                       lambda i: [(KD3[:, :, i * P:(i + 1) * P], 0, 2)], P, t)
            yield 1.5
            phase(keep)

        def attend(l, q, kvs, H, DS, obanks, *w):
            keep = mark()
            QM3, QD3, QG3 = q_views(q)
            views = [kv_views(m) for m in kvs]
            nk = 2 * len(kvs)
            W = nk * P
            PR = [alloc(512) for _ in range(4)]
            PT = [alloc(512) for _ in range(3)]
            RS = alloc(48)
            pfree, ptfree = [None] * 4, [None] * 3
            Yt = alloc(2048)
            units = []
            for i in range(2):
                for h in range(4):
                    units.append((i, 0, h, QM3[0:96, h], [v[0][0:96, h] for v in views], 64 * h, h == 3))
                for h in range(8):
                    r = slice(32 * (h % 4), 32 * (h % 4) + 32)
                    units.append((i, 1, h, QD3[r, h // 4], [v[1][r, h // 4] for v in views],
                                  256 + 64 * (h // 2), h == 7))
                for h in range(8):
                    r = slice(64 * (h % 2), 64 * (h % 2) + 64)
                    units.append((i, 2, h, QG3[r, h // 2], [v[2][r, h // 4] for v in views],
                                  512 + 64 * (h // 4), h == 7))
            obank, info = {}, {}
            done = [[], []]
            N = len(units)

            def score(n):
                i, kind, h, qa, ks, _, _ = units[n]
                b = Bank()
                for m, k in enumerate(ks):
                    t = mm(b.ap[:, m * 256:(m + 1) * 256], qa[:, i * P:(i + 1) * P], k, True, True, b.free, *w,
                           mark=(m == len(ks) - 1))
                mx = stats(2)
                c = 24 * i + (0, 4, 12)[kind] + h
                rsum(mx[:, 0:1], b.ap[:, 0:W], ALU.max, t, link=False)
                t = ts(mx[:, 1:2], mx[:, 0:1], -SCALES[kind], None, ALU.mult, None)
                t = act(PR[n % 4][:, 0:W], b.ap[:, 0:W], ACT.Exp, t, pfree[n % 4], bias=mx[:, 1:2],
                        scale=SCALES[kind], accum=RS[:, c:c + 1], link=False)
                b.done(t)
                info[n] = t

            def turn(n):
                b = Bank()
                for k in range(nk):
                    t = tr(b.ap[:, k * P:(k + 1) * P], PR[n % 4][:, k * P:(k + 1) * P], ident, b.free, info[n],
                           mark=(k == nk - 1))
                pfree[n % 4] = t
                t = cp(PT[n % 3][:, 0:W], b.ap[:, 0:W], t, ptfree[n % 3], eng=("act" if n % 2 == 0 else "dve"),
                       link=False)
                b.done(t)
                info[n] = [t, info[n]]

            def values(n):
                i, kind, h, _, _, vc, final = units[n]
                if h == 0:
                    obank[(i, kind)] = Bank(obanks[(3 * i + kind) % len(obanks)])
                b = obank[(i, kind)]
                for k in range(nk):
                    t = mm(b.ap[:, 64 * h:64 * h + 64], PT[n % 3][:, k * P:(k + 1) * P],
                           views[k // 2][3][:, k % 2, vc:vc + 64], k == 0, k == nk - 1, b.free, info[n],
                           mark=(k == nk - 1))
                ptfree[n % 3] = t
                if not final:
                    return
                c = [4, 8, 8][kind]
                r = RS[:, 24 * i + (0, 4, 12)[kind]:24 * i + (4, 12, 20)[kind]]
                recip(r, r, t, info[n])
                o3 = b.ap[:, 0:64 * c].rearrange("p (h d) -> p h d", h=c)
                rb = r.unsqueeze(2).to_broadcast([P, c, 64])
                y = Yt[:, i * 1024:(i + 1) * 1024]
                if kind != 1:
                    d = y[:, 0:256] if kind == 0 else y[:, 512:1024]
                    t = tt(d.rearrange("p (h d) -> p h d", h=c), o3, rb, ALU.mult, t)
                    b.done(t)
                    done[i].append(t)
                    return
                on, sqd = DS[:, 0:512], DS[:, 512:768]
                t = tt(on.rearrange("p (h d) -> p h d", h=8), o3, rb, ALU.mult, t)
                b.done(t)
                on4 = on.rearrange("p (h u d) -> p h u d", h=4, u=2)
                d3 = y[:, 256:512].rearrange("p (h d) -> p h d", h=4)
                stt(d3, on4[:, :, 1, :], lamc[:, l:l + 1], on4[:, :, 0, :], ALU.mult, ALU.add)
                s3 = sqd.rearrange("p (h d) -> p h d", h=4)
                tt(s3, d3, d3, ALU.mult)
                sd = stats(4)
                t = rsum(sd, s3, ALU.add)
                r2, _ = rstd(sd, 4, 64, t)
                tt(d3, d3, r2.unsqueeze(2).to_broadcast([P, 4, 64]), ALU.mult)
                done[i].append(tt(d3, d3, srow[:, 320 * l:320 * l + 64].unsqueeze(1).to_broadcast([P, 4, 64]),
                                  ALU.mult))

            A, B = (2, 3) if l else (1, 2)
            for n in range(N + B):
                if n < N:
                    score(n)
                yield 0.0 if l else 0.4
                if A <= n < N + A:
                    turn(n - A)
                yield 0.0 if l else 0.4
                if n >= B:
                    values(n - B)
                if n == N // 2 + B + 1:
                    ty = turn_split(Yt[:, 0:1024], H, 0, done[0], *w)
                yield 0.0 if l else 0.6
            yield 3.0
            out = turn_split(Yt[:, 1024:2048], H, 1, done[1])
            yield 2.0
            phase(keep)
            return ty + out

        def add_normed(x3, Y, junk, gB, *w):
            ssx = stats(2)
            t = sumsq(v2(Y, 2), ssx, junk, *w)
            r, _ = rstd(ssx, 2, D, t)
            for i in range(2):
                y = v2(Y, 2)[:, i, :]
                stt(y, y, r[:, i:i + 1], gB, ALU.mult, ALU.mult, *w)
                t = tt(x3[:, i, :], x3[:, i, :], y, ALU.add)
            return t

        def out_proj(l, x3, m, H, t_y):
            keep = mark()
            gB, Y, junk = alloc(1024), alloc(2048), alloc(1024)
            t_gB = spread(m["ga"], gB)
            for j in range(4):
                b = Bank()
                t = tok([("wout2", l, j, (c * 1024, (c + 1) * 1024)) for c in range(2)], H, b, 256, t_y)
                t = cp(v2(Y, 2)[:, :, j * 256:(j + 1) * 256], v2(b.ap, 2), t, eng="act", link=False)
                b.done(t)
                yield 0.0
            t = add_normed(x3, Y, junk, gB, t, t_gB)
            phase(keep)
            return t

        def ffn(l, x3, m, H, rest, *w):
            keep = mark()
            gB, Y, junk = alloc(1024), alloc(2048), alloc(2048)
            t_h = yield from norm_T(x3, m["FA"], m["FB"], Y, junk, H, *w)
            yield ("lock", "ffn")
            use_banks([4])
            t_gB = spread(m["gf"], gB)
            acc = [Bank(i) for i in range(4)]
            held = {}
            hb_free = list(Q.latest(e) for e in ("act", "dve"))
            for j in range(NF + LAG):
                if j < NF:
                    b = Bank()
                    for n in range(2):
                        t = feat(("ffn", l, 2 * j + n, (0, 1024)), H, b.ap[:, n * 256:(n + 1) * 256], b, t_h)
                    a = junk[:, (j % 3) * 256:(j % 3) * 256 + 256]
                    u = act(a, b.ap[:, 0:256], ACT.Silu, t, afree[j % 3], hb_free, link=False)
                    u = tt(a, a, b.ap[:, 256:512], ALU.mult, u, link=False)
                    b.done(u)
                    held[j] = split_hidden(j, a, u)
                if j >= LAG:
                    x, t = held.pop(j - LAG)
                    t_y = second_product(j - LAG, ("ffd", l, j - LAG, (0, 1024)), acc, x, t, NF)
                yield 0.0
            t = []
            for i in range(2):
                for h in range(2):
                    c = acc[2 * i + h]
                    u = cp(v2(Y, 2)[:, i, h * 512:(h + 1) * 512], c.ap, t_y, eng="act" if h else "dve", link=False)
                    c.done(u)
                    t.append(u)
            locks.pop("ffn")
            use_banks(rest)
            t = add_normed(x3, Y, junk[:, 0:1024], gB, t, t_gB)
            phase(keep)
            return t

        locks = {}
        DSL, DSC = TMP[:, 0:1280], TMP[:, 1280:2560]

        def latent():
            nonlocal t_x
            use_banks([4, 5, 6])
            t_gB = spread(MOD[:, 40:48], gB)
            for i in range(2):
                for h in range(2):
                    c = acc[2 * i + h]
                    s = slice(h * 512, (h + 1) * 512)
                    y = yb[:, s]
                    t = tt(y, c.ap, gB[:, s], ALU.mult, t_peer, t_gB)
                    c.done(t)
                    t = tt(X3[:, i, s], X3[:, i, s], y, ALU.add, t_x)
            ss = stats(2)
            t = sumsq(X3, ss, yb, t)
            r, _ = rstd(ss, 2, D, t)
            for i in range(2):
                t_x = stt(X3[:, i, :], X3[:, i, :], r[:, i:i + 1], fn, ALU.mult, ALU.mult, t_fn)
            heap(S3, L0, L1)
            phase()
            yield ("flag", "lam")
            kvl, q = alloc(KV), alloc(2560)
            for l in range(2):
                yield from qkv(l, 0, X3, lat[l], H1, kvl, q, DSL, t_x, flags["lam"])
                yield ("flag", ("kv", l))
                use_banks([4, 5, 6] if l == 0 else [0, 1, 2, 3, 4, 5, 6])
                t_y = yield from attend(l, q, [kvl, flags[("kv", l)][0]], H1, DSL, [7], flags[("kv", l)][1])
                flags[("free", l)] = True
                use_banks([5, 6])
                t_x = yield from out_proj(l, X3, lat[l], H1, t_y)
                yield 8.0
                t_x = yield from ffn(l, X3, lat[l], H1, [5, 6], t_x)
                yield 8.0

        def context():
            nonlocal t_xc
            use_banks([0, 1, 2])
            heap(S3, L1, C1)
            low = mark()
            q = alloc(2560)
            for l in range(2):
                r = srow[:, 320 * l + 192:320 * l + 320].rearrange("p (a b c) -> p a b c", a=2, b=2)
                pr, e, e2 = alloc(64), stats(2), stats(2)
                t = tt(v2(pr, 2), r[:, :, 0, :], r[:, :, 1, :], ALU.mult, t_srow)
                t = rsum(e, v2(pr, 2), ALU.add)
                t = act(e2, e, ACT.Exp, t)
                lm = lamc[:, l:l + 1]
                tt(lm, e2[:, 1:2], e2[:, 0:1], ALU.subtract, t)
                ts(lm, lm, LAM_INIT[l], None, ALU.subtract, None)
                g = srow[:, 320 * l:320 * l + 64]
                t = ts(g, g, 1.0 - LAM_INIT[l], None, ALU.mult, None)
            flags["lam"] = t
            yield ("lock", "ffn")
            yield from qkv(0, 1, XC3, cxt[0], HC, kvc, q, DSC, t_xc)
            flags[("kv", 0)] = (kvc, list(Q.thread.last.values()))
            t_y = yield from attend(0, q, [kvc], HC, DSC, [3])
            phase(low)
            t_xc = yield from out_proj(0, XC3, cxt[0], HC, t_y)
            yield 8.0
            t_xc = yield from ffn(0, XC3, cxt[0], HC, [5, 6], t_xc)
            yield ("flag", ("free", 0))
            kv1 = alloc(KV)
            yield from qkv(1, 1, XC3, cxt[1], HC, kv1, None, DSC, t_xc)
            flags[("kv", 1)] = (kv1, list(Q.thread.last.values()))

        threads = [Thread("L", latent()), Thread("C", context())]
        for t in threads:
            for e in ENGINES + ("dma",):
                t.pend[e] = [begun]
        interleave(Q, threads, flags, locks)
        Q.thread = main
        t = load("out", out_d.rearrange("b (i p) d -> p (b i) d", p=P), X3, t_x, eng="sp")
        Q.wait("sp", [t, flags["xs"]])
        if order is None:
            return used

        block = st.enter_context(nc.Block())

        def run(eng, name):
            for op in Q.ops[name]:
                if op[0] == "w":
                    eng.wait_ge(op[1], op[2])
                else:
                    ins = op[1](eng)
                    if op[2] is not None:
                        ins.then_inc(op[2], op[3])

        @block.sync
        def _(eng):
            run(eng, "sp")

        @block.gpsimd
        def _(eng):
            run(eng, "pool")

        @block.scalar
        def _(eng):
            run(eng, "act")

        @block.vector
        def _(eng):
            run(eng, "dve")

        @block.tensor
        def _(eng):
            run(eng, "pe")

    return used


def constants():
    c = np.zeros((P, NCON), np.float32)
    c[:, 0:128] = np.eye(P, dtype=np.float32)
    c[:, 128:256] = np.arange(P, dtype=np.float32)[None, :]
    tok_ = np.arange(256)
    row, colm = (tok_ // 64).astype(np.float32), (tok_ % 64).astype(np.float32)
    for name, rot in (("S", 32), ("L", 64)):
        q = rot // 4
        inv = np.power(np.float32(10000.0), -np.arange(q, dtype=np.float32) / np.float32(q)).astype(np.float32)
        ang = np.concatenate([row[:, None] * inv, colm[:, None] * inv], axis=-1).astype(np.float32)
        for f, a in (("cos", np.cos(ang)), ("sin", np.sin(ang))):
            o, w = CONS[f + name]
            c[:, o:o + w] = a.astype(np.float32).reshape(2, P, w // 2).transpose(1, 0, 2).reshape(P, w)
    o, _ = CONS["sel"]
    c[0:2, o] = 1.0
    c[2:4, o + 1] = 1.0
    return c


def kernel(**inputs):
    import concourse.bacc as bacc
    from concourse.bass_utils import run_bass_kernel_spmd as launch

    a = {k: np.asarray(v) for k, v in inputs.items()}
    f = np.float32

    def c8(v):
        return v.reshape(-1, P).T

    def tiles(w, n):
        k = w.shape[0] // P
        return w.reshape(k, P, w.shape[1] // n, n).transpose(2, 1, 0, 3).reshape(w.shape[1] // n, P, k * n)

    cols = np.concatenate(
        [c8(a["c"][0]), c8(a["c_2"][0]), c8(a["c_ctx_2"]), c8(a["b_ada"][0]), c8(a["b_ada_2"][0]),
         c8(a["b_ada_2"][1]), c8(a["norm1_w"][0]), c8(a["norm2_w"][0])]
        + [c8(a[n][l]) for n in ("g_attn_pre_2", "g_attn_post_2", "g_ffn_pre_2", "g_ffn_post_2") for l in range(2)]
        + [c8(a["g_mla_q_2"][l]) for l in range(2)] + [c8(a["g_mla_kv_2"][l]) for l in range(2)]
        + [c8(a["b_alpha"][0]), a["sgu_b"][0].T], axis=1)
    rows = np.concatenate(
        [a["gla_norm_w"][0], a["sgu_ln_w"][0], a["sgu_ln_b"][0], a["final_norm_w"]]
        + [a[n][l] for l in range(2) for n in ("g_diff_sub_2", "g_gqa_q_2", "g_gqa_k_2", "lambda_q1_2",
                                               "lambda_k1_2", "lambda_q2_2", "lambda_k2_2")])
    win = a["w_in"][0]
    e = a["peer_down"][0].reshape(P, P, 8, P).transpose(1, 3, 2, 0).reshape(P, P, D)
    u = a["peer_up"][0].reshape(P, P, D).transpose(1, 0, 2)
    w2 = a["w_in_2"]
    o2 = np.cumsum([0, 256, 160, 256, 256, 256, 512, 128, 128])
    qa, kva, dq, dk, dv, gq, gk, gv = [w2[:, :, o2[n]:o2[n + 1]] for n in range(8)]
    w2r = np.concatenate([qa, dq, dk, dv, gq, gk, gv], axis=2)
    ffn = np.concatenate([a["w_ffn_gate_2"].reshape(2, D, NF, 1, P), a["w_ffn_up_2"].reshape(2, D, NF, 1, P)],
                         axis=3).reshape(2, D, NF * 256)
    arrays = {
        "cols": cols,
        "cons": constants(),
        "rows": rows,
        "ada": tiles(a["w_ada"][0], 512),
        "ada2": np.stack([tiles(a["w_ada_2"][l], 512) for l in range(2)]),
        "wqk": tiles(win[:, :1024], P),
        "win": tiles(np.concatenate([win[:, 1024:3072], win[:, 3088:]], axis=1), 256),
        "walr": tiles(win[:, 3072:3088], 16)[0],
        "wau": a["w_alpha_up"][0],
        "sgw": a["sgu_w"][0].transpose(2, 0, 1).reshape(P, 1024),
        "wout": tiles(a["w_out"][0], 256),
        "wq": tiles(a["peer_w_q"][0], P),
        "keys": np.concatenate([a["peer_keys1"][0].T, a["peer_keys2"][0].T], axis=1),
        "peer": np.concatenate([e, u], axis=2),
        "x": a["x"],
        "ctx": a["ctx_2"],
        "win2": np.stack([tiles(w2r[l], 256) for l in range(2)]),
        "win2k": np.stack([tiles(kva[l], 160)[0] for l in range(2)]),
        "wqb": np.stack([tiles(a["w_mla_qb_2"][l], 384)[0] for l in range(2)]),
        "wkvb": a["w_mla_kvb_2"],
        "wout2": np.stack([tiles(a["w_out_2"][l], 256) for l in range(2)]),
        "ffn": np.stack([tiles(ffn[l], P) for l in range(2)]),
        "ffd": a["w_ffn_down_2"].reshape(2, NF, P, D),
    }
    arrays = {n: np.ascontiguousarray(v) for n, v in arrays.items()}

    def make(order):
        nc = bacc.Bacc("TRN2", target_bir_lowering=False, num_devices=1)
        dram = {n: nc.dram_tensor("in_" + n, v.shape, mybir.dt.from_np(v.dtype), kind="ExternalInput").ap()
                for n, v in arrays.items()}
        xs = nc.dram_tensor("xs", (P, 2048), F32, kind="Internal").ap()
        out = nc.dram_tensor("out_0", (1, 256, D), F32, kind="ExternalOutput").ap()
        return nc, program(nc, dram, out, xs, order)

    _, order = make(None)
    nc, _ = make(order)
    r = launch(nc, [{"in_" + n: v for n, v in arrays.items()}], core_ids=[0])
    return r.results[0]["out_0"]
```

```python
from contextlib import ExitStack

import numpy as np
import concourse.bass as bass
from concourse import mybir

ALU = mybir.AluOpType
ACT = mybir.ActivationFunctionType
AX = mybir.AxisListType
F32 = mybir.dt.float32
F32R = mybir.dt.float32r
U32 = mybir.dt.uint32
P = 128
EPS = 1e-6
D = 1024
NEG = -3.0e38
LAM_INIT = [0.8 - 0.6 * float(np.exp(-0.3 * l)) for l in range(2)]
SCALES = [1.0 / float(np.sqrt(96.0)), 1.0 / float(np.sqrt(32.0)), 1.0 / 8.0]
NRAW = 4
NSPL = 3
NF = 22
ENGINES = ("pe", "act", "dve", "pool")

COLS = {}
_n = 0
for _name, _w in [("c", 8), ("c2", 8), ("cc2", 8), ("b_ada", 48), ("b_ada2a", 48), ("b_ada2b", 48), ("norm1", 8),
                  ("norm2", 8), ("apre0", 8), ("apre1", 8), ("apost0", 8), ("apost1", 8), ("fpre0", 8),
                  ("fpre1", 8), ("fpost0", 8), ("fpost1", 8), ("mq0", 2), ("mq1", 2), ("mkv0", 1), ("mkv1", 1),
                  ("b_alpha", 4), ("sgu_b", 8)]:
    COLS[_name] = (_n, _w)
    _n += _w
NCOL = _n
CONS = {}
_n = 0
for _name, _w in [("ident", 128), ("iota", 128), ("cosS", 32), ("sinS", 32), ("cosL", 64), ("sinL", 64), ("sel", 2), ("half", 20)]:
    CONS[_name] = (_n, _w)
    _n += _w
NCON = _n


class Thread:

    def __init__(self, name, steps=None):
        self.name, self.steps, self.ready, self.over = name, steps, 0.0, False
        self.need, self.rank = None, 0
        self.last = {}
        self.pend = {}


class Queues:

    def __init__(self, sems):
        self.sem = sems
        self.ops = {e: [] for e in ENGINES + ("sp",)}
        self.count = {e: 0 for e in ENGINES}
        self.seen = {e: {} for e in self.ops}
        self.vals = {}
        self.thread = Thread("start")
        self.clock = 0.0

    def wait(self, eng, tokens):
        for t in tokens:
            if t is None:
                continue
            if isinstance(t, list):
                self.wait(eng, t)
                continue
            name, sem, val = t
            if self.seen[eng].get(name, 0) < val:
                self.seen[eng][name] = val
                self.ops[eng].append(("w", sem, val))

    def put(self, eng, fn, waits, mark=True):
        self.wait(eng, self.thread.pend.pop(eng, []))
        self.wait(eng, waits)
        if not mark:
            self.ops[eng].append(("i", fn, None, 0))
            return None
        self.count[eng] += 1
        self.ops[eng].append(("i", fn, self.sem[eng], 1))
        t = (eng, self.sem[eng], self.count[eng])
        self.thread.last[eng] = t
        return t

    def latest(self, eng):
        return (eng, self.sem[eng], self.count[eng]) if self.count[eng] else None

    def dma(self, eng, out, in_, name, sem, waits):
        self.wait(eng, self.thread.pend.pop("dma", []))
        self.wait(eng, waits)
        self.vals[name] = self.vals.get(name, 0) + 16
        self.ops[eng].append(("i", lambda e: e.dma_start(out, in_), sem, 16))
        return (name, sem, self.vals[name])

    def barrier(self):
        now = list(self.thread.last.values())
        for e in ENGINES + ("dma",):
            self.thread.pend[e] = now + self.thread.pend.get(e, [])


def interleave(q, threads, flags, locks):
    outer = q.thread

    def step(t):
        q.thread = t
        try:
            said = next(t.steps)
        except StopIteration:
            t.over = True
            return
        t.need = None
        if isinstance(said, tuple):
            t.need = said
        else:
            t.ready = q.clock + said

    def blocked(t):
        if t.need is None:
            return False
        kind, key = t.need
        if kind == "flag":
            return key not in flags
        return locks.get(key, t.name) != t.name

    while True:
        alive = [t for t in threads if not t.over]
        if not alive or threads[-1].over:
            break
        free = [t for t in alive if not blocked(t)]
        assert free
        now = [t for t in free if t.ready <= q.clock]
        if not now:
            q.clock = min(t.ready for t in free)
            continue
        t = min(now, key=lambda t: (flags.get("filler") == t.name, t.rank))
        if t.need is not None and t.need[0] == "lock":
            locks[t.need[1]] = t.name
        step(t)
    q.thread = outer


def program(nc, dram, out_d, xs_d, order):
    used = []
    with ExitStack() as st:
        def sb(name, words, dt=F32, where=st):
            return where.enter_context(nc.sbuf_tensor(name, [P, words], dt))

        sems = {e: st.enter_context(nc.semaphore("s_" + e)) for e in ENGINES}
        Q = Queues(sems)

        def mm(out, lhsT, rhs, start, stop, *w, mark=False, passes=4):
            n = 1
            for s in rhs.shape[1:]:
                n *= s
            Q.clock += passes * max(n, 64) / 2400.0
            return Q.put("pe", lambda e: e.matmul(out, lhsT, rhs, start=start, stop=stop, skip_group_check=True),
                         w, mark)

        def tr(out, in_, idn, *w, mark=False):
            Q.clock += 0.055
            return Q.put("pe", lambda e: e.transpose(out, in_, idn), w, mark)

        def own(eng, link):
            return Q.latest(eng) if link else None

        def act(out, in_, func, *w, bias=0.0, scale=1.0, accum=None, link=True):
            w = [own("act", link), list(w)]
            if accum is None:
                return Q.put("act", lambda e: e.activation(out, in_, func, bias=bias, scale=scale), w)
            return Q.put("act", lambda e: e.activation(out, in_, func, bias=bias, scale=scale, accum_out=accum), w)

        def tt(out, a, b, op, *w, eng="dve", link=True):
            return Q.put(eng, lambda e: e.tensor_tensor(out, a, b, op), [own(eng, link), list(w)])

        def ts(out, a, s1, s2, op0, op1, *w, link=True):
            if op1 is None:
                return Q.put("dve", lambda e: e.tensor_scalar(out, a, s1, None, op0), [own("dve", link), list(w)])
            return Q.put("dve", lambda e: e.tensor_scalar(out, a, s1, s2, op0, op1), [own("dve", link), list(w)])

        def stt(out, a, s, b, op0, op1, *w, link=True):
            return Q.put("dve", lambda e: e.scalar_tensor_tensor(out=out, in0=a, scalar=s, in1=b, op0=op0, op1=op1),
                         [own("dve", link), list(w)])

        def cp(out, a, *w, eng="dve", link=True):
            if eng == "act":
                return act(out, a, ACT.Copy, *w, link=link)
            return Q.put(eng, lambda e: e.tensor_copy(out, a), [own(eng, link), list(w)])

        def rsum(out, a, op, *w, link=True):
            return Q.put("dve", lambda e: e.tensor_reduce(out, a, AX.X, op), [own("dve", link), list(w)])

        def recip(out, a, *w):
            return Q.put("dve", lambda e: e.reciprocal(out, a), [own("dve", True), list(w)])

        def aff(ap, pattern, base, cm, *w):
            return Q.put("pool", lambda e: e.affine_select(out=ap, in_=ap, compare_op=ALU.is_ge, fill=0.0, base=base,
                                                           pattern=pattern, channel_multiplier=cm),
                         [own("pool", True), list(w)])

        RAW = sb("RAW", NRAW * 1024)
        SPL = sb("SPL", NSPL * 2048, F32R)
        HH, HL = sb("HH", 2048, F32R), sb("HL", 2048, F32R)
        WHL = sb("WHL", 3 * 512, F32R)
        CS = sb("CS", 48, F32R)
        cols, cons = sb("cols", NCOL), sb("cons", NCON)
        MOD, AB, ST = sb("MOD", 240), sb("AB", 176), sb("ST", 320)
        TMP = sb("TMP", 2816)
        R = sb("R", 28672)
        bk = [st.enter_context(nc.psum_tensor(f"bk{i}", [P, 512], F32)) for i in range(8)]
        misc = {}

        def load(name, out, in_, *w, eng="pool"):
            if name not in misc:
                misc[name] = st.enter_context(nc.semaphore("d_" + name))
            return Q.dma(eng, out, in_, name, misc[name], w)

        def v2(ap, a):
            return ap.rearrange("p (a b) -> p a b", a=a)

        H1 = (v2(HH[:, :], 8), v2(HL[:, :], 8))
        col = {n: cols[:, o:o + w] for n, (o, w) in COLS.items()}
        con = {n: cons[:, o:o + w] for n, (o, w) in CONS.items()}
        ident, iota = con["ident"], con["iota"]

        raw_sem = [st.enter_context(nc.semaphore(f"raw{i}")) for i in range(NRAW)]
        stream = {"use": 0, "dma": 0, "split": 0}
        ring = Thread("ring")
        raw_t, raw_free, split_t, split_free = {}, {}, {}, {}

        def source(key):
            a = dram[key[0]]
            for k in key[1:-1]:
                a = a[k]
            lo, hi = key[-1]
            return a[:, lo:hi]

        def ring_dma(n):
            s = n % NRAW
            src = source(order[n])
            w = src.shape[1]
            raw_t[n] = Q.dma("sp", RAW[:, s * 1024:s * 1024 + w], src, f"raw{s}", raw_sem[s],
                             [raw_free.get(n - NRAW)])
            stream["dma"] += 1

        def ring_split(n):
            s, z = n % NRAW, n % NSPL
            w = source(order[n]).shape[1]
            raw = RAW[:, s * 1024:s * 1024 + w]
            hi, lo = SPL[:, z * 2048:z * 2048 + w], SPL[:, z * 2048 + 1024:z * 2048 + 1024 + w]
            a = act(hi, raw, ACT.Copy, raw_t[n], split_free.get(n - NSPL), link=False)
            near = [k[0][:3] == "ada" for k in order[max(n - 1, 0):n + 2]]
            pool = all(near) if "pace" in flags else n % 3 == 1 and all(near) == any(near)
            b = tt(lo, raw, hi.bitcast(F32), ALU.subtract, a, eng=("pool" if pool else "dve"), link=False)
            raw_free[n] = [a, b]
            split_t[n] = [a, b]
            stream["split"] += 1

        class Chunk:
            def __init__(self, key):
                self.n = stream["use"]
                stream["use"] += 1
                used.append(key)
                w = key[-1][1] - key[-1][0]
                z = self.n % NSPL
                self.hi, self.lo = SPL[:, z * 2048:z * 2048 + w], SPL[:, z * 2048 + 1024:z * 2048 + 1024 + w]
                self.t = None
                if order is None:
                    return
                assert order[self.n] == key
                mine, Q.thread = Q.thread, ring
                while stream["split"] < min(self.n + NSPL, len(order)):
                    while stream["dma"] < min(stream["split"] + NRAW, len(order)):
                        ring_dma(stream["dma"])
                    ring_split(stream["split"])
                while stream["dma"] < min(stream["split"] + NRAW, len(order)):
                    ring_dma(stream["dma"])
                Q.thread = mine
                self.t = split_t[self.n]

            def done(self, token):
                split_free[self.n] = token

        def pairs(a, b):
            return ((a[0], b[0]), (a[0], b[1]), (a[1], b[0]))

        bank_free = [None] * 8
        rots = {}

        class Bank:
            def __init__(self, index=None):
                if index is None:
                    r = rots[Q.thread.name]
                    index = r[0][r[1] % len(r[0])]
                    r[1] += 1
                self.i, self.ap, self.free = index, bk[index][:, :], bank_free[index]

            def done(self, *tokens):
                bank_free[self.i] = list(tokens)

        def use_banks(s):
            rots[Q.thread.name] = [s, 0]

        heaps = {}

        def alloc(words):
            h = heaps[Q.thread.name]
            a = h["n"]
            h["n"] += words
            assert h["n"] <= h["end"], (Q.thread.name, h["n"] - h["start"], h["end"] - h["start"])
            return h["in"][:, a:a + words]

        def heap(tensor, start, end):
            heaps[Q.thread.name] = {"in": tensor, "start": start, "n": start, "end": end}

        def phase(keep=None):
            h = heaps[Q.thread.name]
            h["n"] = h["start"] if keep is None else keep
            Q.barrier()

        def mark():
            return heaps[Q.thread.name]["n"]

        stat = {"n": {}}

        def stats(n):
            b = 160 if Q.thread.name in ("B", "C") else 0
            a = stat["n"].get(b, 0)
            if a + n > 160:
                a = 0
            stat["n"][b] = a + n
            return ST[:, b + a:b + a + n]

        def rstd(ss, n, width, *w):
            a, y, r, out = stats(n), stats(n), stats(n), stats(n)
            t = ts(a, ss, 1.0 / width, EPS, ALU.mult, ALU.add, *w)
            t = tt(r, a, con["half"][:, 0:n], ALU.pow, t, t_cons, eng="pool")
            tt(y, r, r, ALU.mult, t)
            stt(y, y, -0.5, a, ALU.mult, ALU.mult)
            t = stt(out, y, 1.5, r, ALU.add, ALU.mult)
            return out, t

        def sumsq(src3, ss, junk, *w):
            for i in range(2):
                t = act(junk, src3[:, i, :], ACT.Square, *w, accum=ss[:, i:i + 1])
            return t

        def norm(x3, xn, junk, *w):
            known = flags.pop(("ss", Q.thread.name), None)
            if known is None:
                ss = stats(2)
                t = sumsq(x3, ss, junk[:, 0:1024], *w)
                yield 2.5
            else:
                ss, t = known
            r, t = rstd(ss, 2, D, t)
            yield 2.5
            return [ts(v2(xn, 2)[:, i, :], x3[:, i, :], r[:, i:i + 1], None, ALU.mult, None) for i in range(2)]

        def norm_T(x3, A, B, xn, ht, H, *w, tx=None):
            if tx is None:
                tx = yield from norm(x3, xn, ht, *w)
                yield 1.5
            out = []
            ht3 = v2(ht, 8)
            for i in range(2):
                c = slice(i * P, (i + 1) * P)
                src = v2(xn, 2)[:, i, :]
                us = []
                for k0 in (0, 4):
                    b = Bank()
                    for k in range(4):
                        t = tr(b.ap[:, k * P:(k + 1) * P], src[:, (k0 + k) * P:(k0 + k + 1) * P], ident, b.free,
                               tx[i], *w, mark=(k == 3))
                    for k in range(4):
                        q = slice(k0 + k, k0 + k + 1)
                        if k0:
                            u = ts(ht3[:, k0 + k, c], b.ap[:, k * P:(k + 1) * P], A[:, q], B[:, q], ALU.mult,
                                   ALU.add, t, link=False)
                        else:
                            u = act(ht3[:, k, c], b.ap[:, k * P:(k + 1) * P], ACT.Identity, t, scale=A[:, q],
                                    bias=B[:, q], link=False)
                    b.done(u)
                    us.append(u)
                u = act(H[0][:, :, c], ht3[:, :, c], ACT.Copy, us)
                yield 0.5
                out += [u, tt(H[1][:, :, c], ht3[:, :, c], H[0][:, :, c].bitcast(F32), ALU.subtract, u, us)]
            yield 2.0
            return out

        def turn_split(src, H, i, *w):
            out = []
            for k0 in (0, 4):
                b = Bank()
                for k in range(4):
                    t = tr(b.ap[:, k * P:(k + 1) * P], src[:, (k0 + k) * P:(k0 + k + 1) * P], ident, b.free, *w,
                           mark=(k == 3))
                c = slice(i * P, (i + 1) * P)
                hi, lo = H[0][:, k0:k0 + 4, c], H[1][:, k0:k0 + 4, c]
                u = cp(hi, v2(b.ap, 4), t, eng="act", link=False)
                v = tt(lo, v2(b.ap, 4), hi.bitcast(F32), ALU.subtract, u, link=False)
                b.done(v)
                out += [u, v]
            return out

        def tok(keys, H, b, n, *w):
            first = True
            for c, key in enumerate(keys):
                ch = Chunk(key)
                wp = (v2(ch.hi, 4), v2(ch.lo, 4))
                for i in range(2):
                    for k in range(4):
                        hs = [h[:, 4 * c + k, i * P:(i + 1) * P] for h in H]
                        for m, (x, y) in enumerate(pairs(hs, [q[:, k, :] for q in wp])):
                            last = i == 1 and k == 3 and m == 2
                            t = mm(b.ap[:, i * n:(i + 1) * n], x, y, first, c == 1 and k == 3 and m == 2, b.free,
                                   ch.t, *w, mark=last, passes=1)
                            first = False
                ch.done(t)
            return t

        def feat(key, H, out, b, *w):
            ch = Chunk(key)
            wp = (v2(ch.hi, 8), v2(ch.lo, 8))
            for k in range(8):
                for m, (x, y) in enumerate(pairs([q[:, k, :] for q in wp], [h[:, k, :] for h in H])):
                    t = mm(out, x, y, k == 0 and m == 0, k == 7 and m == 2, b.free, ch.t, *w,
                           mark=(k == 7 and m == 2), passes=1)
            ch.done(t)
            return t

        def spread(gcol, dst, *w):
            out = []
            for h in range(2):
                b = Bank()
                for k in range(4):
                    t = mm(b.ap[:, k * P:(k + 1) * P], gcol[:, 4 * h + k:4 * h + k + 1].to_broadcast([P, P]), ident,
                           True, True, b.free, *w, mark=(k == 3))
                u = cp(dst[:, h * 512:(h + 1) * 512], b.ap, t, eng="act", link=False)
                b.done(u)
                out.append(u)
            return out

        flags = {}

        scope = ExitStack()
        EXT = sb("EXT", 4096, where=scope)
        X = EXT[:, 0:2048]
        X3 = v2(X, 2)
        heap(R, 28640, 28672)
        t_cols = load("cols", cols[:, :], dram["cols"][:, :], eng="act")
        t_cons = load("cons", cons[:, :], dram["cons"][:, :], eng="act")
        t_x = load("x", X3, dram["x"].rearrange("b (i p) d -> p (b i) d", p=P))
        sil = alloc(24)
        t = act(sil, cols[:, 0:24], ACT.Silu, t_cols)
        c1 = CS[:, 0:16].rearrange("p (k m) -> p k m", m=2)
        c2 = CS[:, 16:48].rearrange("p (k s m) -> p s k m", s=2, m=2)
        s3 = v2(sil[:, 8:24], 2)
        cp(c1[:, :, 0], sil[:, 0:8], t)
        tt(c1[:, :, 1], sil[:, 0:8], c1[:, :, 0].bitcast(F32), ALU.subtract)
        cp(c2[:, :, :, 0], s3)
        t_cs = tt(c2[:, :, :, 1], s3, c2[:, :, :, 0].bitcast(F32), ALU.subtract)
        rowb = {"n": 0, "free": [None, None], "at": 0}

        def ada(name, cs, ns, groups, bias, dst, pace=0.0):
            m = 2 * ns
            for g in groups:
                flags["idle"] = list(Q.thread.last.values())
                if Q.thread.name == "B":
                    yield ("flag", "run")
                flags.pop("idle")
                b = Bank()
                for c in range(4):
                    ch = Chunk(name + (g, (c * 1024, (c + 1) * 1024)))
                    for k in range(2):
                        x = cs[:, (2 * c + k) * m:(2 * c + k + 1) * m]
                        for n, y in enumerate((ch.hi, ch.lo)):
                            last = k == 1 and n == 1
                            t = mm(b.ap[0:m, :], x, y[:, k * 512:(k + 1) * 512], c == 0 and k == 0 and n == 0,
                                   c == 3 and last, b.free, ch.t, t_cs, mark=last, passes=1)
                    ch.done(t)
                    yield flags.get("pace", pace)
                z = rowb["n"] % 2
                rowb["n"] += 1
                row = TMP[:, rowb["at"] + z * 512:rowb["at"] + (z + 1) * 512]
                u = cp(row[0:m, :], b.ap[0:m, :], t, rowb["free"][z], eng="act", link=False)
                b.done(u)
                yield 4.0
                b = Bank()
                for n in range(4):
                    t = mm(b.ap[:, n * ns:(n + 1) * ns], row[0:m, n * P:(n + 1) * P], con["sel"][0:m, 0:ns], True,
                           True, b.free, u, t_cons, mark=(n == 3))
                rowb["free"][z] = t
                d = v2(dst, ns)[:, :, 4 * g:4 * g + 4]
                t = tt(d, b.ap[:, 0:4 * ns].rearrange("p (n s) -> p s n", s=ns),
                       bias[:, 4 * g:4 * g + 4].unsqueeze(1).to_broadcast([P, ns, 4]), ALU.add, t, link=False)
                b.done(t)
                flags[name + ("t",)] = t

        def affine_cols(n, w, scale, *wt):
            o = AB[:, n * 16:n * 16 + 8]
            return o, stt(o, scale, 1.0, w, ALU.add, ALU.mult, *wt)

        lat, cxt = [], []

        def modulations():
            use_banks([6, 7])
            yield 25.0
            yield from ada(("ada",), CS[:, 0:16], 1, range(4, 12), col["b_ada"], MOD[:, 0:48], pace=3.0)
            flags["A2"] = affine_cols(1, col["norm2"], MOD[:, 32:40], flags[("ada", "t")])
            for l in range(2):
                mod = MOD[:, 48 + 96 * l:144 + 96 * l]
                yield from ada(("ada2", l), CS[:, 16:48], 2, range(12), col["b_ada2" + "ab"[l]], mod, pace=3.0)
                for s, lst in ((0, lat), (1, cxt)):
                    m = mod[:, 48 * s:48 * s + 48]
                    n = 2 + 4 * l + 2 * s
                    a, _ = affine_cols(n, col[f"apre{l}"], m[:, 8:16], flags[("ada2", l, "t")])
                    f, _ = affine_cols(n + 1, col[f"fpre{l}"], m[:, 32:40])
                    ga, gf = AB[:, n * 16 + 8:n * 16 + 16], AB[:, n * 16 + 24:n * 16 + 32]
                    tt(ga, m[:, 16:24], col[f"apost{l}"], ALU.mult)
                    tt(gf, m[:, 40:48], col[f"fpost{l}"], ALU.mult)
                    lst.append(dict(A=a, B=m[:, 0:8], FA=f, FB=m[:, 24:32], ga=ga, gf=gf))
            flags["late"] = list(Q.thread.last.values())

        gateT, i1T, i2T = TMP[:, 2048:2304], TMP[:, 2304:2560], TMP[:, 2560:2816]
        t_idx = []

        def mixer():
            nonlocal t_x
            use_banks([0, 1, 2, 3, 4, 5])
            heap(R, 0, 28640)
            big, ht = EXT[:, 2048:4096], alloc(2048)
            tx = yield from norm(X3, big, ht, t_x)
            yield from ada(("ada",), CS[:, 0:16], 1, range(0, 4), col["b_ada"], MOD[:, 0:48])
            A1, t_A1 = affine_cols(0, col["norm1"], MOD[:, 8:16], flags[("ada", "t")])
            t_h = yield from norm_T(X3, A1, MOD[:, 0:8], big, ht, H1, t_cons, t_A1, tx=tx)
            HT3 = v2(ht, 8)
            qT, kT, vt = alloc(1024), alloc(1024), alloc(2048)
            sgw, walr, wau = alloc(1024), alloc(128), alloc(512)
            t_walr = load("walr", walr, dram["walr"][:, :])
            t_wau = load("wau", wau[0:16, :], dram["wau"][:, :])
            gws, lnw, lnb = alloc(1024), alloc(1024), alloc(1024)
            t_rows = [load("row", d, dram["rows"][o:o + 1024].partition_broadcast(P))
                      for d, o in ((gws, 0), (lnw, 1024), (lnb, 2048))]
            alrT = alloc(256)
            t_sgw = load("sgw", sgw, dram["sgw"][:, :])
            t_sgw = aff(v2(sgw, 8), [[0, 8], [1, 128]], 0, -1, t_sgw)
            msk = alloc(256)
            t_msk = Q.put("pool", lambda e: e.memset(msk, 1.0), [])
            t_msk = Q.put("pool", lambda e: e.memset(msk.rearrange("p (a b) -> p a b", b=64)[:, :, 0:1], 0.0),
                          [t_msk])
            b = Bank()
            for k in range(8):
                t = mm(b.ap[0:16, 0:256], v2(walr, 8)[:, k, :], HT3[:, k, :], k == 0, k == 7, b.free, t_walr, t_h,
                       mark=(k == 7))
            t_alr = cp(alrT[0:16, :], b.ap[0:16, 0:256], t)
            b.done(t_alr)
            for j in range(4):
                b = Bank()
                for n in range(2):
                    t = feat(("wqk", 2 * j + n, (0, 1024)), H1, b.ap[:, n * 256:(n + 1) * 256], b, t_h)
                dst = (qT if j < 2 else kT)[:, (j % 2) * 512:(j % 2) * 512 + 512]
                t_qk = cp(dst, b.ap, t, eng="act", link=False)
                b.done(t_qk)
                yield 0.0
            z, la, Gc, eA = alloc(1024), alloc(1024), alloc(1024), alloc(1024)
            for j in range(2):
                b = Bank()
                for i in range(2):
                    h = 2 * j + i
                    t = mm(b.ap[:, i * 256:i * 256 + 256], wau[0:16, h * P:(h + 1) * P], alrT[0:16, :], True, True,
                           b.free, t_wau, t_alr, mark=(i == 1))
                for i in range(2):
                    h = 2 * j + i
                    t_z = ts(z[:, h * 256:(h + 1) * 256], b.ap[:, i * 256:i * 256 + 256],
                             col["b_alpha"][:, h:h + 1], None, ALU.add, None, t, link=False)
                b.done(t_z)
            def project(c0, evac, side=None):
                for j in range(4):
                    b = Bank()
                    t = tok([("win", c0 + j, (c * 1024, (c + 1) * 1024)) for c in range(2)], H1, b, 256)
                    evac(j, b, t)
                    if side is not None:
                        next(side, None)
                    yield 0.0

            def evac_to(dst, func):
                def evac(j, b, t):
                    t = act(v2(dst, 2)[:, :, j * 256:(j + 1) * 256], v2(b.ap, 2), func, t, link=False)
                    b.done(t)
                    flags["ev"] = t
                return evac

            vt3 = v2(vt, 2)
            G16 = Gc.rearrange("p (c t) -> p c t", t=64)
            egl = alloc(16)
            qd, ki, kt = z, eA, la
            dt = {}

            def scan(out, d0, d1, *w):
                return Q.put("dve", lambda e: e.tensor_tensor_scan(out, d0, d1, 0.0, ALU.mult, ALU.add),
                             [own("dve", True), list(w)])

            def decays():
                t = stt(eA, z, -1.0, z, ALU.mult, ALU.min, t_z)
                t = act(eA, eA, ACT.Exp, t)
                yield
                t = ts(eA, eA, 1.0, None, ALU.add, None, t)
                t = act(eA, eA, ACT.Ln, t)
                yield
                stt(la, z, 0.0, eA, ALU.min, ALU.subtract, t)
                for h in range(4):
                    s = slice(h * 256, (h + 1) * 256)
                    t_G = scan(Gc[:, s], msk, la[:, s], t_msk)
                yield
                dt["egl"] = act(egl, G16[:, :, 63], ACT.Exp, t_G, scale=1.0 / 16)
                e2 = act(eA, Gc, ACT.Exp, t_G, scale=-1.0 / 16)
                t = tt(la.rearrange("p (c t) -> p c t", t=64), G16[:, :, 63:64].to_broadcast([P, 16, 64]), G16,
                       ALU.subtract)
                yield
                e3 = act(la, la, ACT.Exp, t, scale=1.0 / 16)
                e1 = act(z, Gc, ACT.Exp, t, scale=1.0 / 16)
                tt(ki, kT, ki, ALU.mult, e2)
                yield
                dt["kt"] = tt(kt, kT, la, ALU.mult, e3, t_qk)
                dt["qd"] = stt(qd, qT, 128 ** -0.5, qd, ALU.mult, ALU.mult, e1, t_qk)
                yield

            side = decays()
            yield from project(0, evac_to(vt, ACT.Copy), side)
            t_v = flags["ev"]
            sv, su = alloc(2048), alloc(2048)
            yield from project(12, evac_to(sv, ACT.Gelu), side)
            t_sv = flags["ev"]
            t_egl, t_ktail, t_qd = dt["egl"], dt["kt"], dt["qd"]
            ktT = alloc(1024)
            ktT4 = ktT.rearrange("p (i h k) -> p i h k", i=2, h=4)
            t_ktT = []
            for i in range(2):
                b = Bank()
                for h in range(4):
                    t = tr(b.ap[:, h * P:(h + 1) * P], kt[:, h * 256 + i * P:h * 256 + (i + 1) * P], ident, b.free,
                           t_ktail, mark=(h == 3))
                t = cp(ktT[:, i * 512:(i + 1) * 512], b.ap, t, eng="act", link=False)
                b.done(t)
                t_ktT.append(t)
            AT = alloc(1024)
            t_AT = []
            for i in range(2):
                b = Bank()
                for h in range(4):
                    s = slice(h * 256 + i * P, h * 256 + (i + 1) * P)
                    t = mm(b.ap[:, h * P:(h + 1) * P], ki[:, s], qd[:, s], True, True, b.free, t_qd, mark=(h == 3))
                a = AT[:, i * 512:(i + 1) * 512]
                t = cp(a, b.ap, t, eng="act", link=False)
                b.done(t)
                aff(v2(a, 4), [[0, 4], [1, 128]], 0, -1, t)
                t_AT.append(aff(v2(a, 4)[:, :, 64:128], [[0, 4], [0, 64]], -64, 1))
            S = [alloc(1024) for _ in range(3)]
            t_S = [None] * 4
            for c in range(3):
                rows = slice(64 * (c % 2), 64 * (c % 2) + 64)
                for j in range(2):
                    b = Bank()
                    for i in range(2):
                        h = 2 * j + i
                        t = mm(b.ap[:, i * 256:(i + 1) * 256], ktT4[rows, c // 2, h, :],
                               vt3[rows, c // 2, h * 256:(h + 1) * 256], True, True, b.free, t_ktT[c // 2], t_v,
                               mark=(i == 1))
                    for i in range(2):
                        h = 2 * j + i
                        d = S[c][:, h * 256:(h + 1) * 256]
                        if c == 0:
                            u = cp(d, b.ap[:, i * 256:(i + 1) * 256], t, link=False)
                        else:
                            u = stt(d, S[c - 1][:, h * 256:(h + 1) * 256], egl[:, 4 * h + c:4 * h + c + 1],
                                    b.ap[:, i * 256:(i + 1) * 256], ALU.mult, ALU.add, t, t_egl, t_S[c], link=False)
                    b.done(u)
                t_S[c + 1] = u

            def layer_norm():
                mu, sq = stats(2), stats(2)
                rsum(mu, sv3, ALU.add, t_sv)
                ts(mu, mu, -1.0 / D, None, ALU.mult, None)
                for i in range(2):
                    t = ts(sv3[:, i, :], sv3[:, i, :], mu[:, i:i + 1], None, ALU.add, None)
                t = sumsq(sv3, sq, xn3[:, 0, :], t)
                yield
                rl, _ = rstd(sq, 2, D, t)
                stt(sv3[:, 0, :], sv3[:, 0, :], rl[:, 0:1], lnw, ALU.mult, ALU.mult, t_rows)
                yield
                stt(sv3[:, 1, :], sv3[:, 1, :], rl[:, 1:2], lnw, ALU.mult, ALU.mult, t_rows)
                tt(sv3[:, 0, :], sv3[:, 0, :], lnb, ALU.add)
                yield
                dt["ln"] = tt(sv3[:, 1, :], sv3[:, 1, :], lnb, ALU.add)
                yield

            xn = big
            sv3, xn3 = v2(sv, 2), v2(xn, 2)
            yield from project(8, evac_to(su, ACT.Gelu), layer_norm())
            t_su, t_ln = flags["ev"], dt["ln"]
            o = alloc(2048)
            so = stats(8)
            for i in range(2):
                for j in range(2):
                    b = Bank()
                    for m in range(2):
                        h = 2 * j + m
                        oc = slice(m * 256, (m + 1) * 256)
                        t = mm(b.ap[:, oc], AT[:, i * 512 + h * P:i * 512 + (h + 1) * P],
                               vt3[:, i, h * 256:(h + 1) * 256], True, False, b.free, t_AT[i], t_v)
                        for c in (2 * i, 2 * i + 1):
                            if c == 0:
                                continue
                            r = slice(64 * (c % 2), 64 * (c % 2) + 64)
                            t = mm(b.ap[r, oc], qd[:, h * 256 + c * 64:h * 256 + c * 64 + 64],
                                   S[c - 1][:, h * 256:(h + 1) * 256], False, c % 2 == 1, t_S[c],
                                   mark=(c % 2 == 1 and m == 1))
                    dst = o[:, i * 1024 + j * 512:i * 1024 + (j + 1) * 512]
                    t = cp(dst, b.ap, t, link=False)
                    b.done(t)
                    for m in range(2):
                        n = i * 4 + 2 * j + m
                        t_o = act(xn[:, m * 256:(m + 1) * 256], dst[:, m * 256:(m + 1) * 256], ACT.Square, t,
                                  accum=so[:, n:n + 1])
            ro, t_ro = rstd(so, 8, 256, t_o)
            for n in range(8):
                s = slice(n * 256, (n + 1) * 256)
                hs = slice((n % 4) * 256, (n % 4) * 256 + 256)
                t_on = stt(o[:, s], o[:, s], ro[:, n:n + 1], gws[:, hs], ALU.mult, ALU.mult, t_rows, t_ro,
                           link=False)
            for i in range(2):
                for j in range(2):
                    b = Bank()
                    for m in range(4):
                        g = 4 * j + m
                        t = mm(b.ap[:, m * P:(m + 1) * P], sgw[:, g * P:(g + 1) * P], sv3[:, i, g * P:(g + 1) * P],
                               True, True, b.free, t_sgw, t_ln, mark=(m == 3))
                    for m in range(4):
                        g = 4 * j + m
                        d = v2(su, 2)[:, i, g * P:(g + 1) * P]
                        t_s = stt(d, b.ap[:, m * P:(m + 1) * P], col["sgu_b"][:, g:g + 1], d, ALU.add, ALU.mult, t,
                                  t_su, link=False)
                    b.done(t_s)

            def evac_gate(dst, func, *w):
                def evac(j, b, t):
                    tmp = xn[:, (j % 2) * 512:(j % 2) * 512 + 512]
                    t = act(v2(tmp, 2), v2(b.ap, 2), func, t, Q.latest("dve"), link=False)
                    b.done(t)
                    d = v2(dst, 2)[:, :, j * 256:(j + 1) * 256]
                    flags["m"] = tt(d, d, v2(tmp, 2), ALU.mult, t, *w, link=False)
                return evac

            yield from project(4, evac_gate(o, ACT.Silu, t_on))
            yield from project(16, evac_gate(o, ACT.Sigmoid, t_on, flags["m"]))
            yield from project(20, evac_gate(su, ACT.Sigmoid, t_s))
            t_m = []
            for i in range(2):
                oi = v2(o, 2)[:, i, :]
                t_m.append(tt(oi, oi, v2(su, 2)[:, i, :], ALU.add, flags["m"]))
            yield ("flag", "A2")
            gB = lnw
            t_gB = spread(MOD[:, 16:24], gB, flags["A2"][1], t_ln)
            t_mT = []
            for i in range(2):
                t_mT += turn_split(v2(o, 2)[:, i, :], H1, i, t_m[i])
            yield 2.0
            for j in range(4):
                b = Bank()
                t = tok([("wout", j, (c * 1024, (c + 1) * 1024)) for c in range(2)], H1, b, 256, t_mT)
                y = v2(xn, 4)[:, j, :]
                g = gB[:, j * 256:(j + 1) * 256].unsqueeze(1).to_broadcast([P, 2, 256])
                t = tt(v2(y, 2), v2(b.ap, 2), g, ALU.mult, t, t_gB)
                b.done(t)
                t_x = tt(X3[:, :, j * 256:(j + 1) * 256], X3[:, :, j * 256:(j + 1) * 256], v2(y, 2), ALU.add)
                yield 0.0
            phase()
            flags["xs"] = load("xs", xs_d[:, :], X, t_x)
            keys = alloc(256)
            t_keys = load("keys", keys, dram["keys"][:, :])
            t_h = yield from norm_T(X3, flags["A2"][0], MOD[:, 24:32], alloc(2048), alloc(2048), H1, t_x)
            SC = alloc(4096)
            SC2 = alloc(1024)
            qh = [alloc(512), alloc(512)]
            qfree = [None, None]
            V16, I16 = alloc(512), alloc(512).bitcast(U32)
            V5 = V16.rearrange("p (i s h k) -> p i s h k", i=2, s=2, h=8)
            I5 = I16.rearrange("p (i s h k) -> p i s h k", i=2, s=2, h=8)

            def top16(lists, *w):
                def vmax(out, in_, *w):
                    return Q.put("dve", lambda e: e.max(out, in_), w)

                def vidx(out, m, in_, *w):
                    return Q.put("dve", lambda e: e.max_index(out, m, in_), w)

                def drop(work, m, vals, *w):
                    return Q.put("dve", lambda e: e.match_replace(work, m, vals, NEG), w)

                t = [vmax(vo[:, 0:8], vals, *w) for vals, vo, io, work in lists]
                u = [drop(work, vo[:, 0:8], vals, t[n], own("dve", True) if n == 0 else None)
                     for n, (vals, vo, io, work) in enumerate(lists)]
                for n, (vals, vo, io, work) in enumerate(lists):
                    vidx(io[:, 0:8], vo[:, 0:8], vals, t[n])
                t = [vmax(vo[:, 8:16], work, u[n]) for n, (vals, vo, io, work) in enumerate(lists)]
                return [vidx(io[:, 8:16], vo[:, 8:16], work, t[n]) for n, (vals, vo, io, work) in enumerate(lists)]

            for h in range(8):
                b = Bank()
                for n in range(2):
                    t = feat(("wq", 2 * h + n, (0, 1024)), H1, b.ap[:, n * 256:(n + 1) * 256], b, t_h)
                q = qh[h % 2]
                t_q = cp(q, b.ap, t, qfree[h % 2], eng="act", link=False)
                b.done(t_q)
                yield 0.0
                b = Bank()
                for i in range(2):
                    for s in range(2):
                        t = mm(b.ap[:, (i * 2 + s) * P:(i * 2 + s + 1) * P],
                               q[:, s * 256 + i * P:s * 256 + (i + 1) * P], keys[:, s * P:(s + 1) * P], True, True,
                               b.free, t_q, t_keys, mark=(i == 1 and s == 1))
                qfree[h % 2] = t
                sc = SC[:, h * 512:(h + 1) * 512]
                t = cp(sc, b.ap, t, eng="act", link=False)
                b.done(t)
                top16([(sc[:, n * P:(n + 1) * P], V5[:, n // 2, n % 2, h, :], I5[:, n // 2, n % 2, h, :],
                        SC2[:, n * P:(n + 1) * P]) for n in range(4)], t)
                yield 0.0
            IF = alloc(512)
            t_if = cp(IF, I16)
            I5f = IF.rearrange("p (i s h k) -> p i s h k", i=2, s=2, h=8)
            yield 12.0
            flags["pace"] = 1.0
            for i in range(2):
                if i == 1:
                    flags.pop("run")
                cand = alloc(2048)
                c4 = cand.rearrange("p (h a b) -> p h a b", h=8, a=16)
                tt(c4, V5[:, i, 0, :, :].unsqueeze(3).to_broadcast([P, 8, 16, 16]),
                   V5[:, i, 1, :, :].unsqueeze(2).to_broadcast([P, 8, 16, 16]), ALU.add)
                tv, tp = alloc(128), alloc(128).bitcast(U32)
                for h4 in (0, 4):
                    top16([(cand[:, h * 256:(h + 1) * 256], tv[:, h * 16:(h + 1) * 16], tp[:, h * 16:(h + 1) * 16],
                            SC2[:, (h - h4) * 256:(h - h4 + 1) * 256]) for h in range(h4, h4 + 4)],
                          own("dve", True))
                    yield 8.0
                sel = []
                for s in range(2):
                    pu, pf, res, ohb = alloc(128).bitcast(U32), alloc(128), alloc(128), alloc(2048)
                    eng = ("dve", "pool")[s]
                    if s == 0:
                        ts(pu, tp, 4, None, ALU.logical_shift_right, None)
                    else:
                        ts(pu, tp, 15, None, ALU.bitwise_and, None)
                    t = cp(pf, pu)
                    oh = ohb.rearrange("p (n a) -> p n a", a=16)
                    t = tt(oh, pf.unsqueeze(2).to_broadcast([P, 128, 16]),
                       iota[:, 0:16].unsqueeze(1).to_broadcast([P, 128, 16]), ALU.is_equal, t)
                    oh4 = ohb.rearrange("p (h k a) -> p h k a", h=8, k=16)
                    t = tt(oh4, oh4, I5f[:, i, s, :, :].unsqueeze(2).to_broadcast([P, 8, 16, 16]), ALU.mult, t_if,
                           t, eng=eng)
                    sel.append((res, oh, t))
                gt = alloc(128)
                tv3, gt3 = v2(tv, 8), v2(gt, 8)
                sm = stats(8)
                t = tt(gt3, tv3, tv3[:, :, 0:1].to_broadcast([P, 8, 16]), ALU.subtract)
                t = act(gt, gt, ACT.Exp, t)
                rsum(sm, gt3, ALU.add, t)
                recip(sm, sm)
                t = tt(gt3, gt3, sm.unsqueeze(2).to_broadcast([P, 8, 16]), ALU.mult)
                for res, oh, t in sel:
                    t = rsum(res, oh, ALU.add, t)
                yield 10.0
                b = Bank()
                for n, src in enumerate((gt, sel[0][0], sel[1][0])):
                    t2 = tr(b.ap[:, n * P:(n + 1) * P], src, ident, b.free, t, mark=(n == 2))
                u = cp(TMP[:, 2048:2816].rearrange("p (n t) -> p n t", n=3)[:, :, i * P:(i + 1) * P],
                       v2(b.ap[:, 0:384], 3), t2, eng="act", link=False)
                b.done(u)
                t_idx.append(u)
            yield ("flag", "idle")
            flags.pop("pace")

        fill = Thread("B", modulations())
        first = Thread("A", mixer())
        flags["run"] = True
        interleave(Q, [fill, first], flags, {})
        ends = [list(t.last.values()) for t in (fill, first)] + [flags["xs"]]

        main = Thread("M")
        Q.thread = main
        for e in ENGINES + ("dma",):
            main.pend[e] = [ends]
        use_banks([4, 5, 6, 7])
        NE = 16
        G3 = [v2(EXT[:, :], NE), v2(R[:, :], P - NE)]
        oh_free = [None] * 4
        io = iota.unsqueeze(1).to_broadcast([P, 2, P])
        for t4 in range(64):
            b = Bank()
            for z2 in range(2):
                z = (2 * t4 + z2) % 4
                o1 = v2(TMP[:, z * 512:z * 512 + 256], 2)
                o2 = v2(TMP[:, z * 512 + 256:z * 512 + 512], 2)
                two = slice(4 * t4 + 2 * z2, 4 * t4 + 2 * z2 + 2)
                u = tt(o1, io, i1T[:, two].unsqueeze(2).to_broadcast([P, 2, P]), ALU.is_equal, oh_free[z], t_idx,
                       link=False)
                u = tt(o1, o1, gateT[:, two].unsqueeze(2).to_broadcast([P, 2, P]), ALU.mult, u, eng="pool",
                       link=False)
                v = tt(o2, io, i2T[:, two].unsqueeze(2).to_broadcast([P, 2, P]), ALU.is_equal, link=False)
                for m in range(2):
                    n = 2 * z2 + m
                    t = mm(b.ap[:, n * P:(n + 1) * P], o1[:, m, :], o2[:, m, :], True, True, b.free, u, v,
                           mark=(m == 1))
                oh_free[z] = t
            four = slice(4 * t4, 4 * t4 + 4)
            g = b.ap.rearrange("p (m e) -> p e m", m=4)
            for d, e in ((G3[0], slice(0, NE)), (G3[1], slice(NE, P))):
                t_G = cp(d[:, :, four], g[:, e, :], t, eng="act", link=False)
            b.done(t_G)

        wfree = [None] * 3
        afree = [None] * 3

        def split_hidden(j, a, *w):
            z = j % 3
            hi, lo = WHL[:, z * 512:z * 512 + 256], WHL[:, z * 512 + 256:z * 512 + 512]
            u = act(hi, a, ACT.Copy, wfree[z], *w, link=False)
            v = tt(lo, a, hi.bitcast(F32), ALU.subtract, u, *w, link=False)
            afree[z] = [u, v]
            return (hi, lo), [u, v]

        def second_product(j, key, acc, x, t, n):
            ch = Chunk(key)
            for i in range(2):
                for h in range(2):
                    c = acc[2 * i + h]
                    xs = [q[:, i * P:(i + 1) * P] for q in x]
                    ys = [q[:, h * 512:(h + 1) * 512] for q in (ch.hi, ch.lo)]
                    for m, (p, q) in enumerate(pairs(xs, ys)):
                        u = mm(c.ap, p, q, j == 0 and m == 0, j == n - 1 and m == 2, c.free, ch.t, t,
                               mark=(i == 1 and h == 1 and m == 2), passes=1)
            ch.done(u)
            wfree[j % 3] = u
            return u

        acc = [Bank(i) for i in range(4)]
        LAG = 2

        def peer():
            held = {}
            for j in range(P + LAG):
                if j < P:
                    b = Bank()
                    t = feat(("peer", j, (0, 1024)), H1, b.ap[:, 0:256], b)
                    a = TMP[:, (j % 3) * 256:(j % 3) * 256 + 256]
                    u = act(a, b.ap[:, 0:256], ACT.Gelu, t, afree[j % 3], oh_free, link=False)
                    b.done(u)
                    v = tt(a, a, (G3[0][:, j, :] if j < NE else G3[1][:, j - NE, :]), ALU.mult, u, t_G, link=False)
                    held[j] = split_hidden(j, a, v)
                    yield 0.0
                if j >= LAG:
                    x, t = held.pop(j - LAG)
                    flags["y"] = second_product(j - LAG, ("peer", j - LAG, (1024, 2048)), acc, x, t, P)
                if j == 100:
                    flags["room"] = [v]
                yield 0.0

        scope.close()
        S3 = R
        HC = (v2(sb("HCH", 2048, F32R)[:, :], 8), v2(sb("HCL", 2048, F32R)[:, :], 8))
        X3, XC3 = v2(S3[:, 0:2048], 2), v2(S3[:, 2048:4096], 2)
        heap(S3, 4096, 4096 + 644)
        srow, lamc = alloc(640), alloc(4)
        KV = 3328
        base = 4096 + 644
        kvc = S3[:, base:base + KV]
        C0, L0 = base + KV, 17088
        L1 = L0 + 11584
        heap(S3, L0, L1)
        gB, fn, yb = alloc(1024), alloc(1024), alloc(1024)

        def kv_views(m):
            return (v2(m[:, 0:1024], 4), v2(m[:, 1024:1536], 2), v2(m[:, 1536:2048], 2), v2(m[:, 2048:3328], 2))

        def q_views(m):
            return (v2(m[:, 0:1024], 4), v2(m[:, 1024:1536], 2), v2(m[:, 1536:2560], 4))

        def rope(x4, cs, sn, n, half, DS, *w):
            step = 0.3 if n * half < 100 else 0.7
            c = v2(cs, 2).unsqueeze(2).to_broadcast([P, 2, n, half])
            s = v2(sn, 2).unsqueeze(2).to_broadcast([P, 2, n, half])
            a4 = DS[:, 0:2 * n * half].rearrange("p (i n d) -> p i n d", i=2, n=n)
            b4 = DS[:, 640:640 + 2 * n * half].rearrange("p (i n d) -> p i n d", i=2, n=n)
            x1, x2 = x4[:, :, :, 0:half], x4[:, :, :, half:2 * half]
            tt(a4, x1, s, ALU.mult, *w)
            yield step
            tt(b4, x2, s, ALU.mult)
            yield step
            tt(x1, x1, c, ALU.mult)
            yield step
            tt(x1, x1, b4, ALU.subtract)
            yield step
            tt(x2, x2, c, ALU.mult)
            yield step
            return tt(x2, x2, a4, ALU.add)

        def turned(srcs, dst, rows, *w):
            us = []
            for i in range(2):
                b = Bank()
                blocks = srcs(i)
                for n, a in enumerate(blocks):
                    t = tr(b.ap[0:rows, n * P:(n + 1) * P], a, ident, b.free, *w, mark=(n == len(blocks) - 1))
                for d, f, c in dst(i):
                    u = cp(d, v2(b.ap[0:rows, f * P:(f + c) * P], c), t, eng="act", link=False)
                b.done(u)
                us.append(u)
            return us

        def qkv(l, s, x3, m, H, kv, q, DS, *w):
            keep = mark()
            HTv = alloc(2048)
            xn = alloc(2048)
            t_h = yield from norm_T(x3, m["A"], m["B"], xn, HTv, H, *w)
            phase(keep)
            KM3, KD3, KG3, VV3 = kv_views(kv)
            PM, PG = alloc(832), alloc(1280)
            PM3, PG3 = v2(PM, 2), v2(PG, 2)
            PD3 = v2(PG[:, 0:1024], 2)
            wkvb = alloc(512)
            nm = f"{l}{s}"
            t_wkvb = load("wkvb" + nm, wkvb, dram["wkvb"][l])
            if q is not None:
                QM3, QD3, QG3 = q_views(q)
                wqb = alloc(768)
                t_wqb = load("wqb" + nm, wqb, dram["wqb"][l])
            KA, aT = alloc(768), alloc(1024)
            KK = alloc(512)
            KA4 = KA.rearrange("p (i h d) -> p i h d", i=2, h=4)

            def chunk(j, n=256):
                b = Bank()
                nme = "win2k" if j == 7 else "win2"
                key = (nme, l) if j == 7 else (nme, l, j)
                return b, tok([key + ((c * 4 * n, (c + 1) * 4 * n),) for c in range(2)], H, b, n, t_h)

            def scaled(src3, kc, t):
                width = kc * P
                ssx = stats(2)
                for i in range(2):
                    t = act(DS[:, 0:width], src3[:, i, :], ACT.Square, t, Q.latest("dve"), accum=ssx[:, i:i + 1])
                yield 0.5
                r, _ = rstd(ssx, 2, width, t)
                yield 0.5
                for i in range(2):
                    t = ts(aT[:, 512 + i * width:512 + (i + 1) * width] if kc == 1 else
                           src3[:, i, :], src3[:, i, :], r[:, i:i + 1], None, ALU.mult, None)
                return t

            def low_rank(src3, kc, g, wb, t_wb, n, t, t_a):
                width = kc * P
                aT3 = v2(aT[:, 0:kc * 256], kc)
                b = Bank()
                for i in range(2):
                    src = aT[:, 512 + i * width:512 + (i + 1) * width] if kc == 1 else src3[:, i, :]
                    for k in range(kc):
                        t2 = tr(b.ap[:, k * 256 + i * P:k * 256 + (i + 1) * P], src[:, k * P:(k + 1) * P], ident,
                                b.free, t, mark=(i == 1 and k == kc - 1))
                for k in range(kc):
                    u = act(aT3[:, k, :], b.ap[:, k * 256:(k + 1) * 256], ACT.Identity, t2, t_a,
                            scale=g[:, k:k + 1], link=False)
                b.done(u)
                yield 2.0
                out = []
                for i in range(2):
                    b = Bank()
                    for k in range(kc):
                        t = mm(b.ap[:, 0:n], aT3[:, k, i * P:(i + 1) * P], v2(wb, kc)[:, k, :], k == 0, k == kc - 1,
                               b.free, u, t_wb, mark=(k == kc - 1))
                    out.append((b, t))
                return out

            b, t = chunk(7, 160)
            t_km = cp(PM3[:, :, 256:416], v2(b.ap[:, 0:320], 2), t, eng="act", link=False)
            b.done(t_km)
            yield 0.0
            if q is not None:
                b, t = chunk(0)
                t_qm = cp(PM3[:, :, 0:256], v2(b.ap, 2), t, eng="act", link=False)
                b.done(t_qm)
                yield 0.0
            t_sk = yield from scaled(PM3[:, :, 256:384], 1, t_km)
            if q is not None:
                t_sq = yield from scaled(PM3[:, :, 0:256], 2, t_qm)
            for j in ((4, 5, 6) if q is not None else (6,)):
                b, t2 = chunk(j)
                if j == 6:
                    u = cp(PG3[:, :, 512:640], v2(b.ap, 2)[:, :, 0:128], t2, eng="act", link=False)
                    u = cp(VV3[:, :, 512:640], v2(b.ap, 2)[:, :, 128:256], t2, eng="act", link=False)
                else:
                    u = cp(PG3[:, :, (j - 4) * 256:(j - 3) * 256], v2(b.ap, 2), t2, eng="act", link=False)
                b.done(u)
                yield 0.0
            t_pg = u
            out = yield from low_rank(PM3[:, :, 256:384], 1, col[f"mkv{l}"], wkvb, t_wkvb, 512, t_sk, None)
            for i, (b, t) in enumerate(out):
                kvp = b.ap.rearrange("p (h d) -> p h d", h=4)
                cp(KA4[:, i, :, 0:64], kvp[:, :, 0:64], t, link=False)
                u = cp(VV3[:, i, 0:256].rearrange("p (h d) -> p h d", h=4), kvp[:, :, 64:128], t, link=False)
                b.done(u)
            t_kv = t
            kpe = PM3[:, :, 384:416].unsqueeze(2)
            if s == 0:
                yield from rope(kpe, con["cosS"], con["sinS"], 1, 16, DS, t_km)
            t = cp(KA4[:, :, :, 64:96], kpe.to_broadcast([P, 2, 4, 32]), t_km)
            t_ka = turned(lambda i: [KA4[:, i, h, :] for h in range(4)],
                          lambda i: [(KM3[0:96, :, i * P:(i + 1) * P], 0, 4)], 96, t)
            n0 = 0 if q is not None else 8
            nh = 10 - n0
            hd = PG3.rearrange("p i (n d) -> p i n d", d=64)[:, :, n0:10, :]
            sq4 = DS[:, 0:2 * nh * 64].rearrange("p (i n d) -> p i n d", i=2, n=nh)
            ssg = stats(2 * nh)
            t = tt(sq4, hd, hd, ALU.mult, t_pg)
            yield 1.0
            t = rsum(v2(ssg, 2), sq4, ALU.add)
            yield 1.0
            r, _ = rstd(ssg, 2 * nh, 64, t)
            yield 1.0
            tt(hd, hd, v2(r, 2).unsqueeze(3).to_broadcast([P, 2, nh, 64]), ALU.mult)
            yield 1.0
            for i in range(2):
                if q is not None:
                    tt(hd[:, i, 0:8, :], hd[:, i, 0:8, :],
                       srow[:, 320 * l + 64:320 * l + 128].unsqueeze(1).to_broadcast([P, 8, 64]), ALU.mult)
                t = tt(hd[:, i, nh - 2:nh, :], hd[:, i, nh - 2:nh, :],
                       srow[:, 320 * l + 128:320 * l + 192].unsqueeze(1).to_broadcast([P, 2, 64]), ALU.mult)
                yield 0.5
            if s == 0:
                t = yield from rope(hd, con["cosL"], con["sinL"], nh, 32, DS)
            KK5 = KK.rearrange("p (i n u d) -> p i n u d", i=2, n=2, u=2)
            for i in range(2):
                t = cp(KK5[:, i, :, :, :], hd[:, i, nh - 2:nh, :].unsqueeze(2).to_broadcast([P, 2, 2, 64]))
            b, t2 = chunk(3)
            u = cp(VV3[:, :, 256:512], v2(b.ap, 2), t2, eng="act", link=False)
            b.done(u)
            if q is not None:
                out_q = yield from low_rank(PM3[:, :, 0:256], 2, col[f"mq{l}"], wqb, t_wqb, 384, t_sq, t_kv)
                for i, (b, t3) in enumerate(out_q):
                    u = cp(KA[:, i * 384:(i + 1) * 384], b.ap[:, 0:384], t3, t_ka, eng="act")
                    b.done(u)
                if s == 0:
                    u = yield from rope(KA4[:, :, :, 64:96], con["cosS"], con["sinS"], 4, 16, DS, u)
                yield 6.0
            else:
                yield 8.0
            tg = turned(lambda i: [KK[:, i * 256 + n * P:i * 256 + (n + 1) * P] for n in range(2)],
                        lambda i: [(KG3[:, :, i * P:(i + 1) * P], 0, 2)], P, t)
            if q is not None:
                tg = turned(lambda i: [PG3[:, i, n * P:(n + 1) * P] for n in range(4)],
                            lambda i: [(QG3[:, :, i * P:(i + 1) * P], 0, 4)], P, t)
                turned(lambda i: [KA4[:, i, h, :] for h in range(4)],
                       lambda i: [(QM3[0:96, :, i * P:(i + 1) * P], 0, 4)], 96, u)
            tg2 = Q.latest("pe")
            for j in ((1, 2) if q is not None else (2,)):
                b, t2 = chunk(j)
                u = cp(PD3[:, :, (j - 1) * 256:j * 256], v2(b.ap, 2), t2, tg2, Q.latest("dve"), eng="act",
                       link=False)
                b.done(u)
                yield 0.0
            d0 = 0 if q is not None else 256
            t = u
            if s == 0:
                dd = PD3[:, :, d0:512].rearrange("p i (n d) -> p i n d", d=32)
                t = yield from rope(dd, con["cosS"], con["sinS"], (512 - d0) // 32, 16, DS, u)
            yield 5.0
            if q is not None:
                turned(lambda i: [PD3[:, i, n * P:(n + 1) * P] for n in range(4)],
                       lambda i: [(QD3[:, :, i * P:(i + 1) * P], 0, 2), (KD3[:, :, i * P:(i + 1) * P], 2, 2)], P, t)
            else:
                turned(lambda i: [PD3[:, i, 256 + n * P:256 + (n + 1) * P] for n in range(2)],
                       lambda i: [(KD3[:, :, i * P:(i + 1) * P], 0, 2)], P, t)
            yield 1.5
            phase(keep)

        def attend(l, q, kvs, H, DS, obanks, *w):
            keep = mark()
            QM3, QD3, QG3 = q_views(q)
            views = [kv_views(m) for m in kvs]
            nk = 2 * len(kvs)
            W = nk * P
            PR = [alloc(512) for _ in range(4)]
            PT = [alloc(512) for _ in range(3)]
            RS = alloc(48)
            pfree, ptfree = [None] * 4, [None] * 3
            Yt = alloc(2048)
            units = []
            for i in range(2):
                for h in range(4):
                    units.append((i, 0, h, QM3[0:96, h], [v[0][0:96, h] for v in views], 64 * h, h == 3))
                for h in range(8):
                    r = slice(32 * (h % 4), 32 * (h % 4) + 32)
                    units.append((i, 1, h, QD3[r, h // 4], [v[1][r, h // 4] for v in views],
                                  256 + 64 * (h // 2), h == 7))
                for h in range(8):
                    r = slice(64 * (h % 2), 64 * (h % 2) + 64)
                    units.append((i, 2, h, QG3[r, h // 2], [v[2][r, h // 4] for v in views],
                                  512 + 64 * (h // 4), h == 7))
            obank, info = {}, {}
            done = [[], []]
            N = len(units)

            def score(n):
                i, kind, h, qa, ks, _, _ = units[n]
                b = Bank()
                for m, k in enumerate(ks):
                    t = mm(b.ap[:, m * 256:(m + 1) * 256], qa[:, i * P:(i + 1) * P], k, True, True, b.free, *w,
                           mark=(m == len(ks) - 1))
                mx = stats(2)
                c = 24 * i + (0, 4, 12)[kind] + h
                rsum(mx[:, 0:1], b.ap[:, 0:W], ALU.max, t, link=False)
                t = ts(mx[:, 1:2], mx[:, 0:1], -SCALES[kind], None, ALU.mult, None)
                t = act(PR[n % 4][:, 0:W], b.ap[:, 0:W], ACT.Exp, t, pfree[n % 4], bias=mx[:, 1:2],
                        scale=SCALES[kind], accum=RS[:, c:c + 1], link=False)
                b.done(t)
                info[n] = t

            def turn(n):
                b = Bank()
                for k in range(nk):
                    t = tr(b.ap[:, k * P:(k + 1) * P], PR[n % 4][:, k * P:(k + 1) * P], ident, b.free, info[n],
                           mark=(k == nk - 1))
                pfree[n % 4] = t
                t = cp(PT[n % 3][:, 0:W], b.ap[:, 0:W], t, ptfree[n % 3], eng=("act" if n % 2 == 0 or 12 <= n % 20 < 16 or l == 0 and nk == 2 else "dve"),
                       link=False)
                b.done(t)
                info[n] = [t, info[n]]

            def values(n):
                i, kind, h, _, _, vc, final = units[n]
                if h == 0:
                    obank[(i, kind)] = Bank(obanks[(3 * i + kind) % len(obanks)])
                b = obank[(i, kind)]
                for k in range(nk):
                    t = mm(b.ap[:, 64 * h:64 * h + 64], PT[n % 3][:, k * P:(k + 1) * P],
                           views[k // 2][3][:, k % 2, vc:vc + 64], k == 0, k == nk - 1, b.free, info[n],
                           mark=(k == nk - 1))
                ptfree[n % 3] = t
                if not final:
                    return
                c = [4, 8, 8][kind]
                r = RS[:, 24 * i + (0, 4, 12)[kind]:24 * i + (4, 12, 20)[kind]]
                recip(r, r, t, info[n])
                o3 = b.ap[:, 0:64 * c].rearrange("p (h d) -> p h d", h=c)
                rb = r.unsqueeze(2).to_broadcast([P, c, 64])
                y = Yt[:, i * 1024:(i + 1) * 1024]
                if kind != 1:
                    d = y[:, 0:256] if kind == 0 else y[:, 512:1024]
                    t = tt(d.rearrange("p (h d) -> p h d", h=c), o3, rb, ALU.mult, t)
                    b.done(t)
                    done[i].append(t)
                    return
                on, sqd = DS[:, 0:512], DS[:, 512:768]
                t = tt(on.rearrange("p (h d) -> p h d", h=8), o3, rb, ALU.mult, t)
                b.done(t)
                on4 = on.rearrange("p (h u d) -> p h u d", h=4, u=2)
                d3 = y[:, 256:512].rearrange("p (h d) -> p h d", h=4)
                stt(d3, on4[:, :, 1, :], lamc[:, l:l + 1], on4[:, :, 0, :], ALU.mult, ALU.add)
                s3 = sqd.rearrange("p (h d) -> p h d", h=4)
                tt(s3, d3, d3, ALU.mult)
                sd = stats(4)
                t = rsum(sd, s3, ALU.add)
                r2, _ = rstd(sd, 4, 64, t)
                tt(d3, d3, r2.unsqueeze(2).to_broadcast([P, 4, 64]), ALU.mult)
                done[i].append(tt(d3, d3, srow[:, 320 * l:320 * l + 64].unsqueeze(1).to_broadcast([P, 4, 64]),
                                  ALU.mult))

            A, B = 2, 3
            for n in range(N + B):
                if n < N:
                    score(n)
                if A <= n < N + A:
                    turn(n - A)
                if n >= B:
                    values(n - B)
                if n == N // 2 + B + 1:
                    ty = turn_split(Yt[:, 0:1024], H, 0, done[0], *w)
                yield 0.0 if l else 1.0
            yield 3.0
            out = turn_split(Yt[:, 1024:2048], H, 1, done[1])
            yield 2.0
            phase(keep)
            return ty + out

        def add_normed(x3, Y, junk, gB, *w):
            ssx = stats(2)
            t = sumsq(v2(Y, 2), ssx, junk, *w)
            yield 1.5
            r, _ = rstd(ssx, 2, D, t)
            ssn = stats(2)
            yield 2.0
            for i in range(2):
                y = v2(Y, 2)[:, i, :]
                stt(y, y, r[:, i:i + 1], gB, ALU.mult, ALU.mult, *w)
                yield 1.0
                t = tt(x3[:, i, :], x3[:, i, :], y, ALU.add)
                u = act(y, x3[:, i, :], ACT.Square, t, accum=ssn[:, i:i + 1])
                yield 1.0
            flags[("ss", Q.thread.name)] = (ssn, u)
            return [t, u]

        def out_proj(l, x3, m, H, t_y):
            keep = mark()
            gB, Y, junk = alloc(1024), alloc(2048), alloc(1024)
            t_gB = spread(m["ga"], gB)
            for j in range(4):
                b = Bank()
                t = tok([("wout2", l, j, (c * 1024, (c + 1) * 1024)) for c in range(2)], H, b, 256, t_y)
                t = cp(v2(Y, 2)[:, :, j * 256:(j + 1) * 256], v2(b.ap, 2), t, eng="act", link=False)
                b.done(t)
                yield 0.0
            t = yield from add_normed(x3, Y, junk, gB, t, t_gB)
            phase(keep)
            return t

        def ffn(l, x3, m, H, rest, *w):
            keep = mark()
            gB, Y, junk = alloc(1024), alloc(2048), alloc(2048)
            t_h = yield from norm_T(x3, m["FA"], m["FB"], Y, junk, H, *w)
            t_gB = spread(m["gf"], gB)
            yield ("lock", "ffn")
            use_banks([4])
            if Q.thread.name == "L":
                flags["filler"] = "L"
            acc = [Bank(i) for i in range(4)]
            held = {}
            hb_free = list(Q.latest(e) for e in ("act", "dve"))
            for j in range(NF + LAG):
                if j < NF:
                    b = Bank()
                    for n in range(2):
                        t = feat(("ffn", l, 2 * j + n, (0, 1024)), H, b.ap[:, n * 256:(n + 1) * 256], b, t_h)
                        if n == 0:
                            yield 0.0
                    a = junk[:, (j % 3) * 256:(j % 3) * 256 + 256]
                    u = act(a, b.ap[:, 0:256], ACT.Silu, t, afree[j % 3], hb_free, link=False)
                    u = tt(a, a, b.ap[:, 256:512], ALU.mult, u, link=False)
                    b.done(u)
                    held[j] = split_hidden(j, a, u)
                    yield 0.0
                if j >= LAG:
                    x, t = held.pop(j - LAG)
                    t_y = second_product(j - LAG, ("ffd", l, j - LAG, (0, 1024)), acc, x, t, NF)
                yield 0.0
            t = []
            for i in range(2):
                for h in range(2):
                    c = acc[2 * i + h]
                    u = cp(v2(Y, 2)[:, i, h * 512:(h + 1) * 512], c.ap, t_y, eng="act" if h else "dve", link=False)
                    c.done(u)
                    t.append(u)
            locks.pop("ffn")
            flags.pop("filler", None)
            use_banks(rest)
            t = yield from add_normed(x3, Y, junk[:, 0:1024], gB, t, t_gB)
            phase(keep)
            return t

        locks = {}
        DSL, DSC = TMP[:, 0:1280], TMP[:, 1280:2560]

        def latent():
            use_banks([4, 5])
            yield ("lock", "ffn")
            flags["filler"] = "L"
            yield from peer()
            flags.pop("filler")
            yield ("flag", "second")
            t_x, t_fn, t_gB = flags["second"]
            for i in range(2):
                for h in range(2):
                    c = acc[2 * i + h]
                    s = slice(h * 512, (h + 1) * 512)
                    y = yb[:, s]
                    t = tt(y, c.ap, gB[:, s], ALU.mult, flags["y"], t_gB)
                    c.done(t)
                    t = tt(X3[:, i, s], X3[:, i, s], y, ALU.add, t_x)
            locks.pop("ffn")
            use_banks([5, 6, 7])
            yield 2.0
            ss = stats(2)
            t = sumsq(X3, ss, yb, t)
            yield 2.0
            r, _ = rstd(ss, 2, D, t)
            yield 2.0
            for i in range(2):
                t_x = stt(X3[:, i, :], X3[:, i, :], r[:, i:i + 1], fn, ALU.mult, ALU.mult, t_fn)
                yield 1.0
            heap(S3, L0, L1)
            phase()
            yield ("flag", "lam")
            kvl, q = alloc(KV), alloc(2560)
            for l in range(2):
                yield from qkv(l, 0, X3, lat[l], H1, kvl, q, DSL, t_x, flags["lam"])
                yield ("flag", ("kv", l))
                use_banks([5, 6] if l == 0 else [0, 1, 2, 3, 4, 5])
                t_y = yield from attend(l, q, [kvl, flags[("kv", l)][0]], H1, DSL, [7] if l == 0 else [6, 7],
                                        flags[("kv", l)][1])
                flags[("free", l)] = True
                use_banks([5, 6, 7])
                t_x = yield from out_proj(l, X3, lat[l], H1, t_y)
                yield 1.0
                t_x = yield from ffn(l, X3, lat[l], H1, [5, 6, 7], t_x)
                yield 1.0
            flags["out"] = t_x

        def context():
            use_banks([6, 7])
            heap(S3, C0, L0)
            yield ("flag", "late")
            yield ("flag", "room")
            for e in ENGINES + ("dma",):
                Q.thread.pend[e] = [flags["late"], flags["room"]]
            t_x = load("x3", S3[:, 0:2048], xs_d[:, :])
            Q.thread.pend["dma"] = [flags["room"]]
            t_xc = load("xc", XC3, dram["ctx"].rearrange("b (i p) d -> p (b i) d", p=P))
            t_srow = load("srow", srow, dram["rows"][4096:4736].partition_broadcast(P))
            t_fn = load("fn", fn, dram["rows"][3072:4096].partition_broadcast(P))
            t_gB = spread(MOD[:, 40:48], gB)
            flags["second"] = (t_x, t_fn, t_gB)
            low = mark()
            q = alloc(2560)
            yield 3.0
            for l in range(2):
                r = srow[:, 320 * l + 192:320 * l + 320].rearrange("p (a b c) -> p a b c", a=2, b=2)
                pr, e, e2 = alloc(64), stats(2), stats(2)
                t = tt(v2(pr, 2), r[:, :, 0, :], r[:, :, 1, :], ALU.mult, t_srow)
                t = rsum(e, v2(pr, 2), ALU.add)
                t = act(e2, e, ACT.Exp, t)
                lm = lamc[:, l:l + 1]
                tt(lm, e2[:, 1:2], e2[:, 0:1], ALU.subtract, t)
                ts(lm, lm, LAM_INIT[l], None, ALU.subtract, None)
                g = srow[:, 320 * l:320 * l + 64]
                t = ts(g, g, 1.0 - LAM_INIT[l], None, ALU.mult, None)
            flags["lam"] = t
            yield from qkv(0, 1, XC3, cxt[0], HC, kvc, q, DSC, t_xc)
            flags[("kv", 0)] = (kvc, list(Q.thread.last.values()))
            yield ("lock", "ffn")
            use_banks([0, 1, 2])
            t_y = yield from attend(0, q, [kvc], HC, DSC, [3, 4])
            phase(low)
            t_xc = yield from out_proj(0, XC3, cxt[0], HC, t_y)
            yield 1.0
            t_xc = yield from ffn(0, XC3, cxt[0], HC, [5, 6, 7], t_xc)
            yield ("flag", ("free", 0))
            kv1 = alloc(KV)
            yield from qkv(1, 1, XC3, cxt[1], HC, kv1, None, DSC, t_xc)
            flags[("kv", 1)] = (kv1, list(Q.thread.last.values()))

        L, C = Thread("L", latent()), Thread("C", context())
        C.rank = 1
        for t in (L, C, fill):
            for e in ENGINES:
                t.pend[e] = [list(main.last.values())]
        rots["B"] = [[7], 0]
        rowb["at"] = 1024
        flags["run"] = True
        threads = [fill, C, L]
        interleave(Q, threads, flags, locks)
        Q.thread = main
        t = load("out", out_d.rearrange("b (i p) d -> p (b i) d", p=P), X3, flags["out"], eng="sp")
        Q.wait("sp", [t, flags["xs"]])
        if order is None:
            return used

        block = st.enter_context(nc.Block())

        def run(eng, name):
            for op in Q.ops[name]:
                if op[0] == "w":
                    eng.wait_ge(op[1], op[2])
                else:
                    ins = op[1](eng)
                    if op[2] is not None:
                        ins.then_inc(op[2], op[3])

        @block.sync
        def _(eng):
            run(eng, "sp")

        @block.gpsimd
        def _(eng):
            run(eng, "pool")

        @block.scalar
        def _(eng):
            run(eng, "act")

        @block.vector
        def _(eng):
            run(eng, "dve")

        @block.tensor
        def _(eng):
            run(eng, "pe")

    return used


def constants():
    c = np.zeros((P, NCON), np.float32)
    c[:, 0:128] = np.eye(P, dtype=np.float32)
    c[:, 128:256] = np.arange(P, dtype=np.float32)[None, :]
    tok_ = np.arange(256)
    row, colm = (tok_ // 64).astype(np.float32), (tok_ % 64).astype(np.float32)
    for name, rot in (("S", 32), ("L", 64)):
        q = rot // 4
        inv = np.power(np.float32(10000.0), -np.arange(q, dtype=np.float32) / np.float32(q)).astype(np.float32)
        ang = np.concatenate([row[:, None] * inv, colm[:, None] * inv], axis=-1).astype(np.float32)
        for f, a in (("cos", np.cos(ang)), ("sin", np.sin(ang))):
            o, w = CONS[f + name]
            c[:, o:o + w] = a.astype(np.float32).reshape(2, P, w // 2).transpose(1, 0, 2).reshape(P, w)
    o, _ = CONS["sel"]
    c[0:2, o] = 1.0
    c[:, CONS["half"][0]:CONS["half"][0] + 20] = -0.5
    c[2:4, o + 1] = 1.0
    return c


def kernel(**inputs):
    import concourse.bacc as bacc
    from concourse.bass_utils import run_bass_kernel_spmd as launch

    a = {k: np.asarray(v) for k, v in inputs.items()}
    f = np.float32

    def c8(v):
        return v.reshape(-1, P).T

    def tiles(w, n):
        k = w.shape[0] // P
        return w.reshape(k, P, w.shape[1] // n, n).transpose(2, 1, 0, 3).reshape(w.shape[1] // n, P, k * n)

    cols = np.concatenate(
        [c8(a["c"][0]), c8(a["c_2"][0]), c8(a["c_ctx_2"]), c8(a["b_ada"][0]), c8(a["b_ada_2"][0]),
         c8(a["b_ada_2"][1]), c8(a["norm1_w"][0]), c8(a["norm2_w"][0])]
        + [c8(a[n][l]) for n in ("g_attn_pre_2", "g_attn_post_2", "g_ffn_pre_2", "g_ffn_post_2") for l in range(2)]
        + [c8(a["g_mla_q_2"][l]) for l in range(2)] + [c8(a["g_mla_kv_2"][l]) for l in range(2)]
        + [c8(a["b_alpha"][0]), a["sgu_b"][0].T], axis=1)
    rows = np.concatenate(
        [a["gla_norm_w"][0], a["sgu_ln_w"][0], a["sgu_ln_b"][0], a["final_norm_w"]]
        + [a[n][l] for l in range(2) for n in ("g_diff_sub_2", "g_gqa_q_2", "g_gqa_k_2", "lambda_q1_2",
                                               "lambda_k1_2", "lambda_q2_2", "lambda_k2_2")])
    win = a["w_in"][0]
    e = a["peer_down"][0].reshape(P, P, 8, P).transpose(1, 3, 2, 0).reshape(P, P, D)
    u = a["peer_up"][0].reshape(P, P, D).transpose(1, 0, 2)
    w2 = a["w_in_2"]
    o2 = np.cumsum([0, 256, 160, 256, 256, 256, 512, 128, 128])
    qa, kva, dq, dk, dv, gq, gk, gv = [w2[:, :, o2[n]:o2[n + 1]] for n in range(8)]
    w2r = np.concatenate([qa, dq, dk, dv, gq, gk, gv], axis=2)
    ffn = np.concatenate([a["w_ffn_gate_2"].reshape(2, D, NF, 1, P), a["w_ffn_up_2"].reshape(2, D, NF, 1, P)],
                         axis=3).reshape(2, D, NF * 256)
    arrays = {
        "cols": cols,
        "cons": constants(),
        "rows": rows,
        "ada": tiles(a["w_ada"][0], 512),
        "ada2": np.stack([tiles(a["w_ada_2"][l], 512) for l in range(2)]),
        "wqk": tiles(win[:, :1024], P),
        "win": tiles(np.concatenate([win[:, 1024:3072], win[:, 3088:]], axis=1), 256),
        "walr": tiles(win[:, 3072:3088], 16)[0],
        "wau": a["w_alpha_up"][0],
        "sgw": a["sgu_w"][0].transpose(2, 0, 1).reshape(P, 1024),
        "wout": tiles(a["w_out"][0], 256),
        "wq": tiles(a["peer_w_q"][0], P),
        "keys": np.concatenate([a["peer_keys1"][0].T, a["peer_keys2"][0].T], axis=1),
        "peer": np.concatenate([e, u], axis=2),
        "x": a["x"],
        "ctx": a["ctx_2"],
        "win2": np.stack([tiles(w2r[l], 256) for l in range(2)]),
        "win2k": np.stack([tiles(kva[l], 160)[0] for l in range(2)]),
        "wqb": np.stack([tiles(a["w_mla_qb_2"][l], 384)[0] for l in range(2)]),
        "wkvb": a["w_mla_kvb_2"],
        "wout2": np.stack([tiles(a["w_out_2"][l], 256) for l in range(2)]),
        "ffn": np.stack([tiles(ffn[l], P) for l in range(2)]),
        "ffd": a["w_ffn_down_2"].reshape(2, NF, P, D),
    }
    arrays = {n: np.ascontiguousarray(v) for n, v in arrays.items()}

    def make(order):
        nc = bacc.Bacc("TRN2", target_bir_lowering=False, num_devices=1)
        dram = {n: nc.dram_tensor("in_" + n, v.shape, mybir.dt.from_np(v.dtype), kind="ExternalInput").ap()
                for n, v in arrays.items()}
        xs = nc.dram_tensor("xs", (P, 2048), F32, kind="Internal").ap()
        out = nc.dram_tensor("out_0", (1, 256, D), F32, kind="ExternalOutput").ap()
        return nc, program(nc, dram, out, xs, order)

    _, order = make(None)
    nc, _ = make(order)
    r = launch(nc, [{"in_" + n: v for n, v in arrays.items()}], core_ids=[0])
    return r.results[0]["out_0"]
```
